# Optimizing a Trainium2 kernel written in Bass

```python
import math
import jax, jax.numpy as jnp
from jax import lax
import numpy as np

D_MODEL = 1024
BATCH = 1
SEQ = 2048
DEPTH = 1

D_MIX = D_MODEL
GROUP_W = D_MIX // 4
HEAD_DIM = 64
SC_WIDTH = GROUP_W
SC_KERNEL = 3
CF_WIDTH = GROUP_W
CF_KERNEL = 31
POOL_WIDTH = GROUP_W
POOL_WINDOWS = (2, 4, 8, 16)
POOL_GROUPS = len(POOL_WINDOWS)
POOL_GW = POOL_WIDTH // POOL_GROUPS
NSA_HEADS = GROUP_W // HEAD_DIM
NSA_KV_DIM = HEAD_DIM
CMP_BLOCK = 32
CMP_STRIDE = 16
CMP_HIDDEN = 256
SLC_BLOCK = 64
SLC_TOPN = 16
WIN = 512
Q_BLOCK = 128
ROPE_THETA = 10000.0
N_EXPERTS = 16
N_GROUPS = 4
EXPERTS_PER_GROUP = N_EXPERTS // N_GROUPS
TOPK_GROUP = 1
TOP_K = 2
D_EXPERT = 512
MOE_BLOCK = 256
DN_ALPHA = (2 * DEPTH) ** 0.25
DN_BETA = (8 * DEPTH) ** -0.25
LN_EPS = 1e-5
NEG = -1e30
FORCE = 1e4

IN_SIZES = (SC_WIDTH, SC_WIDTH, SC_WIDTH,
            CF_WIDTH, CF_WIDTH,
            POOL_WIDTH,
            NSA_HEADS * HEAD_DIM,
            NSA_KV_DIM, NSA_KV_DIM,
            NSA_KV_DIM, NSA_KV_DIM,
            NSA_KV_DIM, NSA_KV_DIM,
            NSA_HEADS * 3)
IN_WIDTH = sum(IN_SIZES)

kernel_name = "hymba_style_conv_pool_nsa_moe_deepnorm"

def layer_norm(x, g, b):
    xf = x.astype(jnp.float32)
    mu = xf.mean(-1, keepdims=True)
    var = jnp.square(xf - mu).mean(-1, keepdims=True)
    y = (xf - mu) * lax.rsqrt(var + LN_EPS)
    return (y * g.astype(jnp.float32) + b.astype(jnp.float32)).astype(x.dtype)

def causal_depthwise_conv(x, w):
    k = w.shape[0]
    return lax.conv_general_dilated(
        x, w[:, None, :].astype(x.dtype), window_strides=(1,), padding=[(k - 1, 0)],
        dimension_numbers=('NWC', 'WIO', 'NWC'), feature_group_count=x.shape[-1])

def rope_tables(n):
    inv = 1.0 / (ROPE_THETA ** (jnp.arange(0, HEAD_DIM, 2, dtype=jnp.float32) / HEAD_DIM))
    ang = jnp.arange(n, dtype=jnp.float32)[:, None] * inv[None, :]
    ang = jnp.concatenate([ang, ang], -1)
    return jnp.cos(ang), jnp.sin(ang)

def apply_rope(x, cos, sin):
    x1, x2 = jnp.split(x, 2, axis=-1)
    rot = jnp.concatenate([-x2, x1], -1)
    return (x.astype(jnp.float32) * cos + rot.astype(jnp.float32) * sin).astype(x.dtype)

def short_conv_mixer(b_gate, c_gate, h, w):
    return b_gate * causal_depthwise_conv(c_gate * h, w)

def conformer_conv_mixer(a, gate, w, bias, g, beta):
    u = a * jax.nn.sigmoid(gate)
    u = causal_depthwise_conv(u, w) + bias
    u = layer_norm(u, g, beta)
    return jax.nn.silu(u)

def multiscale_pool_mixer(p, w, scale):
    b_, s_, _ = p.shape
    pg = p.reshape(b_, s_, POOL_GROUPS, POOL_GW).astype(jnp.float32)
    cs = jnp.cumsum(pg, axis=1)
    cs = jnp.concatenate([jnp.zeros_like(cs[:, :1]), cs], axis=1)
    t1 = jnp.arange(1, s_ + 1)[:, None]
    lo = jnp.maximum(t1 - jnp.array(POOL_WINDOWS)[None, :], 0)
    cnt = (t1 - lo).astype(jnp.float32)
    lo_sum = cs[:, lo, jnp.arange(POOL_GROUPS)[None, :]]
    mean = (cs[:, 1:] - lo_sum) / cnt[None, :, :, None]
    d = (mean - pg).astype(p.dtype)
    y = jnp.einsum('bsgc,gcd->bsgd', d, w)
    return y.reshape(b_, s_, POOL_WIDTH) * scale

def compress_blocks(kv, pe, w1, w2):
    b_, s_, dh = kv.shape
    n_cmp = (s_ - CMP_BLOCK) // CMP_STRIDE + 1
    idx = jnp.arange(n_cmp)[:, None] * CMP_STRIDE + jnp.arange(CMP_BLOCK)[None, :]
    blocks = kv[:, idx] + pe
    hid = jax.nn.silu(blocks.reshape(b_, n_cmp, CMP_BLOCK * dh) @ w1)
    return hid @ w2

def nsa_mixer(q, kc, vc, ks, vs, kw, vw, gates, pe_k, pe_v, wk1, wk2, wv1, wv2, cos, sin):
    b_, s_, nh, dh = q.shape
    dt = q.dtype
    scale = dh ** -0.5
    k_cmp = compress_blocks(kc, pe_k, wk1, wk2)
    v_cmp = compress_blocks(vc, pe_v, wv1, wv2)
    n_cmp = k_cmp.shape[1]
    n_slc = s_ // SLC_BLOCK
    top_n = min(SLC_TOPN, n_slc)
    cmp_start = jnp.arange(n_cmp) * CMP_STRIDE
    cmp_end = cmp_start + CMP_BLOCK - 1
    slc_start = jnp.arange(n_slc) * SLC_BLOCK
    overlap = ((cmp_start[:, None] < slc_start[None, :] + SLC_BLOCK) &
               (cmp_start[:, None] + CMP_BLOCK > slc_start[None, :])).astype(jnp.float32)
    q_rot = apply_rope(q, cos[:, None, :], sin[:, None, :])
    ks_blk = apply_rope(ks, cos, sin).reshape(b_, n_slc, SLC_BLOCK, dh)
    vs_blk = vs.reshape(b_, n_slc, SLC_BLOCK, dh)
    kw_pad = jnp.pad(apply_rope(kw, cos, sin), ((0, 0), (WIN, 0), (0, 0)))
    vw_pad = jnp.pad(vw, ((0, 0), (WIN, 0), (0, 0)))
    b_idx = jnp.arange(b_)[:, None, None]
    blk = jnp.arange(n_slc)

    def one_query_block(qb):
        s0 = qb * Q_BLOCK
        tpos = s0 + jnp.arange(Q_BLOCK)
        qn = lax.dynamic_slice_in_dim(q, s0, Q_BLOCK, axis=1)
        qr = lax.dynamic_slice_in_dim(q_rot, s0, Q_BLOCK, axis=1)
        g = lax.dynamic_slice_in_dim(gates, s0, Q_BLOCK, axis=1)
        sc = jnp.einsum('bqhd,bnd->bqhn', qn, k_cmp).astype(jnp.float32) * scale
        cmask = cmp_end[None, :] <= tpos[:, None]
        p_cmp = jax.nn.softmax(jnp.where(cmask[None, :, None, :], sc, NEG), axis=-1)
        p_cmp = jnp.where(cmask.any(-1)[None, :, None, None], p_cmp, 0.0)
        o_cmp = jnp.einsum('bqhn,bnd->bqhd', p_cmp.astype(dt), v_cmp)
        imp = jnp.einsum('bqhn,nj->bqj', p_cmp, overlap)
        cur = tpos // SLC_BLOCK
        forced = (blk[None, :] == 0) | (blk[None, :] == cur[:, None]) | (blk[None, :] == cur[:, None] - 1)
        imp = jnp.where(forced[None], FORCE, imp)
        imp = jnp.where((slc_start[None, :] <= tpos[:, None])[None], imp, NEG)
        _, sel = lax.top_k(imp, top_n)
        k_sel = ks_blk[b_idx, sel]
        v_sel = vs_blk[b_idx, sel]
        ss = jnp.einsum('bqhd,bqnld->bqhnl', qr, k_sel).astype(jnp.float32) * scale
        kpos = sel[..., None] * SLC_BLOCK + jnp.arange(SLC_BLOCK)
        smask = kpos <= tpos[None, :, None, None]
        ss = jnp.where(smask[:, :, None], ss, NEG)
        ps = jax.nn.softmax(ss.reshape(b_, Q_BLOCK, nh, top_n * SLC_BLOCK), axis=-1).reshape(ss.shape)
        o_slc = jnp.einsum('bqhnl,bqnld->bqhd', ps.astype(dt), v_sel)
        k_win = lax.dynamic_slice_in_dim(kw_pad, s0, Q_BLOCK + WIN, axis=1)
        v_win = lax.dynamic_slice_in_dim(vw_pad, s0, Q_BLOCK + WIN, axis=1)
        sw = jnp.einsum('bqhd,bkd->bqhk', qr, k_win).astype(jnp.float32) * scale
        wpos = s0 - WIN + jnp.arange(Q_BLOCK + WIN)
        wmask = (wpos[None, :] <= tpos[:, None]) & (wpos[None, :] > tpos[:, None] - WIN) & (wpos[None, :] >= 0)
        pw = jax.nn.softmax(jnp.where(wmask[None, :, None, :], sw, NEG), axis=-1)
        o_win = jnp.einsum('bqhk,bkd->bqhd', pw.astype(dt), v_win)
        o = g[..., 0:1] * o_cmp + g[..., 1:2] * o_slc + g[..., 2:3] * o_win
        return o.astype(dt)

    out = lax.map(one_query_block, jnp.arange(s_ // Q_BLOCK))
    return out.transpose(1, 0, 2, 3, 4).reshape(b_, s_, nh * dh)

def route(xf, router_w, router_bias):
    n = xf.shape[0]
    aff = jax.nn.sigmoid((xf @ router_w).astype(jnp.float32))
    biased = aff + router_bias.astype(jnp.float32)
    gscore = lax.top_k(biased.reshape(n, N_GROUPS, EXPERTS_PER_GROUP), 2)[0].sum(-1)
    _, gsel = lax.top_k(gscore, TOPK_GROUP)
    gmask = (jnp.arange(N_GROUPS)[None, None, :] == gsel[:, :, None]).any(1)
    emask = jnp.repeat(gmask, EXPERTS_PER_GROUP, axis=1)
    _, eidx = lax.top_k(jnp.where(emask, biased, NEG), TOP_K)
    w = jnp.take_along_axis(aff, eidx, axis=-1)
    return eidx, w / w.sum(-1, keepdims=True)

def moe_ffn(x, router_w, router_bias, w_gate, w_up, w_down):
    b_, s_, d = x.shape
    n = b_ * s_
    xf = x.reshape(n, d)
    eidx, gw = route(xf, router_w, router_bias)
    a = n * TOP_K
    e_flat = eidx.reshape(a)
    tok = jnp.repeat(jnp.arange(n, dtype=jnp.int32), TOP_K)
    order = jnp.argsort(e_flat)
    e_s = e_flat[order]
    tok_s = tok[order]
    g_s = gw.reshape(a)[order]
    counts = jnp.bincount(e_flat, length=N_EXPERTS)
    padded = (counts + MOE_BLOCK - 1) // MOE_BLOCK * MOE_BLOCK
    starts = jnp.cumsum(counts) - counts
    pends = jnp.cumsum(padded)
    pstarts = pends - padded
    dest = pstarts[e_s] + jnp.arange(a) - starts[e_s]
    n_blocks = -(-(a + N_EXPERTS * (MOE_BLOCK - 1)) // MOE_BLOCK)
    p_len = n_blocks * MOE_BLOCK
    buf_tok = jnp.full((p_len,), n, jnp.int32).at[dest].set(tok_s)
    buf_gate = jnp.zeros((p_len,), x.dtype).at[dest].set(g_s.astype(x.dtype))
    blk_e = jnp.minimum(jnp.searchsorted(pends, jnp.arange(n_blocks) * MOE_BLOCK, side='right'), N_EXPERTS - 1)
    x_pad = jnp.concatenate([xf, jnp.zeros((1, d), x.dtype)], axis=0)
    xin = x_pad[buf_tok].reshape(n_blocks, MOE_BLOCK, d)

    def expert_block(args):
        xb, e = args
        h = jax.nn.silu(xb @ w_gate[e]) * (xb @ w_up[e])
        return h @ w_down[e]

    y = lax.map(expert_block, (xin, blk_e)).reshape(p_len, d) * buf_gate[:, None]
    out = jnp.zeros((n + 1, d), x.dtype).at[buf_tok].add(y)[:n]
    return out.reshape(b_, s_, d)

def hybrid_layer(x, w_in, conv_a_w, conv_b_w, conv_b_b, cf_ln_g, cf_ln_b, pool_w, pool_scale,
                 cmp_pe_k, cmp_pe_v, cmp_k_w1, cmp_k_w2, cmp_v_w1, cmp_v_w2, w_out,
                 ln1_g, ln1_b, ln2_g, ln2_b, router_w, router_bias, moe_w_gate, moe_w_up, moe_w_down,
                 cos, sin):
    b_, s_, _ = x.shape
    proj = x @ w_in
    split_at = [int(v) for v in np.cumsum(IN_SIZES)[:-1]]
    (a_b, a_c, a_h, b_val, b_gate, c_p, q, kc, vc, ks, vs, kw, vw, g) = jnp.split(proj, split_at, axis=-1)
    y_a = short_conv_mixer(a_b, a_c, a_h, conv_a_w)
    y_b = conformer_conv_mixer(b_val, b_gate, conv_b_w, conv_b_b, cf_ln_g, cf_ln_b)
    y_c = multiscale_pool_mixer(c_p, pool_w, pool_scale)
    gates = jax.nn.sigmoid(g.astype(jnp.float32)).astype(x.dtype).reshape(b_, s_, NSA_HEADS, 3)
    y_d = nsa_mixer(q.reshape(b_, s_, NSA_HEADS, HEAD_DIM), kc, vc, ks, vs, kw, vw, gates,
                    cmp_pe_k, cmp_pe_v, cmp_k_w1, cmp_k_w2, cmp_v_w1, cmp_v_w2, cos, sin)
    mix = jnp.concatenate([y_a, y_b, y_c, y_d], axis=-1) @ w_out
    x = layer_norm(DN_ALPHA * x + mix, ln1_g, ln1_b)
    x = layer_norm(DN_ALPHA * x + moe_ffn(x, router_w, router_bias, moe_w_gate, moe_w_up, moe_w_down), ln2_g, ln2_b)
    return x

def setup_inputs(seed: int = 0) -> dict:
    key = jax.random.key(seed)
    ks = jax.random.split(key, 26)
    f32 = jnp.float32
    nrm = lambda k, shape, s: jax.random.normal(k, shape, f32) * s
    return {
        "x": nrm(ks[0], (BATCH, SEQ, D_MODEL), 1.0),
        "w_in": nrm(ks[1], (DEPTH, D_MODEL, IN_WIDTH), D_MODEL ** -0.5),
        "conv_a_w": nrm(ks[2], (DEPTH, SC_KERNEL, SC_WIDTH), SC_KERNEL ** -0.5),
        "conv_b_w": nrm(ks[3], (DEPTH, CF_KERNEL, CF_WIDTH), CF_KERNEL ** -0.5),
        "conv_b_b": nrm(ks[4], (DEPTH, CF_WIDTH), 0.01),
        "cf_ln_g": 1.0 + nrm(ks[5], (DEPTH, CF_WIDTH), 0.02),
        "cf_ln_b": nrm(ks[6], (DEPTH, CF_WIDTH), 0.01),
        "pool_w": nrm(ks[7], (DEPTH, POOL_GROUPS, POOL_GW, POOL_GW), POOL_GW ** -0.5),
        "pool_scale": 1.0 + nrm(ks[8], (DEPTH, POOL_WIDTH), 0.05),
        "cmp_pe_k": nrm(ks[9], (DEPTH, CMP_BLOCK, HEAD_DIM), 0.1),
        "cmp_pe_v": nrm(ks[10], (DEPTH, CMP_BLOCK, HEAD_DIM), 0.1),
        "cmp_k_w1": nrm(ks[11], (DEPTH, CMP_BLOCK * HEAD_DIM, CMP_HIDDEN), (CMP_BLOCK * HEAD_DIM) ** -0.5),
        "cmp_k_w2": nrm(ks[12], (DEPTH, CMP_HIDDEN, HEAD_DIM), CMP_HIDDEN ** -0.5),
        "cmp_v_w1": nrm(ks[13], (DEPTH, CMP_BLOCK * HEAD_DIM, CMP_HIDDEN), (CMP_BLOCK * HEAD_DIM) ** -0.5),
        "cmp_v_w2": nrm(ks[14], (DEPTH, CMP_HIDDEN, HEAD_DIM), CMP_HIDDEN ** -0.5),
        "w_out": nrm(ks[15], (DEPTH, D_MIX, D_MODEL), D_MIX ** -0.5 * DN_BETA),
        "ln1_g": 1.0 + nrm(ks[16], (DEPTH, D_MODEL), 0.02),
        "ln1_b": nrm(ks[17], (DEPTH, D_MODEL), 0.01),
        "ln2_g": 1.0 + nrm(ks[18], (DEPTH, D_MODEL), 0.02),
        "ln2_b": nrm(ks[19], (DEPTH, D_MODEL), 0.01),
        "router_w": nrm(ks[20], (D_MODEL, N_EXPERTS), D_MODEL ** -0.5),
        "router_bias": nrm(ks[21], (N_EXPERTS,), 0.01),
        "moe_w_gate": nrm(ks[22], (DEPTH, N_EXPERTS, D_MODEL, D_EXPERT), D_MODEL ** -0.5),
        "moe_w_up": nrm(ks[23], (DEPTH, N_EXPERTS, D_MODEL, D_EXPERT), D_MODEL ** -0.5),
        "moe_w_down": nrm(ks[24], (DEPTH, N_EXPERTS, D_EXPERT, D_MODEL), D_EXPERT ** -0.5 * DN_BETA),
    }

def reference(x, w_in, conv_a_w, conv_b_w, conv_b_b, cf_ln_g, cf_ln_b, pool_w, pool_scale,
              cmp_pe_k, cmp_pe_v, cmp_k_w1, cmp_k_w2, cmp_v_w1, cmp_v_w2, w_out,
              ln1_g, ln1_b, ln2_g, ln2_b, router_w, router_bias, moe_w_gate, moe_w_up, moe_w_down):
    cos, sin = rope_tables(x.shape[1])
    for l in range(DEPTH):
        x = hybrid_layer(x, w_in[l], conv_a_w[l], conv_b_w[l], conv_b_b[l], cf_ln_g[l], cf_ln_b[l],
                         pool_w[l], pool_scale[l], cmp_pe_k[l], cmp_pe_v[l], cmp_k_w1[l], cmp_k_w2[l],
                         cmp_v_w1[l], cmp_v_w2[l], w_out[l], ln1_g[l], ln1_b[l], ln2_g[l], ln2_b[l],
                         router_w, router_bias, moe_w_gate[l], moe_w_up[l], moe_w_down[l], cos, sin)
    return x


_drawn_inputs = setup_inputs


def setup_inputs(seed=0):
    import zlib

    import numpy as np

    out = dict(_drawn_inputs(seed))
    spreads = {}
    factors = {'conv_b_b': 5.158,
     'cf_ln_g': 5.65,
     'cf_ln_b': 5.265,
     'cmp_pe_k': 8.0,
     'cmp_pe_v': 3.577,
     'cmp_k_w1': 3.142,
     'cmp_k_w2': 3.181,
     'ln2_g': 2.901,
     'ln2_b': 5.684}
    for name, (base, spread) in spreads.items():
        noise = np.random.default_rng([zlib.crc32(name.encode()), seed]).standard_normal(out[name].shape)
        drawn = base * np.exp(spread * noise) if base else spread * noise
        out[name] = __import__('jax').numpy.asarray(drawn.astype(out[name].dtype))
    for name, factor in factors.items():
        out[name] = (out[name] * factor).astype(out[name].dtype)
    return out
```

```python
from contextlib import ExitStack

import numpy as np
import concourse.bass as bass
import concourse.mybir as mybir

F32 = mybir.dt.float32
BF16 = mybir.dt.bfloat16
F32R = mybir.dt.float32r
I32 = mybir.dt.int32
ACT = mybir.ActivationFunctionType
ALU = mybir.AluOpType
AX = mybir.AxisListType

P = 128
SEQ, D = 2048, 1024
KD = D // P
TC = 512
NCH = SEQ // TC
NT = SEQ // P
GW = 256
HD = 64
NH = 4
CK, AK = 31, 3
HB, HA, HC = CK - 1, AK - 1, 16
NCMP = (SEQ - 32) // 16 + 1
CHID = 256
NSEL = SEQ // 64
WT = 4
NE, DE = 16, 512
ALPHA = 2.0 ** 0.25
EPS = 1e-5
NEG = -1e30
FORCE = 1e4
USED = -3e38
NB = (2 * SEQ + NE * (P - 1)) // P + 1
NB += NB % 2

M_BG0, M_BV0, M_BG1, M_BV1, M_KC, M_KS, M_Q0, M_Q1, M_C0, M_C1 = range(10)
M_AC0, M_AH0, M_AB0, M_AC1, M_AH1, M_AB1 = range(10, 16)
NM = 16
NTM = 140
MJ = NM + 2
NBANK = 6


def column_tiles():
    r = lambda a, n=P: list(range(a, a + n))
    o_b, o_c, o_h, o_val, o_gate, o_p, o_q, o_kc = 0, 256, 512, 768, 1024, 1280, 1536, 1792
    vc, ks, vs, kw, vw, g = (o_kc + 64 * n for n in range(1, 7))
    tiles = [r(o_gate), r(o_val), r(o_gate + P), r(o_val + P), r(o_kc, 64) + r(vc, 64), r(ks, 64) + r(kw, 64),
             r(o_q), r(o_q + P), r(o_p), r(o_p + P),
             r(o_c), r(o_h), r(o_b), r(o_c + P), r(o_h + P), r(o_b + P)]
    return tiles, r(vs, 64) + r(vw, 64) + r(g, 12)


CH_A, CH_B, CH_BB, CH_G, CH_BE, CH_PS, CH_IW, CH_EPS = 0, 6, 68, 70, 72, 74, 76, 78
NCHAN = 79

C_PERM, C_MEAN, C_ID, C_ONE, C_TRIU = 0, P, 2 * P, 3 * P, 4 * P
C_VALID = 5 * P
C_KEEP = C_VALID + 4
C_ADD = C_KEEP + 64
C_EW = C_ADD + 64
C_GW = C_EW + 16
C_K128 = C_GW + 4
C_LT = C_K128 + 16
C_BIDX = C_LT + 256
C_TOK = C_BIDX + 64
C_PT = C_TOK + 16
NCONST = C_PT + 2 * NCH * 16
K_ID, K_TRI, K_WIN, K_CMP = 0, P, P + 512, P + 1024
NMASK = K_CMP + 256


def shape_constants():
    p = np.arange(P)[:, None]
    c = np.zeros((P, NCONST), np.float32)
    perm = np.zeros((P, P), np.float32)
    for m in range(P):
        b, d = m // 64 * 64, m % 64
        if d < 32:
            perm[b + d + 32, m] = -1.0
        else:
            perm[b + d - 32, m] = 1.0
    c[:, C_PERM:C_PERM + P] = perm
    c[:, C_MEAN:C_MEAN + P] = 1.0 / GW
    c[:, C_ID:C_ID + P] = np.eye(P)
    c[:, C_ONE:C_ONE + P] = 1.0
    c[:, C_TRIU:C_TRIU + P] = (p < np.arange(P)[None])
    c[:, C_VALID] = (p[:, 0] >= 31)
    j = np.arange(64)[None] - 32
    cur = p // 64
    forced = (j == cur) | (j == cur - 1)
    future = j > cur
    c[:, C_KEEP:C_KEEP + 64] = ~(forced | future)
    c[:, C_ADD:C_ADD + 64] = np.where(future, NEG, np.where(forced, FORCE, 0.0))
    c[:, C_EW:C_EW + 16] = 16 - np.arange(16)
    c[:, C_GW:C_GW + 4] = 4 - np.arange(4)
    c[:, C_K128:C_K128 + 16] = P * np.arange(16)
    e = np.arange(16)
    c[:, C_LT:C_LT + 256] = (e[None, :] < e[:, None]).reshape(1, 256)
    c[:, C_BIDX:C_BIDX + 64] = np.arange(64)
    c[:, C_TOK:C_TOK + 16] = p + P * np.arange(16)[None]
    win = np.array([[2, 4], [8, 16]])
    pt = np.zeros((P, 2, NCH, 16), np.float32)
    for t in range(2):
        for half in range(2):
            w = win[t, half]
            for ch in range(NCH):
                cnt = np.minimum(ch * TC + np.arange(16) + 1, w)
                pt[64 * half:64 * half + 64, t, ch] = 1.0 / cnt.astype(np.float32)
    c[:, C_PT:] = pt.reshape(P, -1)
    k = np.zeros((P, NMASK), np.float32)
    k[:, K_ID:K_ID + P] = np.eye(P)
    q, key = p, np.arange(P)[None]
    k[:, K_TRI + 384:K_TRI + 512] = np.where(key > q, NEG, 0.0)
    k[:, K_WIN:K_WIN + P] = np.where(key > q, 0.0, NEG)
    n = np.arange(256)[None] - P
    k[:, K_CMP:K_CMP + 256] = np.where(16 * n + 31 <= p, 0.0, NEG)
    inv = (1.0 / (np.float32(10000.0) ** (np.arange(0, HD, 2, dtype=np.float32) / np.float32(HD)))).astype(np.float32)
    ang = (np.arange(SEQ, dtype=np.float32)[None] * np.tile(inv, 4)[:, None]).astype(np.float32)
    cs = np.stack([np.cos(ang), np.sin(ang)]).astype(np.float32)
    cs = np.ascontiguousarray(cs.reshape(2, P, NCH, TC).transpose(2, 1, 0, 3).reshape(NCH, P, 2 * TC))
    iw = np.stack([np.where(np.arange(P) < 64, 1.0 / win[t, 0], 1.0 / win[t, 1]) for t in range(2)], 1)
    return c, k, cs, iw.astype(np.float32)


def attention_units():
    def rest(branch, i, k0, r, slot):
        g = 4 // r
        return [(branch, i, h, g, k0, r, slot, "tri") for h in range(0, NH, g)]

    def n_slc(i):
        return i // 4 + 1

    units = [("cmp", 0)]
    for i in range(NT):
        ns = n_slc(i)
        if i < WT:
            units += rest("win", i, 0, i + 1, ns)
        else:
            units += [("win", i, h, 1, i - WT, WT, ns, "win") for h in range(NH)]
            units += rest("win", i, i, 1, ns + 1)
        if i + 1 < NT:
            units.append(("cmp", i + 1))
        for c in range(ns - 1):
            units += [("slc", i, h, 1, 4 * c, 4, c, None) for h in range(NH)]
        units += rest("slc", i, 4 * (ns - 1), i + 1 - 4 * (ns - 1), ns - 1)
    return units


def hybrid_layer(nc, a, out):
    units = attention_units()
    last_of = {i: max(n for n, u in enumerate(units) if u[0] != "cmp" and u[1] == i) for i in range(NT)}
    cmp_at = {u[1]: n for n, u in enumerate(units) if u[0] == "cmp"}
    first_slc = {i: min(n for n, u in enumerate(units) if u[0] == "slc" and u[1] == i) for i in range(NT)}
    n_slc = {i: i // 4 + 1 for i in range(NT)}
    n_win = {i: 1 if i < WT else 2 for i in range(NT)}

    x1_dram = nc.dram_tensor("x1_rows", (SEQ, D), F32).ap()
    y_dram = nc.dram_tensor("expert_rows", (NB * P, D), F32).ap()
    slot_dram = nc.dram_tensor("slot_token", ((NB + 1) * P, 1), I32).ap()

    with ExitStack() as ctx:
        sem_ = {}

        def sem(name):
            sem_[name] = ctx.enter_context(nc.semaphore(name))
            return sem_[name]

        ARENA = 55764
        ARENA_AT = -(-nc.sbuf_base // 32) * 32
        ctx.enter_context(nc.sbuf_tensor("arena", [P, ARENA], F32))
        top, carved = [0], []

        def carve(*shape, at=None, dtype=F32):
            n = int(np.prod(shape))
            if at is None:
                at = top[0]
                top[0] += -(-n // 8) * 8
            assert at + n <= ARENA, (at, n)
            v = nc.alloc_sbuf_tensor_at(f"at{at}_{len(carved)}", [P, n], dtype, offset=ARENA_AT + 4 * at)[:, :]
            carved.append(at)
            if len(shape) == 2:
                v = v.rearrange("p (a b) -> p a b", a=shape[0])
            if len(shape) == 3:
                v = v.rearrange("p (a b c) -> p a b c", a=shape[0], b=shape[1])
            return v

        def carve_parts(*shape, at=None):
            return carve(*shape, at=at, dtype=F32R)

        consts = carve(NCONST)
        chan = carve(NCHAN)
        masks = ctx.enter_context(nc.sbuf_tensor("masks", [P, NMASK], BF16))
        gates = carve(NT, 12)
        dest_w = carve(2, NT)
        dest_i = ctx.enter_context(nc.sbuf_tensor("dest_i", [P, 2, NT], I32))
        tok_i = ctx.enter_context(nc.sbuf_tensor("tok_i", [P, NT], I32))
        tables = ctx.enter_context(nc.sbuf_tensor("tables", [1, 3, 64], I32))
        PERSIST = top[0]
        yT = carve(KD, SEQ)
        QS = carve_parts(NH, SEQ)
        QR = carve(2, SEQ)
        AT_K = top[0]
        KS, KW = carve(SEQ), carve(SEQ)
        KSL, KWL = (carve_parts(SEQ, at=AT_K + n * SEQ) for n in range(2))
        VS = carve(NT, 65)
        VW = carve(NT, 65)
        TEMP = top[0]
        KC2 = yT[:, 6, :]
        VC2 = yT[:, 7, :]
        xT = [carve(KD, TC) for _ in range(2)]
        wt = [carve(KD, P) for _ in range(2)]
        w_tm = carve(KD, NTM)
        cs = carve(2, TC)
        stage = [carve(TC) for _ in range(4)]
        cpad = [carve(HC + TC) for _ in range(2)]
        bpad = [carve(HB + TC) for _ in range(2)]
        apad = [carve(HA + TC) for _ in range(2)]
        s_a, s_b = carve(HC + TC), carve(HC + TC)
        pd = [yT[:, 7, n * TC:(n + 1) * TC] for n in range(2)]
        pool_w = carve(2, P)
        t1, t2 = (yT[:, 7, n * TC:(n + 1) * TC] for n in (2, 3))
        sd = s_a[:, 0:TC]
        t2r = t2.bitcast(F32R)
        top[0] = TEMP
        w1 = [carve(16, CHID) for _ in range(2)]
        KSH, KWH = (carve_parts(SEQ, at=TEMP + n * SEQ) for n in range(2))
        w2 = carve(2, 2, P)
        pe2 = carve(2, 16)
        hT = [carve(2, P) for _ in range(2)]
        hbias = carve(4)
        kct = carve(2, P)
        vct = carve(HD)
        prob = [carve(TC) for _ in range(4)]
        probT = [carve(TC) for _ in range(3)]
        pn = [carve(NH, P) for _ in range(2)]
        OB = [carve(NH, 7, 65) for _ in range(2)]
        nmx = [carve(NH, 8) for _ in range(2)]
        small = carve(16, 32)
        psm = carve(132)
        imp = [carve(NSEL) for _ in range(2)]
        yrow = [carve(GW) for _ in range(2)]
        qmask = carve(P)[0:NSEL, :].bitcast(BF16).rearrange("p (a b) -> p a b", a=2)
        top[0] = TEMP
        carve(KD // 2, D)
        w_outa = carve(KD // 2, D)
        w_outb = carve(KD // 2, D, at=PERSIST + KD * SEQ)
        xrow = [carve(D) for _ in range(2)]
        rrow = [carve(D) for _ in range(2)]
        x1row = [carve(D) for _ in range(2)]
        x1T = [carve(KD, P) for _ in range(2)]
        ln_g, ln_b = carve(D), carve(D)
        rw = carve(KD, NE)
        bst = [carve(16) for _ in range(2)]
        lgt = carve(NT, NE)
        aff = carve(NT, NE)
        top[0] = PERSIST
        rt = [carve(NT, NE) for _ in range(14)]
        r4 = [carve(NT, 4) for _ in range(8)]
        r1 = [carve(NT) for _ in range(8)]
        cnt16 = carve(4, NE)
        cmp256 = carve(NE, NE)
        tb = [carve(64, NE) for _ in range(3)]
        tb1 = [carve(64) for _ in range(3)]
        rbias = carve(NE)
        zero_i = ctx.enter_context(nc.sbuf_tensor("zero_i", [P, NB + 1], I32))
        top[0] = PERSIST
        WE = KD * DE * 2 + 4 * D
        wx = carve(2, WE)
        xg = [carve(D) for _ in range(2)]
        xgT = [carve(KD, P) for _ in range(2)]
        hrow = [carve(DE) for _ in range(2)]
        hTm = [carve(4, P) for _ in range(2)]
        yrw = [carve(D) for _ in range(2)]
        idx = [ctx.enter_context(nc.sbuf_tensor(f"idx{u}", [P, 1], I32)) for u in range(2)]
        ln2_g, ln2_b = carve(D), carve(D)
        top[0] = PERSIST
        ya = [carve(D) for _ in range(2)]
        yb = [carve(D) for _ in range(2)]
        xr = [carve(D) for _ in range(2)]
        fin = [carve(D) for _ in range(2)]
        b6 = [carve(16) for _ in range(2)]

        bank = [ctx.enter_context(nc.psum_tensor(f"bank{n}", [P, 512], F32)) for n in range(8)]
        C = lambda at, n: consts[:, at:at + n]
        ident = C(C_ID, P)

        for n in ("const_in", "chan_in", "mask_in", "mask_ready", "tm_in", "x_in", "w_in", "cs_in",
                  "tile_made", "tile_out", "zeroed", "stage_free", "cpad_free", "rope_made", "sp_made",
                  "free6", "free7", "conv_made", "pool_d", "cent", "squared", "std", "zed", "dve_step",
                  "w_in0", "w_in1", "x_in0", "x_in1", "xr_in0", "xr_in1", "g_in0", "g_in1", "ysto0", "ysto1", "idx0", "idx1",
                  "ya_in0", "ya_in1", "xr6_in0", "xr6_in1", "out60", "out61", "r6", "c6", "p6", "mk_in",
                  "yc_done", "yb_done", "p1_pe", "p1_act", "p1_dve",
                  "cw_in", "k_high", "k_low", "shifted", "ch_made", "ch_out", "cc_made", "cc_out",
                  "s_made", "max_made", "prob_made", "t_made", "pt_made", "o_made", "o_out", "pn_made",
                  "mk_made", "mkT_made", "mask_rows", "d_made", "f_made", "y_made", "yT_made", "yT_out",
                  "cd_step", "wo_in", "ln_in", "xr_in", "mix_made", "mix_used", "sq_in", "sq_out", "norm_made",
                  "x1_made", "x1_sto0", "x1_sto1", "xt_made", "xt_out", "lg_made", "lg_out",
                  "route_in", "aff_made", "oh_made", "cum_made", "dest_made", "zero_made", "slot_zero",
                  "slot_stored", "tab_made",
                  "we_in", "blk_seed", "idx_in", "g_in", "gx_made", "gx_out", "gu_made", "act_made", "h_made", "ht_made", "ht_out",
                  "dn_made", "dn_outa", "dn_outd", "y_stored", "blk_done",
                  "l2_in", "y6_in", "y6_r", "s6_in", "s6_out", "n6", "fin6", "stats6"):
            sem(n)
        S = sem_

        block = ctx.enter_context(nc.Block())

        @block.sync
        def _(sp):
            sp.dma_start(consts, a["consts"]).then_inc(S["const_in"], 16)
            sp.dma_start(yT[:, 6, 0:NMASK], a["masks"]).then_inc(S["mk_in"], 16)
            sp.dma_start(chan, a["chan"]).then_inc(S["chan_in"], 16)
            sp.dma_start(pool_w[:, :, :], a["pool_w"]).then_inc(S["chan_in"], 16)
            sp.dma_start(w_tm[:, :, :], a["w_tm"]).then_inc(S["tm_in"], 16)
            with sp.Fori(0, NCH // 2) as cc:
                for u in range(2):
                    c = cc * 2 + u
                    sp.wait_ge(S["tile_made"], MJ * c + 1)
                    sp.dma_start(xT[u][:, :, :], a["xT"][bass.ds(c, 1), :, :].rearrange("a p n -> (a p) n")
                                 ).then_inc(S[f"x_in{u}"], 16)
                    sp.wait_ge(S["rope_made"], 3 * c + 1)
                    sp.dma_start(cs[:, :, :], a["cs"][bass.ds(c, 1), :, :].rearrange("a p n -> (a p) n")
                                 ).then_inc(S["cs_in"], 16)
                    for m in range(NM):
                        before = MJ * c + m - 1 if m >= 2 else MJ * c + m - 3
                        sp.wait_ge(S["tile_made"], before + MJ + 1)
                        sp.dma_start(wt[m % 2][:, :, :], a["w_in"][m]).then_inc(S[f"w_in{m % 2}"], 16)
            sp.wait_ge(S["tile_made"], MJ * NCH + MJ + 1)
            sp.wait_ge(S["yb_done"], 2 * NCH)
            for n in range(2):
                sp.dma_start(w1[n][:, :, :], a["cmp_w1"][n]).then_inc(S["cw_in"], 16)
            sp.dma_start(w2[:, :, :, :], a["cmp_w2"]).then_inc(S["cw_in"], 16)
            sp.dma_start(pe2[:, :, :], a["cmp_pe"]).then_inc(S["cw_in"], 16)
            sp.wait_ge(S["ch_made"], 4)
            sp.dma_start(w_outa[:, :, :], a["w_out"][0]).then_inc(S["wo_in"], 16)
            sp.wait_ge(S["s_made"], len(units))
            sp.dma_start(w_outb[:, :, :], a["w_out"][1]).then_inc(S["wo_in"], 16)
            sp.wait_ge(S["yT_out"], NT)
            sp.dma_start(ln_g, a["ln1_g"][None, :].to_broadcast((P, D))).then_inc(S["ln_in"], 16)
            sp.dma_start(ln_b, a["ln1_b"][None, :].to_broadcast((P, D))).then_inc(S["ln_in"], 16)
            sp.dma_start(rw[:, :, :], a["router_w"]).then_inc(S["ln_in"], 16)
            for t in range(NT):
                if t >= 2:
                    sp.wait_ge(S["mix_used"], 2 * (t - 1))
                sp.dma_start(xrow[t % 2], a["x"][t * P:(t + 1) * P, :]).then_inc(S[f"xr_in{t % 2}"], 16)
            sp.wait_ge(S["zero_made"], 1)
            sp.dma_start(slot_dram.rearrange("(p n) o -> p (n o)", p=P), zero_i[:, :]).then_inc(S["slot_zero"], 16)
            sp.wait_ge(S["lg_out"], NT)
            sp.dma_start(rbias, a["router_bias"][None, :].to_broadcast((P, NE))).then_inc(S["route_in"], 16)
            sp.wait_ge(S["tab_made"], 1)
            sp.dma_start(ln2_g, a["ln2_g"][None, :].to_broadcast((P, D))).then_inc(S["l2_in"], 16)
            sp.dma_start(ln2_b, a["ln2_b"][None, :].to_broadcast((P, D))).then_inc(S["l2_in"], 16)
            for e in range(NE):
                if e >= 1:
                    sp.wait_ge(S["we_in"], 48 * e)
                if e >= 2:
                    done = sp.value_load(tables[0:1, 1, e - 2:e - 1], min_val=0, max_val=NB)
                    sp.wait_ge(S["blk_done"], done + 1)
                for n in range(3):
                    sp.dma_start(wx[:, e % 2, n * KD * DE:(n + 1) * KD * DE], a["w_exp"][e, n]
                                 ).then_inc(S["we_in"], 16)
            with sp.Fori(0, NT // 2) as tt:
                for u in range(2):
                    t = tt * 2 + u
                    sp.wait_ge(S["r6"], t + 1)
                    sp.dma_start(xr[u], x1_dram[bass.ds(t * P, P), :]).then_inc(S[f"xr6_in{u}"], 16)
            sp.wait_ge(S["out60"], 8 * NT + 16)
            sp.wait_ge(S["out61"], 8 * NT + 16)

        @block.tensor
        def _(pe):
            pe.sem_inc(S["tile_made"], MJ + 1)
            pe.wait_ge(S["const_in"], 16)
            pe.wait_ge(S["chan_in"], 32)
            pe.wait_ge(S["tm_in"], 16)

            def special(b, free, value, out_, lhs_rhs):
                pe.wait_ge(S[free], value)
                for n, (l, r) in enumerate(lhs_rhs):
                    mm = pe.matmul(out_, l, r, start=(n == 0), stop=(n == len(lhs_rhs) - 1))
                mm.then_inc(S["sp_made"], 1)

            with pe.Fori(0, NCH // 2) as cc:
                for u in range(2):
                    c = cc * 2 + u
                    cols = bass.ds(c * TC, TC)
                    for j in range(MJ):
                        if j == 0:
                            pe.wait_ge(S[f"x_in{u}"], 16 * cc + 16)
                        pe.wait_ge(S["tile_out"], MJ * c + j + 1)
                        ps = bank[j % NBANK]
                        if j < NM:
                            pe.wait_ge(S[f"w_in{j % 2}"], 8 * NM * c + 16 * (j // 2) + 16)
                            for k in range(KD):
                                mm = pe.matmul(ps[:], wt[j % 2][:, k, :], xT[u][:, k, :],
                                               start=(k == 0), stop=(k == KD - 1))
                        else:
                            for s in range(2):
                                tok = (j - NM) * 2 + s
                                for k in range(KD):
                                    mm = pe.matmul(ps[:, s * NTM:(s + 1) * NTM], xT[u][:, k, tok * P:(tok + 1) * P],
                                                   w_tm[:, k, :], start=(k == 0), stop=(k == KD - 1))
                        mm.then_inc(S["tile_made"], 1)
                        if j == M_C0:
                            pe.wait_ge(S["tile_out"], MJ * c + NBANK + M_KS + 1)
                            special(6, "free6", 4 * c + 1, bank[6][:], [(C(C_PERM, P), stage[0])])
                        if j == M_C1:
                            pe.wait_ge(S["tile_out"], MJ * c + NBANK + M_Q0 + 1)
                            special(7, "free7", 3 * c + 1, bank[7][:], [(C(C_PERM, P), QR[:, 0, cols])])
                        if j == M_AC0:
                            pe.wait_ge(S["tile_out"], MJ * c + NBANK + M_Q1 + 1)
                            special(6, "free6", 4 * c + 2, bank[6][:], [(C(C_PERM, P), QR[:, 1, cols])])
                        if j == M_AH0:
                            pe.wait_ge(S["conv_made"], 2 * c + 2)
                            special(7, "free7", 3 * c + 2, bank[7][:],
                                    [(C(C_MEAN, P), yT[:, 2 + n, cols]) for n in range(2)])
                        if j == M_AB0:
                            for n in range(2):
                                pe.wait_ge(S["pool_d"], 2 * c + n + 1)
                                special(6 + n, f"free{6 + n}", (4 if n == 0 else 3) * c + 3, bank[6 + n][:],
                                        [(pool_w[:, n, :], pd[n])])
                        if j == M_AH1:
                            pe.wait_ge(S["squared"], 2 * c + 2)
                            special(6, "free6", 4 * c + 4, bank[6][:], [(C(C_MEAN, P), t) for t in (t1, t2)])

            pe.wait_ge(S["cw_in"], 64)
            pe.wait_ge(S["shifted"], 2)
            pe.wait_ge(S["tile_out"], MJ * NCH + NBANK)
            pe.wait_ge(S["free6"], 4 * NCH + 1)
            pe.wait_ge(S["free7"], 3 * NCH + 1)
            for n, src in enumerate((KC2, VC2)):
                for m in range(2):
                    ps = bank[2 * n + m]
                    for s in range(16):
                        pe.matmul(ps[:, 0:NCMP], w1[n][:, s, m * P:(m + 1) * P],
                                  src[:, 2 * s:2 * s + 16 * (NCMP - 1) + 1:16], start=(s == 0), stop=(s == 15))
                    for s in range(16):
                        mm = pe.matmul(bank[4 + 2 * n + m][:, 0:1], w1[n][:, s, m * P:(m + 1) * P],
                                       pe2[:, n, s:s + 1], start=(s == 0), stop=(s == 15))
                    mm.then_inc(S["ch_made"], 1)
            pe.wait_ge(S["ch_out"], 4)
            for m in range(2):
                mm = pe.matmul(bank[0][:, 0:NCMP], w2[:, 0, m, :], hT[0][:, m, 0:NCMP], start=(m == 0), stop=(m == 1))
            mm.then_inc(S["cc_made"], 1)
            for m in range(2):
                mm = pe.matmul(bank[1][0:NCMP, 0:HD], hT[1][:, m, 0:NCMP], w2[:, 1, m, 0:HD],
                               start=(m == 0), stop=(m == 1))
            mm.then_inc(S["cc_made"], 1)
            pe.wait_ge(S["cc_out"], 5)
            pe.wait_ge(S["k_low"], 2)
            pe.wait_ge(S["mask_ready"], 1)

            def scores(n):
                un = units[n]
                ps = bank[n % 3]
                if n >= 3:
                    pe.wait_ge(S["prob_made"], n - 2)
                if un[0] == "cmp":
                    i = un[1]
                    pe.matmul(ps[:].rearrange("p (h n) -> p h n", h=NH)[:, :, 0:NCMP], masks[:, K_ID:K_ID + P],
                              masks[:, None, K_CMP + P - 8 * i:K_CMP + P - 8 * i + NCMP].to_broadcast((P, NH, NCMP)),
                              start=True, stop=True)
                    for m in range(2):
                        mm = pe.matmul(ps[:, 2 * m * P:2 * (m + 1) * P].rearrange("p (h n) -> p h n", h=2)[:, :, 0:NCMP],
                                       QR[:, m, i * P:(i + 1) * P], kct[:, :, 0:NCMP],
                                       start=False, stop=True, skip_group_check=True)
                    mm.then_inc(S["s_made"], 1)
                    return
                br, i, h0, g, k0, t, slot, mask = un
                n_ = t * P
                if br == "slc" and i >= 8 and n == first_slc[i]:
                    pe.wait_ge(S["mask_rows"], i - 7)
                high, low = (KSH, KSL) if br == "slc" else (KWH, KWL)
                chosen = br == "slc" and i >= 8
                if mask:
                    m = masks[:, K_TRI + 512 - n_:K_TRI + 512] if mask == "tri" else masks[:, K_WIN:K_WIN + n_]
                    pe.matmul(ps[:, 0:g * n_].rearrange("p (g n) -> p g n", g=g), masks[:, K_ID:K_ID + P],
                              m[:, None, :].to_broadcast((P, g, n_)), start=True, stop=True)
                if chosen:
                    blocks = masks[0:NSEL, K_ID + 2 * k0:K_ID + 2 * (k0 + t)]
                    for q in range(g):
                        pe.matmul(ps[:, q * n_:(q + 1) * n_].rearrange("p (b k) -> p b k", k=64), qmask[:, i % 2, :],
                                  blocks[:, :, None].to_broadcast((NSEL, 2 * t, 64)), start=(not mask), stop=True,
                                  skip_group_check=bool(mask))
                for q in range(g):
                    for keys in (high, low):
                        mm = pe.matmul(ps[:, q * n_:(q + 1) * n_], QS[:, h0 + q, i * P:(i + 1) * P],
                                       keys[:, k0 * P:k0 * P + n_],
                                       start=(keys is high and not mask and not chosen), stop=True,
                                       skip_group_check=True)
                mm.then_inc(S["s_made"], 1)

            def turn(n):
                un = units[n]
                pe.wait_ge(S["prob_made"], n + 1)
                if n >= 2:
                    pe.wait_ge(S["pt_made"], n - 1)
                ps = bank[3 + n % 2]
                if un[0] == "cmp":
                    pe.wait_ge(S["pn_made"], un[1] + 1)
                    for h in range(NH):
                        mm = pe.transpose(ps[0:NCMP, h * P:(h + 1) * P], pn[un[1] % 2][:, h, 0:NCMP], ident)
                else:
                    for k in range(un[3] * un[5]):
                        mm = pe.transpose(ps[:, k * P:(k + 1) * P], prob[n % 4][:, k * P:(k + 1) * P], ident)
                mm.then_inc(S["t_made"], 1)

            def values(n):
                un = units[n]
                pe.wait_ge(S["pt_made"], n + 1)
                if n >= 2:
                    pe.wait_ge(S["o_out"], n - 1)
                ps = bank[5 + n % 2]
                pt = probT[n % 3]
                if un[0] == "cmp":
                    for h in range(NH):
                        mm = pe.matmul(ps[:, h * 65:h * 65 + HD], pt[0:NCMP, h * P:(h + 1) * P], vct[0:NCMP, :],
                                       start=True, stop=True)
                else:
                    br, i, h0, g, k0, t, slot, mask = un
                    v = VS if br == "slc" else VW
                    for q in range(g):
                        for k in range(t):
                            mm = pe.matmul(ps[:, q * 65:(q + 1) * 65], pt[:, (q * t + k) * P:(q * t + k + 1) * P],
                                           v[:, k0 + k, :], start=(k == 0), stop=(k == t - 1))
                mm.then_inc(S["o_made"], 1)

            rows, turned = [0], [0]

            def turn_mask(i):
                pe.wait_ge(S["mk_made"], i - 7)
                pe.wait_ge(S["yT_out"], rows[0])
                pe.transpose(bank[7][0:NSEL, 0:P], imp[0], ident).then_inc(S["mkT_made"], 1)
                turned[0] += 1

            def turn_rows(i):
                pe.wait_ge(S["y_made"], i + 1)
                if turned[0]:
                    pe.wait_ge(S["mask_rows"], turned[0])
                if i:
                    pe.wait_ge(S["yT_out"], i)
                rows[0] += 1
                for m in range(2):
                    mm = pe.transpose(bank[7][:, 256 + m * P:256 + (m + 1) * P], yrow[i % 2][:, m * P:(m + 1) * P], ident)
                mm.then_inc(S["yT_made"], 1)

            N = len(units)
            for n in range(-2, N + 5):
                for i in range(NT):
                    if i >= 8 and n + 2 == first_slc[i]:
                        turn_mask(i)
                    if n - 4 == last_of[i]:
                        turn_rows(i)
                if 0 <= n + 2 < N:
                    scores(n + 2)
                if 0 <= n < N:
                    turn(n)
                if 0 <= n - 1 < N:
                    values(n - 1)

            pe.wait_ge(S["wo_in"], 32)
            pe.wait_ge(S["ln_in"], 48)
            pe.wait_ge(S["yT_out"], NT)

            def mix(t):
                if t >= 2:
                    pe.wait_ge(S["mix_used"], 2 * (t - 1))
                for m in range(2):
                    for k in range(KD):
                        mm = pe.matmul(bank[2 * (t % 2) + m][:], yT[:, k, t * P:(t + 1) * P],
                                       (w_outa, w_outb)[k // 4][:, k % 4, m * 512:(m + 1) * 512], start=(k == 0), stop=(k == KD - 1))
                mm.then_inc(S["mix_made"], 1)

            def turn_x1(t):
                pe.wait_ge(S["x1_made"], t + 1)
                if t >= 1:
                    pe.wait_ge(S["xt_out"], 2 * t)
                for k in range(KD):
                    mm = pe.transpose(bank[4 + k // 4][:, (k % 4) * P:(k % 4 + 1) * P], x1row[t % 2][:, k * P:(k + 1) * P], ident)
                mm.then_inc(S["xt_made"], 1)

            def logits(t):
                pe.wait_ge(S["xt_out"], 2 * (t + 1))
                if t >= 1:
                    pe.wait_ge(S["lg_out"], t)
                for k in range(KD):
                    mm = pe.matmul(bank[6][:, 0:NE], x1T[t % 2][:, k, :], rw[:, k, :], start=(k == 0), stop=(k == KD - 1))
                mm.then_inc(S["lg_made"], 1)

            for t in range(NT + 2):
                if t < NT:
                    mix(t)
                if 1 <= t <= NT:
                    turn_x1(t - 1)
                if t >= 2:
                    logits(t - 2)

            pe.wait_ge(S["oh_made"], 1)
            oh = rt[0][:, :, :].rearrange("p a b -> p (a b)")
            pe.matmul(bank[0][:, 0:256], C(C_TRIU, P), oh, start=True, stop=True)
            pe.matmul(bank[1][:, 0:256], C(C_ONE, P), oh, start=True, stop=True).then_inc(S["cum_made"], 1)

            pe.wait_ge(S["tab_made"], 1)

            def turn_in(b, u, half_b=0):
                pe.wait_ge(S[f"g_in{u}"], 16 * (b // 2 if isinstance(b, int) else half_b) + 16)
                pe.wait_ge(S["gx_out"], 2 * b + 1)
                for k in range(KD):
                    mm = pe.transpose(bank[k // 4][:, (k % 4) * P:(k % 4 + 1) * P], xg[u][:, k * P:(k + 1) * P], ident)
                mm.then_inc(S["gx_made"], 1)

            pe.sem_inc(S["blk_done"], 1)
            pe.sem_inc(S["ht_made"], 2)
            turn_in(0, 0)
            with pe.Fori(0, NB // 2) as bb:
                for u in range(2):
                    b = bb * 2 + u
                    e = pe.value_load(tables[0:1, 0, bass.ds(b, 1)], min_val=0, max_val=NE - 1)
                    half = pe.value_load(tables[0:1, 2, bass.ds(b, 1)], min_val=0, max_val=1)
                    pe.wait_ge(S["we_in"], e * 48 + 48)
                    pe.wait_ge(S["gx_out"], 2 * b + 3)
                    pe.wait_ge(S["h_made"], b + 1)
                    for m in range(2):
                        for k in range(KD):
                            at = m * KD * DE + k * DE
                            mm = pe.matmul(bank[2 + m][:], xgT[u][:, k, :],
                                           wx[:, bass.ds(half, 1), at:at + DE].rearrange("p a n -> p (a n)"),
                                           start=(k == 0), stop=(k == KD - 1))
                    mm.then_inc(S["gu_made"], 1)
                    nxt = b + 1
                    turn_in(nxt, 1 - u, bb + u)
                    pe.wait_ge(S["h_made"], b + 2)
                    pe.wait_ge(S["ht_out"], b + 1)
                    for k in range(4):
                        mm = pe.transpose(bank[4][:, k * P:(k + 1) * P], hrow[u][:, k * P:(k + 1) * P], ident)
                    mm.then_inc(S["ht_made"], 1)
                    pe.wait_ge(S["ht_out"], b + 2)
                    pe.wait_ge(S["dn_outa"], b + 1)
                    pe.wait_ge(S["dn_outd"], b + 1)
                    for k in range(4):
                        for m in range(2):
                            at = 2 * KD * DE + k * D + m * 512
                            mm = pe.matmul(bank[5 + m][:], hTm[u][:, k, :],
                                           wx[:, bass.ds(half, 1), at:at + 512].rearrange("p a n -> p (a n)"),
                                           start=(k == 0), stop=(k == 3))
                    mm.then_inc(S["blk_done"], 1)

        @block.scalar
        def _(act):
            act.sem_inc(S["tile_out"], NBANK)
            act.wait_ge(S["chan_in"], 32)
            act.wait_ge(S["zeroed"], 1)

            def apart():
                act.wait_ge(S["zeroed"], 1)

            with act.Fori(0, NCH // 2) as cc:
                for u in range(2):
                    c = cc * 2 + u
                    cols = bass.ds(c * TC, TC)
                    slot = {M_BG0: (0, 6), M_BV0: (1, 6), M_BG1: (2, 7), M_BV1: (3, 5), M_KS: (0, 8),
                            M_AC0: (1, 8), M_AH0: (2, 9), M_AB0: (3, 9), M_AC1: (0, 10), M_AH1: (1, 11), M_AB1: (2, 11)}

                    def copy_out(j):
                        ps = bank[j % NBANK]
                        if j not in slot:
                            apart()
                        act.wait_ge(S["tile_made"], MJ * c + MJ + 1 + j + 1)
                        if j in slot:
                            s, v = slot[j]
                            act.wait_ge(S["stage_free"], 7 * c + v)
                            f = ACT.Sigmoid if j in (M_BG0, M_BG1) else ACT.Copy
                            act.activation(stage[s], ps[:], f).then_inc(S["tile_out"], 1)
                        elif j == M_KC:
                            act.activation(KC2[:, cols], ps[:], ACT.Copy).then_inc(S["tile_out"], 1)
                        elif j in (M_Q0, M_Q1):
                            act.activation(QR[:, j - M_Q0, cols], ps[:], ACT.Copy, scale=0.125
                                           ).then_inc(S["tile_out"], 1)
                        elif j in (M_C0, M_C1):
                            n = j - M_C0
                            act.wait_ge(S["cpad_free"], 2 * c + n + 1)
                            act.activation(cpad[n][:, HC:HC + TC], ps[:], ACT.Copy).then_inc(S["tile_out"], 1)
                        else:
                            v = ps[:, 0:2 * NTM].rearrange("p (s n) -> p s n", s=2)
                            t0 = c * 4 + (j - NM) * 2
                            act.activation(VS[:, bass.ds(t0, 2), 0:64], v[:, :, 0:64], ACT.Copy)
                            act.activation(VW[:, bass.ds(t0, 2), 0:64], v[:, :, 64:128], ACT.Copy)
                            act.activation(gates[:, bass.ds(t0, 2), :], v[:, :, 128:140], ACT.Sigmoid
                                           ).then_inc(S["tile_out"], 1)

                    for j in range(M_AB0 + 1):
                        copy_out(j)
                    for n, t in enumerate((t1, t2)):
                        apart()
                        act.wait_ge(S["cent"], 2 * c + n + 1)
                        act.activation(t, yT[:, 2 + n, cols], ACT.Square).then_inc(S["squared"], 1)
                    for n in range(2):
                        apart()
                        act.wait_ge(S["sp_made"], 7 * c + 5 + n)
                        act.activation(yT[:, 4 + n, cols], bank[6 + n][:], ACT.Copy,
                                       scale=chan[:, CH_PS + n:CH_PS + n + 1]).then_inc(S[f"free{6 + n}"], 1)
                    for j in (M_AC1, M_AH1, M_AB1):
                        copy_out(j)
                    act.wait_ge(S["sp_made"], 7 * c + 7)
                    act.activation(sd, bank[6][:], ACT.Sqrt, bias=chan[:, CH_EPS:CH_EPS + 1]).then_inc(S["std"], 1)
                    act.wait_ge(S["std"], c + 1)
                    act.sem_inc(S["free6"], 1)
                    copy_out(NM)
                    copy_out(NM + 1)
                    for n in range(2):
                        apart()
                        act.wait_ge(S["zed"], 2 * c + n + 1)
                        act.activation(yT[:, 2 + n, cols], yT[:, 2 + n, cols], ACT.Silu,
                                       scale=chan[:, CH_G + n:CH_G + n + 1],
                                       bias=chan[:, CH_BE + n:CH_BE + n + 1]).then_inc(S["yb_done"], 1)
            for n in range(2):
                for m in range(2):
                    act.wait_ge(S["ch_made"], 2 * n + m + 1)
                    act.activation(hbias[:, 2 * n + m:2 * n + m + 1], bank[4 + 2 * n + m][:, 0:1], ACT.Copy
                                   ).then_inc(S["cd_step"], 1)
                    act.wait_ge(S["cd_step"], 2 * n + m + 1)
                    act.activation(hT[n][:, m, 0:NCMP], bank[2 * n + m][:, 0:NCMP], ACT.Silu,
                                   bias=hbias[:, 2 * n + m:2 * n + m + 1]).then_inc(S["ch_out"], 1)
            act.wait_ge(S["ch_made"], 2)
            for high, keys in ((KSH, KS), (KWH, KW)):
                act.activation(high, keys, ACT.Copy).then_inc(S["k_high"], 1)
            act.wait_ge(S["cc_made"], 2)
            for n in range(2):
                r = slice(64 * n, 64 * n + 64)
                act.activation(kct[r, n, 0:NCMP], bank[0][r, 0:NCMP], ACT.Copy).then_inc(S["cc_out"], 1)
            act.activation(vct[0:NCMP, :], bank[1][0:NCMP, 0:HD], ACT.Copy).then_inc(S["cc_out"], 1)

            def exps(n):
                un = units[n]
                act.wait_ge(S["max_made"], n + 1)
                if n >= 4:
                    act.wait_ge(S["t_made"], n - 3)
                if un[0] == "cmp":
                    i = un[1]
                    if i >= 2:
                        act.wait_ge(S["t_made"], cmp_at[i - 2] + 1)
                    for h in range(NH):
                        e = act.activation(pn[i % 2][:, h, 0:NCMP], bank[n % 3][:, h * P:h * P + NCMP], ACT.Exp,
                                           bias=nmx[i % 2][:, h, 7:8])
                else:
                    br, i, h0, g, k0, t, slot, mask = un
                    for q in range(g):
                        r = slice(q * t * P, (q + 1) * t * P)
                        e = act.activation(prob[n % 4][:, r], bank[n % 3][:, r], ACT.Exp,
                                           bias=nmx[i % 2][:, h0 + q, slot:slot + 1])
                e.then_inc(S["prob_made"], 1)

            def outs(n):
                un = units[n]
                act.wait_ge(S["o_made"], n + 1)
                ps = bank[5 + n % 2]
                if un[0] == "cmp":
                    i = un[1]
                    if i >= 2:
                        act.wait_ge(S["y_made"], i - 1)
                    act.activation(OB[i % 2][:, :, n_slc[i] + n_win[i], 0:HD],
                                   ps[:, 0:NH * 65].rearrange("p (h n) -> p h n", h=NH)[:, :, 0:HD], ACT.Copy
                                   ).then_inc(S["o_out"], 1)
                else:
                    br, i, h0, g, k0, t, slot, mask = un
                    act.activation(OB[i % 2][:, h0:h0 + g, slot, :],
                                   ps[:, 0:g * 65].rearrange("p (h n) -> p h n", h=g), ACT.Copy).then_inc(S["o_out"], 1)

            N = len(units)
            for n in range(-1, N + 5):
                for i in range(NT):
                    if n - 2 == last_of[i]:
                        act.wait_ge(S["d_made"], i + 1)
                        ns = n_slc[i] + n_win[i]
                        v = small[:, 0:4, 8:8 + ns]
                        act.activation(v, v, ACT.Exp).then_inc(S["f_made"], 1)
                for i in range(NT):
                    if n - 4 == last_of[i]:
                        act.wait_ge(S["yT_made"], i + 1)
                        act.activation(yT[:, 6:8, i * P:(i + 1) * P],
                                       bank[7][:, 256:512].rearrange("p (m n) -> p m n", m=2), ACT.Copy
                                       ).then_inc(S["yT_out"], 1)
                if 0 <= n + 1 < N:
                    exps(n + 1)
                if 0 <= n - 1 < N:
                    outs(n - 1)
            for t in range(NT + 1):
                if t < NT:
                    act.wait_ge(S["sq_in"], t + 1)
                    act.activation(bst[t % 2][:, 14:15], bst[t % 2][:, 13:14], ACT.Sqrt,
                                   bias=chan[:, CH_EPS:CH_EPS + 1]).then_inc(S["sq_out"], 1)
                if t >= 1:
                    q = t - 1
                    act.wait_ge(S["xt_made"], q + 1)
                    if q >= 2:
                        act.wait_ge(S["lg_made"], q - 1)
                    for m in range(2):
                        act.activation(x1T[q % 2][:, 4 * m:4 * m + 4, :].rearrange("p a b -> p (a b)"), bank[4 + m][:],
                                       ACT.Copy).then_inc(S["xt_out"], 1)
                if t >= 2:
                    q = t - 2
                    act.wait_ge(S["lg_made"], q + 1)
                    act.activation(lgt[:, q, :], bank[6][:, 0:NE], ACT.Copy).then_inc(S["lg_out"], 1)
            act.wait_ge(S["lg_made"], NT)
            act.activation(lgt[:, NT - 1, :], bank[6][:, 0:NE], ACT.Copy).then_inc(S["lg_out"], 1)
            act.wait_ge(S["lg_out"], NT)
            act.activation(aff[:, :, :], lgt[:, :, :], ACT.Sigmoid).then_inc(S["aff_made"], 1)
            act.sem_inc(S["gx_out"], 1)
            act.sem_inc(S["dn_outa"], 1)
            act.sem_inc(S["ysto0"], 16)
            act.sem_inc(S["ysto1"], 16)
            act.wait_ge(S["tab_made"], 1)

            def copy_in(b, u):
                act.wait_ge(S["gx_made"], b + 1)
                for m in range(2):
                    act.activation(xgT[u][:, 4 * m:4 * m + 4, :].rearrange("p a b -> p (a b)"), bank[m][:],
                                   ACT.Copy).then_inc(S["gx_out"], 1)

            copy_in(0, 0)
            with act.Fori(0, NB // 2) as bb:
                for u in range(2):
                    b = bb * 2 + u
                    act.wait_ge(S["gu_made"], b + 1)
                    act.wait_ge(S["ht_made"], b + 1)
                    act.activation(hrow[u], bank[2][:], ACT.Silu).then_inc(S["act_made"], 1)
                    copy_in(b + 1, 1 - u)
                    act.wait_ge(S["blk_done"], b + 2)
                    act.wait_ge(S[f"ysto{u}"], 16 * bb + 16)
                    act.activation(yrw[u][:, 0:512], bank[5][:], ACT.Copy).then_inc(S["dn_outa"], 1)
                    act.wait_ge(S["dn_outa"], b + 2)
                    act.wait_ge(S["dn_outd"], b + 2)
                    act.dma_start(y_dram[bass.ds(b * P, P), :], yrw[u]).then_inc(S[f"ysto{u}"], 16)
            act.sem_inc(S["out60"], 16)
            act.sem_inc(S["out61"], 16)
            with act.Fori(0, NT // 2) as tt:
                for u in range(2):
                    t = tt * 2 + u
                    act.wait_ge(S["s6_in"], t + 1)
                    act.activation(b6[u][:, 14:15], b6[u][:, 13:14], ACT.Sqrt,
                                   bias=chan[:, CH_EPS:CH_EPS + 1]).then_inc(S["s6_out"], 1)
                    act.wait_ge(S["p6"], t + 1)
                    act.dma_start(out[bass.ds(t * P, P), :], fin[u]).then_inc(S[f"out6{u}"], 16)

        @block.vector
        def _(ve):
            V_STEPS = [0]

            def step(ins):
                V_STEPS[0] += 1
                ins.then_inc(S["dve_step"], 1)
                return V_STEPS[0]

            ve.sem_inc(S["stage_free"], 7)
            ve.sem_inc(S["cpad_free"], 2)
            ve.sem_inc(S["rope_made"], 1)
            ve.sem_inc(S["free6"], 1)
            ve.sem_inc(S["free7"], 1)
            for t in bpad:
                ve.memset(t[:, 0:HB], 0.0)
            for t in cpad:
                ve.memset(t[:, 0:HC], 0.0)
            for t in apad:
                ve.memset(t[:, 0:HA], 0.0)
            ve.memset(VS[:, :, 64:65], 1.0)
            ve.memset(VW[:, :, 64:65], 1.0)
            ve.wait_ge(S["const_in"], 16)
            ve.wait_ge(S["chan_in"], 32)
            ve.wait_ge(S["mk_in"], 16)
            ve.tensor_copy(tok_i[:, :], C(C_TOK, NT))
            ve.tensor_copy(masks[:, :], yT[:, 6, 0:NMASK]).then_inc(S["zeroed"], 1)
            ve.wait_ge(S["zeroed"], 1)
            ve.sem_inc(S["mask_ready"], 1)
            w = lambda at: chan[:, at:at + 1]
            PER = 88
            with ve.Fori(0, NCH // 2) as cc:
                for u in range(2):
                    c = cc * 2 + u
                    cols = bass.ds(c * TC, TC)
                    V_STEPS[0] = 0

                    def need(n):
                        ve.wait_ge(S["dve_step"], PER * c + n)

                    at = [0, 0]
                    for n in range(2):
                        ve.wait_ge(S["tile_out"], MJ * c + NBANK + 2 * n + 2)
                        ve.tensor_tensor(bpad[n][:, HB:HB + TC], stage[2 * n], stage[2 * n + 1], ALU.mult
                                         ).then_inc(S["stage_free"], 1)
                    for k in range(CK):
                        for n in range(2):
                            acc = yT[:, 2 + n, cols]
                            if k == 0:
                                ve.wait_ge(S["stage_free"], 7 * c + 8 + n)
                                ins = ve.tensor_scalar(acc, bpad[n][:, 0:TC], w(CH_B + n * CK), w(CH_BB + n),
                                                       ALU.mult, ALU.add)
                            else:
                                need(at[n])
                                ins = ve.scalar_tensor_tensor(acc, bpad[n][:, k:k + TC], w(CH_B + n * CK + k), acc,
                                                              ALU.mult, ALU.add)
                            if k < CK - 1:
                                at[n] = step(ins)
                            else:
                                ins.then_inc(S["conv_made"], 1)
                    for n in range(2):
                        step(ve.tensor_copy(bpad[n][:, 0:HB], bpad[n][:, TC:TC + HB]))

                    ve.wait_ge(S["cs_in"], 16 * c + 16)
                    srcs = [(stage[0], bank[6], "free6"), (QR[:, 0, cols], bank[7], "free7"),
                            (QR[:, 1, cols], bank[6], "free6")]
                    for n, (src, ps, free) in enumerate(srcs):
                        ve.wait_ge(S["sp_made"], 7 * c + n + 1)
                        if n:
                            ve.wait_ge(S["rope_made"], 3 * c + n + 1)
                        x1_ = step(ve.tensor_tensor(t1, src, cs[:, 0, :], ALU.mult))
                        ve.tensor_tensor(t2, ps[:], cs[:, 1, :], ALU.mult).then_inc(S[free], 1)
                        need(x1_)
                        ve.wait_ge(S[free], {0: 4 * c + 2, 1: 3 * c + 2, 2: 4 * c + 3}[n])
                        if n == 0:
                            for m, keys in enumerate((KS, KW)):
                                r = slice(64 * m, 64 * m + 64)
                                for to in (slice(0, 64), slice(64, 128)):
                                    ins = ve.tensor_tensor(keys[to, cols], t1[r, :], t2[r, :], ALU.add)
                            ins.then_inc(S["rope_made"], 1)
                        else:
                            q = step(ve.tensor_tensor(t1, t1, t2, ALU.add))
                            need(q)
                            q = step(ve.tensor_copy(t2r, t1))
                            need(q)
                            for m in range(2):
                                r = slice(64 * m, 64 * m + 64)
                                ve.tensor_tensor(QS[64:128, 2 * n - 2 + m, cols], t1[r, :], t2r[r, :].bitcast(F32), ALU.subtract)
                                ins = ve.tensor_scalar(QS[0:64, 2 * n - 2 + m, cols], t2r[r, :].bitcast(F32), 1.0, None, ALU.mult)
                            ins.then_inc(S["rope_made"], 1)
                        if n == 0:
                            ve.wait_ge(S["rope_made"], 3 * c + 2)
                            ve.sem_inc(S["stage_free"], 1)

                    for n in range(2):
                        x = cpad[n]
                        ve.wait_ge(S["tile_out"], MJ * c + NBANK + M_C0 + n + 1)
                        E = HC + TC
                        q = step(ve.tensor_tensor(s_a[:, 1:E], x[:, 1:E], x[:, 0:E - 1], ALU.add))
                        need(q)
                        if n == 0:
                            q = step(ve.tensor_tensor(s_b[64:128, 3:E], s_a[64:128, 3:E], s_a[64:128, 1:E - 2], ALU.add))
                        else:
                            q = step(ve.tensor_tensor(s_b[:, 3:E], s_a[:, 3:E], s_a[:, 1:E - 2], ALU.add))
                            need(q)
                            q = step(ve.tensor_tensor(s_a[:, 7:E], s_b[:, 7:E], s_b[:, 3:E - 4], ALU.add))
                            need(q)
                            q = step(ve.tensor_tensor(s_b[64:128, 15:E], s_a[64:128, 15:E], s_a[64:128, 7:E - 8], ALU.add))
                        need(q)
                        for lo, sm in ((0, s_a), (64, s_b)):
                            r = slice(lo, lo + 64)
                            ve.scalar_tensor_tensor(pd[n][r, 16:TC], sm[r, HC + 16:E], chan[r, CH_IW + n:CH_IW + n + 1],
                                                    x[r, HC + 16:E], ALU.mult, ALU.subtract)
                            pt = C_PT + n * NCH * 16
                            q = step(ve.tensor_tensor(pd[n][r, 0:16], sm[r, HC:HC + 16],
                                                      consts[r, bass.ds(c * 16 + pt, 16)], ALU.mult))
                            need(q)
                            ins = ve.tensor_tensor(pd[n][r, 0:16], pd[n][r, 0:16], x[r, HC:HC + 16], ALU.subtract)
                            if lo:
                                ins.then_inc(S["pool_d"], 1)
                        ve.tensor_copy(x[:, 0:HC], x[:, TC:TC + HC]).then_inc(S["cpad_free"], 1)

                    ve.wait_ge(S["sp_made"], 7 * c + 4)
                    for n in range(2):
                        ins = ve.tensor_tensor(yT[:, 2 + n, cols], yT[:, 2 + n, cols], bank[7][:], ALU.subtract)
                        ins.then_inc(S["cent"], 1)
                    ve.wait_ge(S["cent"], 2 * c + 2)
                    ve.sem_inc(S["free7"], 1)

                    for n in range(2):
                        x = apad[n]
                        ve.wait_ge(S["tile_out"], MJ * c + NBANK + M_AH0 + 3 * n + 1)
                        cst, hst, bst_ = ((1, 2, 3), (0, 1, 2))[n]
                        ve.tensor_tensor(x[:, HA:HA + TC], stage[cst], stage[hst], ALU.mult).then_inc(S["stage_free"], 1)
                        ve.wait_ge(S["stage_free"], 7 * c + 11 + 2 * n)
                        q = step(ve.tensor_scalar(s_b[:, 0:TC], x[:, 0:TC], w(CH_A + 3 * n), None, ALU.mult))
                        for k in (1, 2):
                            need(q)
                            q = step(ve.scalar_tensor_tensor(s_b[:, 0:TC], x[:, k:k + TC], w(CH_A + 3 * n + k), s_b[:, 0:TC],
                                                             ALU.mult, ALU.add))
                        q = step(ve.tensor_copy(x[:, 0:HA], x[:, TC:TC + HA]))
                        need(q)
                        ve.wait_ge(S["tile_out"], MJ * c + NBANK + M_AB0 + 3 * n + 1)
                        ve.tensor_tensor(yT[:, n, cols], s_b[:, 0:TC], stage[bst_], ALU.mult).then_inc(S["stage_free"], 1)
                        ve.wait_ge(S["stage_free"], 7 * c + 12 + 2 * n)

                    ve.wait_ge(S["std"], c + 1)
                    q = step(ve.reciprocal(sd, sd))
                    need(q)
                    for n in range(2):
                        ve.tensor_tensor(yT[:, 2 + n, cols], yT[:, 2 + n, cols], sd, ALU.mult).then_inc(S["zed"], 1)
                    ve.wait_ge(S["zed"], 2 * c + 2)
                    assert V_STEPS[0] == PER, V_STEPS[0]
            BASE = PER * NCH
            V_STEPS[0] = 0

            def need(n):
                ve.wait_ge(S["dve_step"], BASE + n)

            ve.wait_ge(S["tile_out"], MJ * NCH + NBANK)
            ve.wait_ge(S["yb_done"], 2 * NCH)
            ve.wait_ge(S["sp_made"], 7 * NCH)
            ve.tensor_copy(VC2[0:64, :], KC2[64:128, :])
            ve.tensor_copy(VC2[64:128, 0:SEQ - 1], KC2[64:128, 1:SEQ]).then_inc(S["shifted"], 1)
            ve.wait_ge(S["shifted"], 1)
            ve.tensor_copy(KC2[64:128, 0:SEQ - 1], KC2[0:64, 1:SEQ]).then_inc(S["shifted"], 1)
            step(ve.memset(psm, 0.0))
            for n, (high, keys, low) in enumerate(((KSH, KS, KSL), (KWH, KW, KWL))):
                ve.wait_ge(S["k_high"], n + 1)
                ve.tensor_tensor(low, keys, high.bitcast(F32), ALU.subtract).then_inc(S["k_low"], 1)
            ve.memset(kct[64:128, 0, :], 0.0).then_inc(S["cc_out"], 1)
            ve.memset(kct[0:64, 1, :], 0.0).then_inc(S["cc_out"], 1)

            def maxes(n):
                un = units[n]
                ve.wait_ge(S["s_made"], n + 1)
                ps = bank[n % 3]
                if un[0] == "cmp":
                    ins = ve.tensor_reduce(nmx[un[1] % 2][:, :, 7:8],
                                           ps[:].rearrange("p (h n) -> p h n", h=NH)[:, :, 0:NCMP], AX.X, ALU.max, negate=True)
                else:
                    br, i, h0, g, k0, t, slot, mask = un
                    ins = ve.tensor_reduce(nmx[i % 2][:, h0:h0 + g, slot:slot + 1],
                                           ps[:, 0:g * t * P].rearrange("p (g n) -> p g n", g=g), AX.X, ALU.max, negate=True)
                ins.then_inc(S["max_made"], 1)

            def normalise(n):
                i = units[n][1]
                ve.wait_ge(S["prob_made"], n + 1)
                p_ = pn[i % 2]
                tot, inv = small[:, 0:4, 20:21], small[:, 0:4, 21:22]
                q = step(ve.tensor_reduce(tot, p_[:, :, 0:NCMP], AX.X, ALU.add))
                need(q)
                q = step(ve.reciprocal(inv, tot))
                need(q)
                if i == 0:
                    q = step(ve.tensor_scalar(inv, inv, C(C_VALID, 1), None, ALU.mult))
                    need(q)
                ve.tensor_tensor(p_[:, :, 0:NCMP], p_[:, :, 0:NCMP], inv.to_broadcast((P, NH, NCMP)), ALU.mult
                                 ).then_inc(S["pn_made"], 1)

            def copy_turned(n):
                un = units[n]
                ve.wait_ge(S["t_made"], n + 1)
                if n >= 3:
                    ve.wait_ge(S["o_made"], n - 2)
                ps = bank[3 + n % 2]
                if un[0] == "cmp":
                    ins = ve.tensor_copy(probT[n % 3][0:NCMP, :], ps[0:NCMP, :])
                else:
                    w_ = un[3] * un[5] * P
                    ins = ve.tensor_copy(probT[n % 3][:, 0:w_], ps[:, 0:w_])
                ins.then_inc(S["pt_made"], 1)

            def importance(i):
                ve.wait_ge(S["pn_made"], i + 1)
                q = step(ve.tensor_reduce(psm[:, 1:1 + NCMP].rearrange("p (n o) -> p n o", o=1),
                                          pn[i % 2][:, :, 0:NCMP].rearrange("p h n -> p n h"), AX.X, ALU.add))
                need(q)
                if i > 8:
                    ve.wait_ge(S["mkT_made"], i - 8)
                q = step(ve.tensor_reduce(imp[0].rearrange("p (n o) -> p n o", o=1),
                                          psm[:, 0:P].rearrange("p (j k) -> p j k", k=4), AX.X, ALU.add))
                need(q)
                q = step(ve.tensor_tensor(imp[0], imp[0], psm[:, 4:132:4], ALU.add))
                need(q)
                q = step(ve.tensor_tensor(imp[0], imp[0], C(C_KEEP + 32 - 2 * i, NSEL), ALU.mult))
                need(q)
                q = step(ve.tensor_tensor(imp[0], imp[0], C(C_ADD + 32 - 2 * i, NSEL), ALU.add))
                need(q)
                q = step(ve.memset(imp[0][:, 0:1], FORCE))
                need(q)
                m8 = small[:, 1, 22:30]
                for r in range(2):
                    src, dst = (imp[0], imp[1]) if r == 0 else (imp[1], imp[0])
                    q = step(ve.max(m8, src))
                    need(q)
                    q = step(ve.match_replace(dst, m8, src, USED))
                    need(q)
                ve.tensor_scalar(imp[0], imp[0], USED / 2, NEG, ALU.is_gt, ALU.mult).then_inc(S["mk_made"], 1)

            def rows_of_mask(i):
                ve.wait_ge(S["mkT_made"], i - 7)
                ve.tensor_copy(qmask[:, i % 2, :], bank[7][0:NSEL, 0:P]).then_inc(S["mask_rows"], 1)

            MM = small[:, 0:4, 0:2]
            LL, RR = small[:, 4:8, 0:2], small[:, 4:8, 2:4]

            def shifts(i):
                ns, nw = n_slc[i], n_win[i]
                q = step(ve.tensor_reduce(MM[:, :, 0:1], nmx[i % 2][:, :, 0:ns], AX.X, ALU.min))
                q = step(ve.tensor_reduce(MM[:, :, 1:2], nmx[i % 2][:, :, ns:ns + nw], AX.X, ALU.min))
                need(q)
                for m, (lo, k) in enumerate(((0, ns), (ns, nw))):
                    ins = ve.tensor_tensor(small[:, 0:4, 8 + lo:8 + lo + k], MM[:, :, m:m + 1].to_broadcast((P, NH, k)),
                                           nmx[i % 2][:, :, lo:lo + k], ALU.subtract)
                    if m == 0:
                        continue
                    ins.then_inc(S["d_made"], 1)

            def combine(i):
                ns, nw = n_slc[i], n_win[i]
                k = ns + nw
                F, FL, AL, ob = small[:, 0:4, 8:8 + k], small[:, 8:12, 0:k], small[:, 12:16, 0:k + 1], OB[i % 2]
                ve.wait_ge(S["f_made"], i + 1)
                ve.wait_ge(S["o_out"], last_of[i] + 1)
                q = step(ve.tensor_tensor(FL, F, ob[:, :, 0:k, 64], ALU.mult))
                need(q)
                step(ve.tensor_reduce(LL[:, :, 0:1], FL[:, :, 0:ns], AX.X, ALU.add))
                q = step(ve.tensor_reduce(LL[:, :, 1:2], FL[:, :, ns:k], AX.X, ALU.add))
                need(q)
                q = step(ve.reciprocal(RR, LL))
                need(q)
                gt = gates[:, i, :].rearrange("p (h g) -> p h g", g=3)
                q = step(ve.tensor_tensor(RR, RR, gt[:, :, 1:3], ALU.mult))
                need(q)
                step(ve.tensor_tensor(AL[:, :, 0:ns], F[:, :, 0:ns], RR[:, :, 0:1].to_broadcast((P, NH, ns)), ALU.mult))
                step(ve.tensor_tensor(AL[:, :, ns:k], F[:, :, ns:k], RR[:, :, 1:2].to_broadcast((P, NH, nw)), ALU.mult))
                q = step(ve.tensor_copy(AL[:, :, k:k + 1], gt[:, :, 0:1]))
                need(q)
                v = ob[:, :, 0:k + 1, 0:HD]
                q = step(ve.tensor_tensor(v, v, AL[:, :, :, None].to_broadcast((P, NH, k + 1, HD)), ALU.mult))
                need(q)
                if i >= 2:
                    ve.wait_ge(S["yT_made"], i - 1)
                ve.tensor_reduce(yrow[i % 2].rearrange("p (h d o) -> p h d o", h=NH, o=1),
                                 v.rearrange("p h n d -> p h d n"), AX.X, ALU.add).then_inc(S["y_made"], 1)

            N = len(units)
            for n in range(-1, N + 5):
                for i in range(NT):
                    if i >= 8 and n + 2 == first_slc[i]:
                        rows_of_mask(i)
                if 0 <= n + 1 < N:
                    maxes(n + 1)
                if 0 <= n < N:
                    if units[n][0] == "cmp":
                        normalise(n)
                    copy_turned(n)
                    if units[n][0] == "cmp" and units[n][1] >= 8:
                        importance(units[n][1])
                for i in range(NT):
                    if n - 2 == last_of[i]:
                        shifts(i)
                    if n - 3 == last_of[i]:
                        combine(i)

            ve.wait_ge(S["ln_in"], 48)
            for t in range(NT):
                u = t % 2
                r_, st = rrow[u], bst[u]
                ve.wait_ge(S["mix_made"], t + 1)
                ve.wait_ge(S[f"xr_in{u}"], 16 * (t // 2) + 16)
                for m in range(2):
                    c_ = slice(m * 512, (m + 1) * 512)
                    ve.scalar_tensor_tensor(r_[:, c_], xrow[u][:, c_], ALPHA, bank[2 * u + m][:], ALU.mult, ALU.add
                                            ).then_inc(S["mix_used"], 1)
                ve.wait_ge(S["mix_used"], 2 * (t + 1))
                step(ve.bn_stats(st[:, 0:6], r_[:, 0:512]))
                q = step(ve.bn_stats(st[:, 6:12], r_[:, 512:1024]))
                need(q)
                ve.bn_aggr(st[:, 12:14], st[:, 0:12]).then_inc(S["sq_in"], 1)
                ve.wait_ge(S["sq_out"], t + 1)
                q = step(ve.reciprocal(st[:, 15:16], st[:, 14:15]))
                need(q)
                if t >= 2:
                    ve.wait_ge(S["xt_made"], t - 1)
                    ve.wait_ge(S[f"x1_sto{u}"], 16 * (t // 2))
                ve.tensor_scalar(x1row[u], r_, st[:, 12:13], st[:, 15:16], ALU.subtract, ALU.mult
                                 ).then_inc(S["norm_made"], 1)

            ve.wait_ge(S["aff_made"], 1)
            ve.wait_ge(S["route_in"], 16)

            def do(ins):
                need(step(ins))

            b16 = lambda x, n: x[:, :, None].to_broadcast((P, NT, n))
            bia = rt[1]
            do(ve.tensor_tensor(bia[:, :, :], aff[:, :, :], rbias[:, None, :].to_broadcast((P, NT, NE)), ALU.add))
            v = bia[:, :, :].rearrange("p t (g k) -> p t g k", k=4)
            vk = [v[:, :, :, k] for k in range(4)]
            do(ve.tensor_tensor(r4[0][:, :, :], vk[0], vk[1], ALU.max))
            do(ve.tensor_tensor(r4[1][:, :, :], vk[0], vk[1], ALU.min))
            do(ve.tensor_tensor(r4[2][:, :, :], vk[2], vk[3], ALU.max))
            do(ve.tensor_tensor(r4[3][:, :, :], vk[2], vk[3], ALU.min))
            do(ve.tensor_tensor(r4[4][:, :, :], r4[0][:, :, :], r4[2][:, :, :], ALU.max))
            do(ve.tensor_tensor(r4[5][:, :, :], r4[0][:, :, :], r4[2][:, :, :], ALU.min))
            do(ve.tensor_tensor(r4[6][:, :, :], r4[1][:, :, :], r4[3][:, :, :], ALU.max))
            do(ve.tensor_tensor(r4[5][:, :, :], r4[5][:, :, :], r4[6][:, :, :], ALU.max))
            do(ve.tensor_tensor(r4[7][:, :, :], r4[4][:, :, :], r4[5][:, :, :], ALU.add))

            def first_max(out_, x, order, eq, wgt, m1, m2, n):
                do(ve.tensor_reduce(m1[:, :, None], x, AX.X, ALU.max))
                do(ve.tensor_tensor(eq, x, b16(m1, n), ALU.is_equal))
                do(ve.tensor_tensor(wgt, eq, order[:, None, :].to_broadcast((P, NT, n)), ALU.mult))
                do(ve.tensor_reduce(m2[:, :, None], wgt, AX.X, ALU.max))
                do(ve.tensor_tensor(out_, wgt, b16(m2, n), ALU.is_equal))

            first_max(r4[2][:, :, :], r4[7][:, :, :], C(C_GW, 4), r4[0][:, :, :], r4[1][:, :, :], r1[0], r1[1], 4)
            do(ve.tensor_copy(rt[2][:, :, :].rearrange("p t (g k) -> p t g k", k=4),
                              r4[2][:, :, :, None].to_broadcast((P, NT, 4, 4))))
            do(ve.tensor_tensor(rt[3][:, :, :], bia[:, :, :], rt[2][:, :, :], ALU.mult))
            do(ve.tensor_scalar(rt[4][:, :, :], rt[2][:, :, :], -NEG, NEG, ALU.mult, ALU.add))
            do(ve.tensor_tensor(rt[5][:, :, :], rt[3][:, :, :], rt[4][:, :, :], ALU.add))
            for c in range(2):
                oh = rt[8 + c][:, :, :]
                first_max(oh, rt[5][:, :, :], C(C_EW, NE), rt[6][:, :, :], rt[7][:, :, :], r1[2], r1[3], NE)
                do(ve.scalar_tensor_tensor(rt[5][:, :, :], oh, 2 * NEG, rt[5][:, :, :], ALU.mult, ALU.add))
                do(ve.tensor_tensor(rt[6][:, :, :], aff[:, :, :], oh, ALU.mult))
                do(ve.tensor_reduce(r1[4 + c][:, :, None], rt[6][:, :, :], AX.X, ALU.add))
            ve.tensor_tensor(rt[0][:, :, :], rt[8][:, :, :], rt[9][:, :, :], ALU.add).then_inc(S["oh_made"], 1)
            do(ve.tensor_tensor(r1[2], r1[4], r1[5], ALU.add))
            do(ve.reciprocal(r1[3], r1[2]))
            for c in range(2):
                do(ve.tensor_tensor(dest_w[:, c, :], r1[4 + c], r1[3], ALU.mult))
            ve.wait_ge(S["cum_made"], 1)
            fl = lambda t: t[:, :, :].rearrange("p a b -> p (a b)")
            do(ve.tensor_copy(fl(rt[10]), bank[0][:, 0:256]))
            do(ve.tensor_copy(fl(rt[11]), bank[1][:, 0:256]))
            do(ve.memset(rt[12][:, 0, :], 0.0))
            for t in range(1, NT):
                do(ve.tensor_tensor(rt[12][:, t, :], rt[12][:, t - 1, :], rt[11][:, t - 1, :], ALU.add))
            cnt, nblk, sb_, incl = (cnt16[:, k, :] for k in range(4))
            do(ve.tensor_tensor(cnt, rt[12][:, NT - 1, :], rt[11][:, NT - 1, :], ALU.add))
            do(ve.tensor_tensor(cmp256[:, :, :], cnt[:, :, None].to_broadcast((P, NE, NE)),
                                C(C_K128, NE)[:, None, :].to_broadcast((P, NE, NE)), ALU.is_gt))
            do(ve.tensor_reduce(nblk[:, :, None], cmp256[:, :, :], AX.X, ALU.add))
            do(ve.tensor_tensor(cmp256[:, :, :], C(C_LT, 256).rearrange("p (a b) -> p a b", a=NE),
                                nblk[:, None, :].to_broadcast((P, NE, NE)), ALU.mult))
            do(ve.tensor_reduce(sb_[:, :, None], cmp256[:, :, :], AX.X, ALU.add))
            do(ve.tensor_tensor(incl, sb_, nblk, ALU.add))
            do(ve.tensor_tensor(rt[13][:, :, :], rt[10][:, :, :], rt[12][:, :, :], ALU.add))
            do(ve.scalar_tensor_tensor(rt[13][:, :, :], sb_[:, None, :].to_broadcast((P, NT, NE)), float(P),
                                       rt[13][:, :, :], ALU.mult, ALU.add))
            for c in range(2):
                do(ve.tensor_tensor(rt[6][:, :, :], rt[8 + c][:, :, :], rt[13][:, :, :], ALU.mult))
                do(ve.tensor_reduce(r1[6 + c][:, :, None], rt[6][:, :, :], AX.X, ALU.add))
                do(ve.tensor_copy(dest_i[:, c, :], r1[6 + c]))
            ve.sem_inc(S["dest_made"], 1)
            do(ve.tensor_tensor(tb[0][0:1, :, :], incl[0:1, None, :].to_broadcast((1, 64, NE)),
                                consts[0:1, C_BIDX:C_BIDX + 64, None].to_broadcast((1, 64, NE)), ALU.is_le))
            do(ve.tensor_reduce(tb1[0][0:1, :, None], tb[0][0:1, :, :], AX.X, ALU.add))
            do(ve.tensor_scalar(tb1[0][0:1, :], tb1[0][0:1, :], float(NE - 1), None, ALU.min))
            do(ve.tensor_copy(tables[0:1, 0, :], tb1[0][0:1, :]))
            do(ve.tensor_copy(tables[0:1, 1, 0:NE], incl[0:1, :]))
            do(ve.tensor_scalar(tables[0:1, 2, :], tables[0:1, 0, :], 1, None, ALU.bitwise_and))
            ve.sem_inc(S["tab_made"], 1)

            ve.sem_inc(S["h_made"], 1)
            ve.sem_inc(S["ht_out"], 1)
            ve.sem_inc(S["dn_outd"], 1)
            with ve.Fori(0, NB // 2) as bb:
                for u in range(2):
                    b = bb * 2 + u
                    ve.wait_ge(S["act_made"], b + 1)
                    ve.tensor_tensor(hrow[u], hrow[u], bank[3][:], ALU.mult).then_inc(S["h_made"], 1)
                    ve.wait_ge(S["ht_made"], b + 3)
                    ve.tensor_copy(hTm[u][:, :, :].rearrange("p a b -> p (a b)"), bank[4][:]).then_inc(S["ht_out"], 1)
                    ve.wait_ge(S["blk_done"], b + 2)
                    ve.wait_ge(S[f"ysto{u}"], 16 * bb + 16)
                    ve.tensor_copy(yrw[u][:, 512:1024], bank[6][:]).then_inc(S["dn_outd"], 1)

            ve.sem_inc(S["r6"], 2)
            ve.sem_inc(S["c6"], 2)
            base6 = BASE + V_STEPS[0]
            with ve.Fori(0, NT // 2) as tt:
                for u in range(2):
                    t = tt * 2 + u
                    V_STEPS[0] = 6 * u
                    def need6(n):
                        ve.wait_ge(S["dve_step"], base6 + 12 * tt + n)
                    st = b6[u]
                    ve.wait_ge(S[f"ya_in{u}"], 32 * tt + 32)
                    q = step(ve.tensor_scalar(ya[u], ya[u], dest_w[:, 0, bass.ds(t, 1)], None, ALU.mult))
                    need6(q)
                    q = step(ve.scalar_tensor_tensor(ya[u], yb[u], dest_w[:, 1, bass.ds(t, 1)], ya[u], ALU.mult, ALU.add))
                    need6(q)
                    ve.wait_ge(S[f"xr6_in{u}"], 16 * tt + 16)
                    ve.scalar_tensor_tensor(ya[u], xr[u], ALPHA, ya[u], ALU.mult, ALU.add).then_inc(S["r6"], 1)
                    ve.wait_ge(S["r6"], t + 3)
                    step(ve.bn_stats(st[:, 0:6], ya[u][:, 0:512]))
                    q = step(ve.bn_stats(st[:, 6:12], ya[u][:, 512:1024]))
                    need6(q)
                    ve.sem_inc(S["stats6"], 1)
                    q = step(ve.bn_aggr(st[:, 12:14], st[:, 0:12]))
                    need6(q)
                    ve.sem_inc(S["s6_in"], 1)
                    ve.wait_ge(S["s6_out"], t + 1)
                    q = step(ve.reciprocal(st[:, 15:16], st[:, 14:15]))
                    need6(q)
                    ve.wait_ge(S[f"out6{u}"], 16 * tt + 16)
                    ve.tensor_scalar(fin[u], ya[u], st[:, 12:13], st[:, 15:16], ALU.subtract, ALU.mult
                                     ).then_inc(S["c6"], 1)

        @block.gpsimd
        def _(po):
            po.memset(zero_i[:, :], 0).then_inc(S["zero_made"], 1)
            po.wait_ge(S["ln_in"], 48)
            for t in range(NT):
                x_ = x1row[t % 2]
                po.wait_ge(S["norm_made"], t + 1)
                po.tensor_tensor(x_, x_, ln_g, ALU.mult).then_inc(S["n6"], 1)
                po.wait_ge(S["n6"], t + 1)
                po.tensor_tensor(x_, x_, ln_b, ALU.add).then_inc(S["x1_made"], 1)
                po.wait_ge(S["x1_made"], t + 1)
                po.dma_start(x1_dram[t * P:(t + 1) * P, :], x_).then_inc(S[f"x1_sto{t % 2}"], 16)
            po.wait_ge(S["slot_zero"], 16)
            po.wait_ge(S["dest_made"], 1)
            for c in range(2):
                for t in range(NT):
                    po.indirect_dma_start(slot_dram, bass.IndirectOffsetOnAxis(ap=dest_i[:, c, t:t + 1], axis=0),
                                          tok_i[:, t:t + 1], None).then_inc(S["slot_stored"], 16)
            po.wait_ge(S["slot_stored"], 32 * NT)
            po.wait_ge(S["x1_sto0"], 8 * NT)
            po.wait_ge(S["x1_sto1"], 8 * NT)
            po.wait_ge(S["tab_made"], 1)

            def fetch(b, u, n, wait_free):
                if wait_free:
                    po.wait_ge(S["gx_made"], b - 1)
                po.dma_start(idx[u][:, :], slot_dram[bass.ds(b * P, P), :]).then_inc(S[f"idx{u}"], 16)
                po.wait_ge(S[f"idx{u}"], 16 * n + 16)
                po.sem_inc(S["idx_in"], 1)
                po.indirect_dma_start(xg[u], None, x1_dram, bass.IndirectOffsetOnAxis(ap=idx[u][:, 0:1], axis=0)
                                      ).then_inc(S[f"g_in{u}"], 16)

            fetch(0, 0, 0, False)
            fetch(1, 1, 0, False)
            fetch(2, 0, 1, True)
            with po.Fori(0, NB // 2 - 1) as bb:
                for u in range(2):
                    fetch(bb * 2 + u + 3, 1 - u, bb + 1 + u, True)
            po.wait_ge(S["ysto0"], 16 + 8 * NB)
            po.wait_ge(S["ysto1"], 16 + 8 * NB)
            po.wait_ge(S["l2_in"], 32)
            po.wait_ge(S["gx_made"], NB + 1)

            def rows(t, u):
                for c, buf in enumerate((ya, yb)):
                    po.indirect_dma_start(buf[u], None, y_dram,
                                          bass.IndirectOffsetOnAxis(ap=dest_i[:, c, t:t + 1], axis=0)
                                          ).then_inc(S[f"ya_in{u}"], 16)

            rows(0, 0)
            rows(1, 1)
            for t in range(NT):
                u = t % 2
                po.wait_ge(S["c6"], t + 3)
                po.tensor_tensor(fin[u], fin[u], ln2_g, ALU.mult).then_inc(S["fin6"], 1)
                po.wait_ge(S["fin6"], t + 1)
                po.tensor_tensor(fin[u], fin[u], ln2_b, ALU.add).then_inc(S["p6"], 1)
                if t + 2 < NT:
                    rows(t + 2, u)


def layout(x, w_in, conv_a_w, conv_b_w, conv_b_b, cf_ln_g, cf_ln_b, pool_w, pool_scale,
           cmp_pe_k, cmp_pe_v, cmp_k_w1, cmp_k_w2, cmp_v_w1, cmp_v_w2, w_out,
           ln1_g, ln1_b, ln2_g, ln2_b, router_w, router_bias, moe_w_gate, moe_w_up, moe_w_down):
    x = np.asarray(x).reshape(SEQ, D)
    w_in = np.asarray(w_in)[0]
    tiles, tm = column_tiles()
    c, k, cs, iw = shape_constants()
    two = lambda v: np.asarray(v).reshape(2, P).T
    taps = lambda v, n: np.asarray(v)[0].reshape(n, 2, P).transpose(2, 1, 0).reshape(P, 2 * n)
    chan = np.concatenate([taps(conv_a_w, AK), taps(conv_b_w, CK), two(conv_b_b), two(cf_ln_g), two(cf_ln_b),
                           two(pool_scale), iw, np.full((P, 1), EPS, np.float32)], 1)
    pw = np.zeros((P, 2, P), np.float32)
    for g in range(4):
        r = slice(64 * (g % 2), 64 * (g % 2) + 64)
        pw[r, g // 2, r] = np.asarray(pool_w)[0, g]
    kt = lambda w_: np.asarray(w_).reshape(KD, P, -1).transpose(1, 0, 2)
    w2 = np.zeros((P, 2, 2, P), np.float32)
    for n, w_ in enumerate((cmp_k_w2, cmp_v_w2)):
        w_ = np.asarray(w_)[0].reshape(2, P, HD).transpose(1, 0, 2)
        w2[:, n, :, 0:HD] = w_
        w2[:, n, :, HD:] = w_
    pe2 = np.stack([np.asarray(p_)[0].reshape(16, P).T for p_ in (cmp_pe_k, cmp_pe_v)], 1)
    we = np.stack([np.asarray(moe_w_gate)[0].reshape(NE, KD, P, DE).transpose(0, 2, 1, 3).reshape(NE, P, KD * DE),
                   np.asarray(moe_w_up)[0].reshape(NE, KD, P, DE).transpose(0, 2, 1, 3).reshape(NE, P, KD * DE),
                   np.asarray(moe_w_down)[0].reshape(NE, 4, P, D).transpose(0, 2, 1, 3).reshape(NE, P, 4 * D)], 1)
    arrays = {
        "x": x,
        "xT": x.reshape(NCH, TC, KD, P).transpose(0, 3, 2, 1).reshape(NCH, P, KD * TC),
        "w_in": np.stack([kt(w_in[:, t]).reshape(P, KD * P) for t in tiles]),
        "w_tm": kt(w_in[:, tm]).reshape(P, -1),
        "consts": c, "masks": k, "cs": cs, "chan": chan, "pool_w": pw.reshape(P, -1),
        "cmp_w1": np.stack([np.asarray(w_)[0].reshape(16, P, CHID).transpose(1, 0, 2).reshape(P, -1)
                            for w_ in (cmp_k_w1, cmp_v_w1)]),
        "cmp_w2": w2.reshape(P, -1), "cmp_pe": pe2.reshape(P, -1),
        "w_out": np.asarray(w_out)[0].reshape(2, KD // 2, P, D).transpose(0, 2, 1, 3).reshape(2, P, -1),
        "ln1_g": np.asarray(ln1_g)[0], "ln1_b": np.asarray(ln1_b)[0],
        "ln2_g": np.asarray(ln2_g)[0], "ln2_b": np.asarray(ln2_b)[0],
        "router_w": kt(router_w).reshape(P, -1), "router_bias": np.asarray(router_bias), "w_exp": we,
    }
    return {"in_" + n: np.ascontiguousarray(v) for n, v in arrays.items()}


def kernel(**inputs):
    import concourse.bacc as bacc
    from concourse.bass_utils import run_bass_kernel_spmd

    arrays = layout(**inputs)
    nc = bacc.Bacc("TRN2", target_bir_lowering=False, num_devices=1, dynamic_dma_scratch_size=2048)
    aps = {n[3:]: nc.dram_tensor(n, v.shape, F32, kind="ExternalInput").ap() for n, v in arrays.items()}
    out = nc.dram_tensor("out", (SEQ, D), F32, kind="ExternalOutput").ap()
    hybrid_layer(nc, aps, out)
    r = run_bass_kernel_spmd(nc, [arrays], core_ids=[0])
    return r.results[0]["out"].reshape(1, SEQ, D)
```

```python
from contextlib import ExitStack

import numpy as np
import concourse.bass as bass
import concourse.mybir as mybir

F32 = mybir.dt.float32
BF16 = mybir.dt.bfloat16
F32R = mybir.dt.float32r
I32 = mybir.dt.int32
ACT = mybir.ActivationFunctionType
ALU = mybir.AluOpType
AX = mybir.AxisListType

P = 128
SEQ, D = 2048, 1024
KD = D // P
TC = 512
NCH = SEQ // TC
NT = SEQ // P
GW = 256
HD = 64
NH = 4
CK, AK = 31, 3
HB, HA, HC = CK - 1, AK - 1, 16
NCMP = (SEQ - 32) // 16 + 1
CHID = 256
NSEL = SEQ // 64
WT = 4
NE, DE = 16, 512
R6 = 4
ALPHA = 2.0 ** 0.25
EPS = 1e-5
NEG = -1e30
FORCE = 1e4
USED = -3e38
NB = (2 * SEQ + NE * (P - 1)) // P + 1
NB += NB % 2
NBMIN = 2 * SEQ // P

M_BG0, M_BV0, M_BG1, M_BV1, M_KC, M_KS, M_Q0, M_Q1, M_C0, M_C1 = range(10)
M_AC0, M_AH0, M_AB0, M_AC1, M_AH1, M_AB1 = range(10, 16)
NM = 16
NTM = 140
MJ = NM + 2
NBANK = 6


def column_tiles():
    r = lambda a, n=P: list(range(a, a + n))
    o_b, o_c, o_h, o_val, o_gate, o_p, o_q, o_kc = 0, 256, 512, 768, 1024, 1280, 1536, 1792
    vc, ks, vs, kw, vw, g = (o_kc + 64 * n for n in range(1, 7))
    tiles = [r(o_gate), r(o_val), r(o_gate + P), r(o_val + P), r(o_kc, 64) + r(vc, 64), r(ks, 64) + r(kw, 64),
             r(o_q), r(o_q + P), r(o_p), r(o_p + P),
             r(o_c), r(o_h), r(o_b), r(o_c + P), r(o_h + P), r(o_b + P)]
    return tiles, r(vs, 64) + r(vw, 64) + r(g, 12)


CH_A, CH_B, CH_BB, CH_G, CH_BE, CH_PS, CH_IW, CH_EPS = 0, 6, 68, 70, 72, 74, 76, 78
NCHAN = 79

C_PERM, C_MEAN, C_ID, C_ONE, C_TRIU = 0, P, 2 * P, 3 * P, 4 * P
C_VALID = 5 * P
C_KEEP = C_VALID + 4
C_ADD = C_KEEP + 64
C_EW = C_ADD + 64
C_GW = C_EW + 16
C_K128 = C_GW + 4
C_LT = C_K128 + 16
C_BIDX = C_LT + 256
C_TOK = C_BIDX + 64
C_PT = C_TOK + 16
NCONST = C_PT + 2 * NCH * 16
K_ID, K_TRI, K_WIN, K_CMP = 0, P, P + 512, P + 1024
NMASK = K_CMP + 256


def shape_constants():
    p = np.arange(P)[:, None]
    c = np.zeros((P, NCONST), np.float32)
    perm = np.zeros((P, P), np.float32)
    for m in range(P):
        b, d = m // 64 * 64, m % 64
        if d < 32:
            perm[b + d + 32, m] = -1.0
        else:
            perm[b + d - 32, m] = 1.0
    c[:, C_PERM:C_PERM + P] = perm
    c[:, C_MEAN:C_MEAN + P] = 1.0 / GW
    c[:, C_ID:C_ID + P] = np.eye(P)
    c[:, C_ONE:C_ONE + P] = 1.0
    c[:, C_TRIU:C_TRIU + P] = (p < np.arange(P)[None])
    c[:, C_VALID] = (p[:, 0] >= 31)
    j = np.arange(64)[None] - 32
    cur = p // 64
    forced = (j == cur) | (j == cur - 1)
    future = j > cur
    c[:, C_KEEP:C_KEEP + 64] = ~(forced | future)
    c[:, C_ADD:C_ADD + 64] = np.where(future, NEG, np.where(forced, FORCE, 0.0))
    c[:, C_EW:C_EW + 16] = 16 - np.arange(16)
    c[:, C_GW:C_GW + 4] = 4 - np.arange(4)
    c[:, C_K128:C_K128 + 16] = P * np.arange(16)
    e = np.arange(16)
    c[:, C_LT:C_LT + 256] = (e[None, :] < e[:, None]).reshape(1, 256)
    c[:, C_BIDX:C_BIDX + 64] = np.arange(64)
    c[:, C_TOK:C_TOK + 16] = p + P * np.arange(16)[None]
    win = np.array([[2, 4], [8, 16]])
    pt = np.zeros((P, 2, NCH, 16), np.float32)
    for t in range(2):
        for half in range(2):
            w = win[t, half]
            for ch in range(NCH):
                cnt = np.minimum(ch * TC + np.arange(16) + 1, w)
                pt[64 * half:64 * half + 64, t, ch] = 1.0 / cnt.astype(np.float32)
    c[:, C_PT:] = pt.reshape(P, -1)
    k = np.zeros((P, NMASK), np.float32)
    k[:, K_ID:K_ID + P] = np.eye(P)
    q, key = p, np.arange(P)[None]
    k[:, K_TRI + 384:K_TRI + 512] = np.where(key > q, NEG, 0.0)
    k[:, K_WIN:K_WIN + P] = np.where(key > q, 0.0, NEG)
    n = np.arange(256)[None] - P
    k[:, K_CMP:K_CMP + 256] = np.where(16 * n + 31 <= p, 0.0, NEG)
    inv = (1.0 / (np.float32(10000.0) ** (np.arange(0, HD, 2, dtype=np.float32) / np.float32(HD)))).astype(np.float32)
    ang = (np.arange(SEQ, dtype=np.float32)[None] * np.tile(inv, 4)[:, None]).astype(np.float32)
    cs = np.stack([np.cos(ang), np.sin(ang)]).astype(np.float32)
    cs = np.ascontiguousarray(cs.reshape(2, P, NCH, TC).transpose(2, 1, 0, 3).reshape(NCH, P, 2 * TC))
    iw = np.stack([np.where(np.arange(P) < 64, 1.0 / win[t, 0], 1.0 / win[t, 1]) for t in range(2)], 1)
    return c, k, cs, iw.astype(np.float32)


def attention_units():
    def rest(branch, i, k0, r, slot):
        g = 4 // r
        return [(branch, i, h, g, k0, r, slot, "tri") for h in range(0, NH, g)]

    def n_slc(i):
        return i // 4 + 1

    units = [("cmp", 0)]
    for i in range(NT):
        ns = n_slc(i)
        if i < WT:
            units += rest("win", i, 0, i + 1, ns + 1)
        else:
            units += [("win", i, h, 1, i - WT, WT, ns + 1, "win") for h in range(NH)]
            units += rest("win", i, i, 1, ns + 2)
        if i + 1 < NT:
            units.append(("cmp", i + 1))
        for c in range(ns - 1):
            units += [("slc", i, h, 1, 4 * c, 4, c + 1, None) for h in range(NH)]
        units += rest("slc", i, 4 * (ns - 1), i + 1 - 4 * (ns - 1), ns)
    return units


def hybrid_layer(nc, a, out):
    units = attention_units()
    last_of = {i: max(n for n, u in enumerate(units) if u[0] != "cmp" and u[1] == i) for i in range(NT)}
    LATE = 8
    cmp_at = {u[1]: n for n, u in enumerate(units) if u[0] == "cmp"}
    first_slc = {i: min(n for n, u in enumerate(units) if u[0] == "slc" and u[1] == i) for i in range(NT)}
    n_slc = {i: i // 4 + 1 for i in range(NT)}
    n_win = {i: 1 if i < WT else 2 for i in range(NT)}

    x1_dram = nc.dram_tensor("x1_rows", (SEQ, D), F32).ap()
    y_dram = nc.dram_tensor("expert_rows", (NB * P, D), F32).ap()
    slot_dram = nc.dram_tensor("slot_token", ((NB + 1) * P, 1), I32).ap()

    with ExitStack() as ctx:
        sem_ = {}

        def sem(name):
            sem_[name] = ctx.enter_context(nc.semaphore(name))
            return sem_[name]

        ARENA = 55760
        ARENA_AT = -(-nc.sbuf_base // 32) * 32
        ctx.enter_context(nc.sbuf_tensor("arena", [P, ARENA], F32))
        top, carved = [0], []

        def carve(*shape, at=None, dtype=F32):
            n = int(np.prod(shape))
            if at is None:
                at = top[0]
                top[0] += -(-n // 8) * 8
            assert at + n <= ARENA, (at, n)
            v = nc.alloc_sbuf_tensor_at(f"at{at}_{len(carved)}", [P, n], dtype, offset=ARENA_AT + 4 * at)[:, :]
            carved.append(at)
            if len(shape) == 2:
                v = v.rearrange("p (a b) -> p a b", a=shape[0])
            if len(shape) == 3:
                v = v.rearrange("p (a b c) -> p a b c", a=shape[0], b=shape[1])
            return v

        def carve_parts(*shape, at=None):
            return carve(*shape, at=at, dtype=F32R)

        consts = carve(NCONST)
        chan = carve(NCHAN)
        masks = ctx.enter_context(nc.sbuf_tensor("masks", [P, NMASK], BF16))
        gates = carve(NT, 12)
        dest_w = carve(2, NT)
        dest_i = ctx.enter_context(nc.sbuf_tensor("dest_i", [P, 2, NT], I32))
        tok_i = ctx.enter_context(nc.sbuf_tensor("tok_i", [P, NT], I32))
        tables = ctx.enter_context(nc.sbuf_tensor("tables", [1, 3, 64], I32))
        PERSIST = top[0]
        WE = KD * DE * 2 + 4 * D
        yT = carve(KD, SEQ)
        QS = carve_parts(NH, SEQ)
        QR = carve(2, SEQ)
        AT_K = top[0]
        KS, KW = carve(SEQ), carve(SEQ)
        KSL, KWL = (carve_parts(SEQ, at=AT_K + n * SEQ) for n in range(2))
        VS = carve(NT, 65)
        VW = carve(NT, 65)
        TEMP = top[0]
        KC2 = yT[:, 6, :]
        VC2 = yT[:, 7, :]
        zeros = carve(TC, at=PERSIST + KD * SEQ + NH * SEQ - TC)
        xT = [carve(KD, TC) for _ in range(2)]
        wt = [carve(KD, P) for _ in range(2)]
        w_tm = carve(KD, NTM)
        cs = carve(2, TC)
        stage = [carve(TC) for _ in range(4)]
        cpad = [carve(HC + TC) for _ in range(2)]
        bpad = [carve(HB + TC) for _ in range(2)]
        apad = [carve(HA + TC) for _ in range(2)]
        s_a, s_b = carve(HC + TC), carve(HC + TC)
        pd = [yT[:, 7, n * TC:(n + 1) * TC] for n in range(2)]
        pool_w = carve(2, P)
        t1, t2 = (yT[:, 7, n * TC:(n + 1) * TC] for n in (2, 3))
        sd = s_a[:, 0:TC]
        t2r = t2.bitcast(F32R)
        top[0] = TEMP
        w1 = [carve(16, CHID), carve(16, CHID, at=ARENA - 16 * CHID)]
        KSH, KWH = (carve_parts(SEQ, at=TEMP + n * SEQ) for n in range(2))
        w2 = carve(2, 2, P)
        pe2 = carve(2, 16)
        hT = [carve(2, P) for _ in range(2)]
        hbias = carve(4)
        kct = carve(2, P)
        vct = carve(HD + 1)
        prob = [carve(TC) for _ in range(4)]
        probT = [carve(TC) for _ in range(3)]
        pn = [carve(NH, P) for _ in range(2)]
        OB = [carve(NH, 7, 65) for _ in range(2)]
        nmx = [carve(NH, 8) for _ in range(2)]
        small = carve(16, 32)
        psm = carve(132)
        imp = [carve(NSEL) for _ in range(2)]
        yrow = [carve(GW) for _ in range(2)]
        qmask = carve(P)[0:NSEL, :].bitcast(BF16).rearrange("p (a b) -> p a b", a=2)
        w_outb = carve(KD // 2, D, at=PERSIST + KD * SEQ)
        xrow = [carve(D, at=PERSIST + KD * SEQ + (4 + n) * D) for n in range(2)]
        rrow = [carve(D, at=PERSIST + KD * SEQ + (6 + n) * D) for n in range(2)]
        w_outa = carve(KD // 2, D, at=ARENA - KD // 2 * D)
        top[0] = PERSIST + 2 * WE
        x1s = carve(NT, D)
        AFTER_X1 = top[0]
        x1T = [carve(KD, P) for _ in range(2)]
        ln_g, ln_b = carve(D), carve(D)
        rw = carve(KD, NE)
        bst = [carve(16) for _ in range(2)]
        lgt = carve(NT, NE)
        aff = carve(NT, NE)
        assert top[0] <= ARENA - KD // 2 * D
        top[0] = PERSIST
        rt = [carve(NT, NE) for _ in range(14)]
        r4 = [carve(NT, 4) for _ in range(8)]
        r1 = [carve(NT) for _ in range(8)]
        cnt16 = carve(4, NE)
        cmp256 = carve(NE, NE)
        tb = [carve(64, NE) for _ in range(3)]
        tb1 = [carve(64) for _ in range(3)]
        rbias = carve(NE)
        zero_i = ctx.enter_context(nc.sbuf_tensor("zero_i", [P, NB + 1], I32))
        top[0] = PERSIST
        wx = carve(2, WE)
        top[0] = AFTER_X1
        xg = [carve(D) for _ in range(2)]
        xgT = [carve(KD, P) for _ in range(2)]
        hrow = [carve(DE) for _ in range(2)]
        hTm = [carve(4, P) for _ in range(2)]
        yrw = [carve(D) for _ in range(2)]
        idx = [ctx.enter_context(nc.sbuf_tensor(f"idx{u}", [P, 1], I32)) for u in range(2)]
        ln2_g, ln2_b = carve(D), carve(D)
        top[0] = PERSIST
        ya = [carve(D) for _ in range(R6)]
        yb = [carve(D) for _ in range(R6)]
        fin = [carve(D) for _ in range(R6)]
        b6 = [carve(16) for _ in range(R6)]

        share = lambda i: small[:, 12:16, 8 * (i % 2):8 * (i % 2) + 1 + n_slc[i] + n_win[i]]
        bank = [ctx.enter_context(nc.psum_tensor(f"bank{n}", [P, 512], F32)) for n in range(8)]
        C = lambda at, n: consts[:, at:at + n]
        ident = C(C_ID, P)

        for n in ("const_in", "chan_in", "mask_ready", "tm_in", "w_in", "cs_in", "tile_made", "tile_out",
                  "zeroed", "stage_free", "cpad_free", "rope_made", "sp_made", "free6", "free7", "conv_made",
                  "pool_d", "cent", "squared", "std", "zed", "dve_step", "w_in0", "w_in1", "x_in0", "x_in1",
                  "xr_in0", "xr_in1", "g_in0", "g_in1", "ysto0", "ysto1", "idx0", "idx1", "ya_in0", "ya_in1",
                  "ya_in2", "ya_in3", "out60", "out61", "out62", "out63", "w6", "r6", "c6", "p6", "mk_in",
                  "yb_done", "cw_in", "k_high", "k_low", "shifted", "ch_made", "ch_out", "cc_made", "cc_out",
                  "s_made", "max_made", "prob_made", "t_made", "pt_made", "o_made", "o_out", "al_made",
                  "po_step", "mk_made", "mkT_made", "mask_rows", "d_made", "f_made", "y_made", "yT_made",
                  "yT_out", "cd_step", "wo_in", "ln_in", "mix_made", "mix_used", "sq_in", "sq_out",
                  "norm_made", "x1_made", "x1_stored", "xt_made", "xt_out", "lg_made", "lg_out", "route_in",
                  "aff_made", "oh_made", "cum_made", "dest_made", "zero_made", "rows_zero", "slot_zero",
                  "slot_stored", "tab_made", "we_in", "idx_in", "gx_made", "gx_out", "gu_made", "act_made",
                  "h_made", "ht_made", "ht_out", "dn_outa", "dn_outd", "blk_done", "l2_in", "s6_in", "s6_out",
                  "n6", "fin6", "stats6"):
            sem(n)
        S = sem_

        block = ctx.enter_context(nc.Block())

        @block.sync
        def _(sp):
            sp.dma_start(consts, a["consts"]).then_inc(S["const_in"], 16)
            sp.dma_start(yT[:, 6, 0:NMASK], a["masks"]).then_inc(S["mk_in"], 16)
            sp.dma_start(chan, a["chan"]).then_inc(S["chan_in"], 16)
            sp.dma_start(pool_w[:, :, :], a["pool_w"]).then_inc(S["chan_in"], 16)
            sp.dma_start(w_tm[:, :, :], a["w_tm"]).then_inc(S["tm_in"], 16)
            with sp.Fori(0, NCH // 2) as cc:
                for u in range(2):
                    c = cc * 2 + u
                    sp.wait_ge(S["tile_made"], MJ * c + 1)
                    sp.dma_start(xT[u][:, :, :], a["xT"][bass.ds(c, 1), :, :].rearrange("a p n -> (a p) n")
                                 ).then_inc(S[f"x_in{u}"], 16)
                    sp.wait_ge(S["rope_made"], 3 * c + 1)
                    sp.dma_start(cs[:, :, :], a["cs"][bass.ds(c, 1), :, :].rearrange("a p n -> (a p) n")
                                 ).then_inc(S["cs_in"], 16)
                    for m in range(NM):
                        before = MJ * c + m - 1 if m >= 2 else MJ * c + m - 3
                        sp.wait_ge(S["tile_made"], before + MJ + 1)
                        sp.dma_start(wt[m % 2][:, :, :], a["w_in"][m]).then_inc(S[f"w_in{m % 2}"], 16)
            sp.wait_ge(S["tile_made"], MJ * NCH + MJ + 1)
            sp.wait_ge(S["yb_done"], 2 * NCH)
            for n in range(2):
                sp.dma_start(w1[n][:, :, :], a["cmp_w1"][n]).then_inc(S["cw_in"], 16)
            sp.dma_start(w2[:, :, :, :], a["cmp_w2"]).then_inc(S["cw_in"], 16)
            sp.dma_start(pe2[:, :, :], a["cmp_pe"]).then_inc(S["cw_in"], 16)
            sp.wait_ge(S["ch_made"], 4)
            sp.dma_start(w_outa[:, :, :], a["w_out"][0]).then_inc(S["wo_in"], 16)
            sp.wait_ge(S["s_made"], len(units))
            sp.dma_start(w_outb[:, :, :], a["w_out"][1]).then_inc(S["wo_in"], 16)
            sp.wait_ge(S["yT_out"], NT)
            sp.dma_start(ln_g, a["ln1_g"][None, :].to_broadcast((P, D))).then_inc(S["ln_in"], 16)
            sp.dma_start(ln_b, a["ln1_b"][None, :].to_broadcast((P, D))).then_inc(S["ln_in"], 16)
            sp.dma_start(rw[:, :, :], a["router_w"]).then_inc(S["ln_in"], 16)
            for t in range(NT):
                if t >= 2:
                    sp.wait_ge(S["mix_used"], 2 * (t - 1))
                sp.dma_start(xrow[t % 2], a["x"][t * P:(t + 1) * P, :]).then_inc(S[f"xr_in{t % 2}"], 16)
            sp.wait_ge(S["zero_made"], 1)
            sp.dma_start(slot_dram.rearrange("(p n) o -> p (n o)", p=P), zero_i[:, :]).then_inc(S["slot_zero"], 16)
            sp.wait_ge(S["mix_made"], NT)
            sp.dma_start(rbias, a["router_bias"][None, :].to_broadcast((P, NE))).then_inc(S["route_in"], 16)
            sp.wait_ge(S["norm_made"], NT)
            for n in range(3):
                sp.dma_start(wx[:, 1, n * KD * DE:(n + 1) * KD * DE], a["w_exp"][0, n]).then_inc(S["we_in"], 16)
            sp.wait_ge(S["tab_made"], 1)
            sp.dma_start(ln2_g, a["ln2_g"][None, :].to_broadcast((P, D))).then_inc(S["l2_in"], 16)
            sp.dma_start(ln2_b, a["ln2_b"][None, :].to_broadcast((P, D))).then_inc(S["l2_in"], 16)
            for e in range(1, NE):
                sp.wait_ge(S["we_in"], 48 * e)
                if e >= 2:
                    done = sp.value_load(tables[0:1, 1, e - 2:e - 1], min_val=0, max_val=NB)
                    sp.wait_ge(S["blk_done"], done + 1)
                for n in range(3):
                    sp.dma_start(wx[:, 1 - e % 2, n * KD * DE:(n + 1) * KD * DE], a["w_exp"][e, n]
                                 ).then_inc(S["we_in"], 16)
            for u in range(R6):
                sp.sem_inc(S[f"out6{u}"], 16)
            with sp.Fori(0, NT // R6) as tt:
                for u in range(R6):
                    t = tt * R6 + u
                    sp.wait_ge(S["p6"], t + 1)
                    sp.dma_start(out[bass.ds(t * P, P), :], fin[u]).then_inc(S[f"out6{u}"], 16)
            for u in range(R6):
                sp.wait_ge(S[f"out6{u}"], 16 * (NT // R6) + 16)

        @block.tensor
        def _(pe):
            pe.sem_inc(S["tile_made"], MJ + 1)
            pe.wait_ge(S["const_in"], 16)
            pe.wait_ge(S["chan_in"], 32)
            pe.wait_ge(S["tm_in"], 16)

            def special(b, free, value, out_, lhs_rhs):
                pe.wait_ge(S[free], value)
                for n, (l, r) in enumerate(lhs_rhs):
                    mm = pe.matmul(out_, l, r, start=(n == 0), stop=(n == len(lhs_rhs) - 1))
                mm.then_inc(S["sp_made"], 1)

            with pe.Fori(0, NCH // 2) as cc:
                for u in range(2):
                    c = cc * 2 + u
                    cols = bass.ds(c * TC, TC)
                    for j in range(MJ):
                        if j == 0:
                            pe.wait_ge(S[f"x_in{u}"], 16 * cc + 16)
                        pe.wait_ge(S["tile_out"], MJ * c + j + 1)
                        ps = bank[j % NBANK]
                        if j < NM:
                            pe.wait_ge(S[f"w_in{j % 2}"], 8 * NM * c + 16 * (j // 2) + 16)
                            for k in range(KD):
                                mm = pe.matmul(ps[:], wt[j % 2][:, k, :], xT[u][:, k, :],
                                               start=(k == 0), stop=(k == KD - 1))
                        else:
                            for s in range(2):
                                tok = (j - NM) * 2 + s
                                for k in range(KD):
                                    mm = pe.matmul(ps[:, s * NTM:(s + 1) * NTM], xT[u][:, k, tok * P:(tok + 1) * P],
                                                   w_tm[:, k, :], start=(k == 0), stop=(k == KD - 1))
                        mm.then_inc(S["tile_made"], 1)
                        if j == M_C0:
                            pe.wait_ge(S["tile_out"], MJ * c + NBANK + M_KS + 1)
                            special(6, "free6", 4 * c + 1, bank[6][:], [(C(C_PERM, P), stage[0])])
                        if j == M_C1:
                            pe.wait_ge(S["tile_out"], MJ * c + NBANK + M_Q0 + 1)
                            special(7, "free7", 3 * c + 1, bank[7][:], [(C(C_PERM, P), QR[:, 0, cols])])
                        if j == M_AC0:
                            pe.wait_ge(S["tile_out"], MJ * c + NBANK + M_Q1 + 1)
                            special(6, "free6", 4 * c + 2, bank[6][:], [(C(C_PERM, P), QR[:, 1, cols])])
                        if j == M_AH0:
                            pe.wait_ge(S["conv_made"], 2 * c + 2)
                            special(7, "free7", 3 * c + 2, bank[7][:],
                                    [(C(C_MEAN, P), yT[:, 2 + n, cols]) for n in range(2)])
                        if j == M_AB0:
                            for n in range(2):
                                pe.wait_ge(S["pool_d"], 2 * c + n + 1)
                                special(6 + n, f"free{6 + n}", (4 if n == 0 else 3) * c + 3, bank[6 + n][:],
                                        [(pool_w[:, n, :], pd[n])])
                        if j == M_AH1:
                            pe.wait_ge(S["squared"], 2 * c + 2)
                            special(6, "free6", 4 * c + 4, bank[6][:], [(C(C_MEAN, P), t) for t in (t1, t2)])

            pe.wait_ge(S["cw_in"], 64)
            pe.wait_ge(S["shifted"], 2)
            pe.wait_ge(S["tile_out"], MJ * NCH + NBANK)
            pe.wait_ge(S["free6"], 4 * NCH + 1)
            pe.wait_ge(S["free7"], 3 * NCH + 1)
            for n, src in enumerate((KC2, VC2)):
                for m in range(2):
                    ps = bank[2 * n + m]
                    for s in range(16):
                        pe.matmul(ps[:, 0:NCMP], w1[n][:, s, m * P:(m + 1) * P],
                                  src[:, 2 * s:2 * s + 16 * (NCMP - 1) + 1:16], start=(s == 0), stop=(s == 15))
                    for s in range(16):
                        mm = pe.matmul(bank[4 + 2 * n + m][:, 0:1], w1[n][:, s, m * P:(m + 1) * P],
                                       pe2[:, n, s:s + 1], start=(s == 0), stop=(s == 15))
                    mm.then_inc(S["ch_made"], 1)
            pe.wait_ge(S["ch_out"], 4)
            for m in range(2):
                mm = pe.matmul(bank[0][:, 0:NCMP], w2[:, 0, m, :], hT[0][:, m, 0:NCMP], start=(m == 0), stop=(m == 1))
            mm.then_inc(S["cc_made"], 1)
            for m in range(2):
                mm = pe.matmul(bank[1][0:NCMP, 0:HD], hT[1][:, m, 0:NCMP], w2[:, 1, m, 0:HD],
                               start=(m == 0), stop=(m == 1))
            mm.then_inc(S["cc_made"], 1)
            pe.wait_ge(S["cc_out"], 6)
            pe.wait_ge(S["k_low"], 2)
            pe.wait_ge(S["mask_ready"], 1)

            def scores(n):
                un = units[n]
                ps = bank[n % 3]
                if n >= 3:
                    pe.wait_ge(S["prob_made"], n - 2)
                if un[0] == "cmp":
                    i = un[1]
                    pe.matmul(ps[:].rearrange("p (h n) -> p h n", h=NH)[:, :, 0:NCMP], masks[:, K_ID:K_ID + P],
                              masks[:, None, K_CMP + P - 8 * i:K_CMP + P - 8 * i + NCMP].to_broadcast((P, NH, NCMP)),
                              start=True, stop=True)
                    for m in range(2):
                        mm = pe.matmul(ps[:, 2 * m * P:2 * (m + 1) * P].rearrange("p (h n) -> p h n", h=2)[:, :, 0:NCMP],
                                       QR[:, m, i * P:(i + 1) * P], kct[:, :, 0:NCMP],
                                       start=False, stop=True, skip_group_check=True)
                    mm.then_inc(S["s_made"], 1)
                    return
                br, i, h0, g, k0, t, slot, mask = un
                n_ = t * P
                if br == "slc" and i >= 8 and n == first_slc[i]:
                    pe.wait_ge(S["mask_rows"], i - 7)
                high, low = (KSH, KSL) if br == "slc" else (KWH, KWL)
                chosen = br == "slc" and i >= 8
                if mask:
                    m = masks[:, K_TRI + 512 - n_:K_TRI + 512] if mask == "tri" else masks[:, K_WIN:K_WIN + n_]
                    pe.matmul(ps[:, 0:g * n_].rearrange("p (g n) -> p g n", g=g), masks[:, K_ID:K_ID + P],
                              m[:, None, :].to_broadcast((P, g, n_)), start=True, stop=True)
                if chosen:
                    blocks = masks[0:NSEL, K_ID + 2 * k0:K_ID + 2 * (k0 + t)]
                    for q in range(g):
                        pe.matmul(ps[:, q * n_:(q + 1) * n_].rearrange("p (b k) -> p b k", k=64), qmask[:, i % 2, :],
                                  blocks[:, :, None].to_broadcast((NSEL, 2 * t, 64)), start=(not mask), stop=True,
                                  skip_group_check=bool(mask))
                for q in range(g):
                    for keys in (high, low):
                        mm = pe.matmul(ps[:, q * n_:(q + 1) * n_], QS[:, h0 + q, i * P:(i + 1) * P],
                                       keys[:, k0 * P:k0 * P + n_],
                                       start=(keys is high and not mask and not chosen), stop=True,
                                       skip_group_check=True)
                mm.then_inc(S["s_made"], 1)

            def turn(n):
                un = units[n]
                pe.wait_ge(S["prob_made"], n + 1)
                if n >= 2:
                    pe.wait_ge(S["pt_made"], n - 1)
                ps = bank[3 + n % 2]
                if un[0] == "cmp":
                    for h in range(NH):
                        mm = pe.transpose(ps[0:NCMP, h * P:(h + 1) * P], pn[un[1] % 2][:, h, 0:NCMP], ident)
                else:
                    for k in range(un[3] * un[5]):
                        mm = pe.transpose(ps[:, k * P:(k + 1) * P], prob[n % 4][:, k * P:(k + 1) * P], ident)
                mm.then_inc(S["t_made"], 1)

            def values(n):
                un = units[n]
                pe.wait_ge(S["pt_made"], n + 1)
                if n >= 2:
                    pe.wait_ge(S["o_out"], n - 1)
                ps = bank[5 + n % 2]
                pt = probT[n % 3]
                if un[0] == "cmp":
                    for h in range(NH):
                        mm = pe.matmul(ps[:, h * 65:(h + 1) * 65], pt[0:NCMP, h * P:(h + 1) * P], vct[0:NCMP, :],
                                       start=True, stop=True)
                else:
                    br, i, h0, g, k0, t, slot, mask = un
                    v = VS if br == "slc" else VW
                    for q in range(g):
                        for k in range(t):
                            mm = pe.matmul(ps[:, q * 65:(q + 1) * 65], pt[:, (q * t + k) * P:(q * t + k + 1) * P],
                                           v[:, k0 + k, :], start=(k == 0), stop=(k == t - 1))
                mm.then_inc(S["o_made"], 1)

            rows, turned = [0], [0]

            def turn_mask(i):
                pe.wait_ge(S["mk_made"], i - 7)
                pe.wait_ge(S["yT_out"], rows[0])
                pe.transpose(bank[7][0:NSEL, 0:P], imp[0], ident).then_inc(S["mkT_made"], 1)
                turned[0] += 1

            def turn_rows(i):
                pe.wait_ge(S["y_made"], i + 1)
                if turned[0]:
                    pe.wait_ge(S["mask_rows"], turned[0])
                if i:
                    pe.wait_ge(S["yT_out"], i)
                rows[0] += 1
                for m in range(2):
                    mm = pe.transpose(bank[7][:, 256 + m * P:256 + (m + 1) * P], yrow[i % 2][:, m * P:(m + 1) * P], ident)
                mm.then_inc(S["yT_made"], 1)

            N = len(units)
            for n in range(-2, N + LATE):
                for i in range(NT):
                    if i >= 8 and n + 2 == first_slc[i]:
                        turn_mask(i)
                    if n - LATE == last_of[i]:
                        turn_rows(i)
                if 0 <= n + 2 < N:
                    scores(n + 2)
                if 0 <= n < N:
                    turn(n)
                if 0 <= n - 1 < N:
                    values(n - 1)

            pe.wait_ge(S["wo_in"], 32)
            pe.wait_ge(S["ln_in"], 48)
            pe.wait_ge(S["yT_out"], NT)

            def mix(t):
                if t >= 2:
                    pe.wait_ge(S["mix_used"], 2 * (t - 1))
                for m in range(2):
                    for k in range(KD):
                        mm = pe.matmul(bank[2 * (t % 2) + m][:], yT[:, k, t * P:(t + 1) * P],
                                       (w_outa, w_outb)[k // 4][:, k % 4, m * 512:(m + 1) * 512], start=(k == 0), stop=(k == KD - 1))
                mm.then_inc(S["mix_made"], 1)

            def turn_x1(t):
                pe.wait_ge(S["x1_made"], t + 1)
                if t >= 1:
                    pe.wait_ge(S["xt_out"], 2 * t)
                for k in range(KD):
                    mm = pe.transpose(bank[4 + k // 4][:, (k % 4) * P:(k % 4 + 1) * P], x1s[:, t, k * P:(k + 1) * P], ident)
                mm.then_inc(S["xt_made"], 1)

            def logits(t):
                pe.wait_ge(S["xt_out"], 2 * (t + 1))
                if t >= 1:
                    pe.wait_ge(S["lg_out"], t)
                for k in range(KD):
                    mm = pe.matmul(bank[6][:, 0:NE], x1T[t % 2][:, k, :], rw[:, k, :], start=(k == 0), stop=(k == KD - 1))
                mm.then_inc(S["lg_made"], 1)

            for t in range(NT + 2):
                if t < NT:
                    mix(t)
                if 1 <= t <= NT:
                    turn_x1(t - 1)
                if t >= 2:
                    logits(t - 2)

            pe.wait_ge(S["oh_made"], 1)
            oh = rt[0][:, :, :].rearrange("p a b -> p (a b)")
            pe.matmul(bank[0][:, 0:256], C(C_TRIU, P), oh, start=True, stop=True)
            pe.matmul(bank[1][:, 0:256], C(C_ONE, P), oh, start=True, stop=True).then_inc(S["cum_made"], 1)

            pe.wait_ge(S["tab_made"], 1)

            def turn_in(b, u, half_b=0):
                pe.wait_ge(S[f"g_in{u}"], 16 * (b // 2 if isinstance(b, int) else half_b) + 16)
                pe.wait_ge(S["gx_out"], 2 * b + 1)
                for k in range(KD):
                    mm = pe.transpose(bank[k // 4][:, (k % 4) * P:(k % 4 + 1) * P], xg[u][:, k * P:(k + 1) * P], ident)
                mm.then_inc(S["gx_made"], 1)

            pe.sem_inc(S["blk_done"], 1)
            pe.sem_inc(S["ht_made"], 2)
            turn_in(0, 0)
            pairs = pe.value_load(tables[0:1, 1, NE:NE + 1], min_val=1, max_val=NB // 2)
            with pe.Fori(0, NB // 2) as bb, pe.If(bb < pairs):
                for u in range(2):
                    b = bb * 2 + u
                    e = pe.value_load(tables[0:1, 0, bass.ds(b, 1)], min_val=0, max_val=NE - 1)
                    half = pe.value_load(tables[0:1, 2, bass.ds(b, 1)], min_val=0, max_val=1)
                    pe.wait_ge(S["we_in"], e * 48 + 48)
                    pe.wait_ge(S["gx_out"], 2 * b + 3)
                    pe.wait_ge(S["h_made"], b + 1)
                    for m in range(2):
                        for k in range(KD):
                            at = m * KD * DE + k * DE
                            mm = pe.matmul(bank[2 + m][:], xgT[u][:, k, :],
                                           wx[:, bass.ds(half, 1), at:at + DE].rearrange("p a n -> p (a n)"),
                                           start=(k == 0), stop=(k == KD - 1))
                    mm.then_inc(S["gu_made"], 1)
                    nxt = b + 1
                    turn_in(nxt, 1 - u, bb + u)
                    pe.wait_ge(S["h_made"], b + 2)
                    pe.wait_ge(S["ht_out"], b + 1)
                    for k in range(4):
                        mm = pe.transpose(bank[4][:, k * P:(k + 1) * P], hrow[u][:, k * P:(k + 1) * P], ident)
                    mm.then_inc(S["ht_made"], 1)
                    pe.wait_ge(S["ht_out"], b + 2)
                    pe.wait_ge(S["dn_outa"], b + 1)
                    pe.wait_ge(S["dn_outd"], b + 1)
                    for k in range(4):
                        for m in range(2):
                            at = 2 * KD * DE + k * D + m * 512
                            mm = pe.matmul(bank[5 + m][:], hTm[u][:, k, :],
                                           wx[:, bass.ds(half, 1), at:at + 512].rearrange("p a n -> p (a n)"),
                                           start=(k == 0), stop=(k == 3))
                    mm.then_inc(S["blk_done"], 1)

        @block.scalar
        def _(act):
            act.sem_inc(S["tile_out"], NBANK)
            act.wait_ge(S["chan_in"], 32)
            act.wait_ge(S["zeroed"], 1)

            def apart():
                act.wait_ge(S["zeroed"], 1)

            with act.Fori(0, NCH // 2) as cc:
                for u in range(2):
                    c = cc * 2 + u
                    cols = bass.ds(c * TC, TC)
                    slot = {M_BG0: (0, 6), M_BV0: (1, 6), M_BG1: (2, 7), M_BV1: (3, 5), M_KS: (0, 8),
                            M_AC0: (1, 8), M_AH0: (2, 9), M_AB0: (3, 9), M_AC1: (0, 10), M_AH1: (1, 11), M_AB1: (2, 11)}

                    def copy_out(j):
                        ps = bank[j % NBANK]
                        if j not in slot:
                            apart()
                        act.wait_ge(S["tile_made"], MJ * c + MJ + 1 + j + 1)
                        if j in slot:
                            s, v = slot[j]
                            act.wait_ge(S["stage_free"], 7 * c + v)
                            f = ACT.Sigmoid if j in (M_BG0, M_BG1) else ACT.Copy
                            act.activation(stage[s], ps[:], f).then_inc(S["tile_out"], 1)
                        elif j == M_KC:
                            act.activation(KC2[:, cols], ps[:], ACT.Copy).then_inc(S["tile_out"], 1)
                        elif j in (M_Q0, M_Q1):
                            act.activation(QR[:, j - M_Q0, cols], ps[:], ACT.Copy, scale=0.125
                                           ).then_inc(S["tile_out"], 1)
                        elif j in (M_C0, M_C1):
                            n = j - M_C0
                            act.wait_ge(S["cpad_free"], 2 * c + n + 1)
                            act.activation(cpad[n][:, HC:HC + TC], ps[:], ACT.Copy).then_inc(S["tile_out"], 1)
                        else:
                            v = ps[:, 0:2 * NTM].rearrange("p (s n) -> p s n", s=2)
                            t0 = c * 4 + (j - NM) * 2
                            act.activation(VS[:, bass.ds(t0, 2), 0:64], v[:, :, 0:64], ACT.Copy)
                            act.activation(VW[:, bass.ds(t0, 2), 0:64], v[:, :, 64:128], ACT.Copy)
                            act.activation(gates[:, bass.ds(t0, 2), :], v[:, :, 128:140], ACT.Sigmoid
                                           ).then_inc(S["tile_out"], 1)

                    for j in range(M_AB0 + 1):
                        copy_out(j)
                    for n, t in enumerate((t1, t2)):
                        apart()
                        act.wait_ge(S["cent"], 2 * c + n + 1)
                        act.activation(t, yT[:, 2 + n, cols], ACT.Square).then_inc(S["squared"], 1)
                    for n in range(2):
                        apart()
                        act.wait_ge(S["sp_made"], 7 * c + 5 + n)
                        act.activation(yT[:, 4 + n, cols], bank[6 + n][:], ACT.Copy,
                                       scale=chan[:, CH_PS + n:CH_PS + n + 1]).then_inc(S[f"free{6 + n}"], 1)
                    for j in (M_AC1, M_AH1, M_AB1):
                        copy_out(j)
                    act.wait_ge(S["sp_made"], 7 * c + 7)
                    act.activation(sd, bank[6][:], ACT.Sqrt, bias=chan[:, CH_EPS:CH_EPS + 1]).then_inc(S["std"], 1)
                    act.wait_ge(S["std"], c + 1)
                    act.sem_inc(S["free6"], 1)
                    copy_out(NM)
                    copy_out(NM + 1)
                    for n in range(2):
                        apart()
                        act.wait_ge(S["zed"], 2 * c + n + 1)
                        act.activation(yT[:, 2 + n, cols], yT[:, 2 + n, cols], ACT.Silu,
                                       scale=chan[:, CH_G + n:CH_G + n + 1],
                                       bias=chan[:, CH_BE + n:CH_BE + n + 1]).then_inc(S["yb_done"], 1)
            for n in range(2):
                for m in range(2):
                    act.wait_ge(S["ch_made"], 2 * n + m + 1)
                    act.activation(hbias[:, 2 * n + m:2 * n + m + 1], bank[4 + 2 * n + m][:, 0:1], ACT.Copy
                                   ).then_inc(S["cd_step"], 1)
                    act.wait_ge(S["cd_step"], 2 * n + m + 1)
                    act.activation(hT[n][:, m, 0:NCMP], bank[2 * n + m][:, 0:NCMP], ACT.Silu,
                                   bias=hbias[:, 2 * n + m:2 * n + m + 1]).then_inc(S["ch_out"], 1)
            act.wait_ge(S["ch_made"], 2)
            for high, keys in ((KSH, KS), (KWH, KW)):
                act.activation(high, keys, ACT.Copy).then_inc(S["k_high"], 1)
            act.wait_ge(S["cc_made"], 2)
            for n in range(2):
                r = slice(64 * n, 64 * n + 64)
                act.activation(kct[r, n, 0:NCMP], bank[0][r, 0:NCMP], ACT.Copy).then_inc(S["cc_out"], 1)
            act.activation(vct[0:NCMP, 0:HD], bank[1][0:NCMP, 0:HD], ACT.Copy).then_inc(S["cc_out"], 1)

            def exps(n):
                un = units[n]
                act.wait_ge(S["max_made"], n + 1)
                if n >= 4:
                    act.wait_ge(S["t_made"], n - 3)
                if un[0] == "cmp":
                    i = un[1]
                    if i >= 2:
                        act.wait_ge(S["t_made"], cmp_at[i - 2] + 1)
                    if i >= 10:
                        act.wait_ge(S["mk_made"], i - 9)
                    for h in range(NH):
                        e = act.activation(pn[i % 2][:, h, 0:NCMP], bank[n % 3][:, h * P:h * P + NCMP], ACT.Exp,
                                           bias=nmx[i % 2][:, h, 0:1])
                else:
                    br, i, h0, g, k0, t, slot, mask = un
                    for q in range(g):
                        r = slice(q * t * P, (q + 1) * t * P)
                        e = act.activation(prob[n % 4][:, r], bank[n % 3][:, r], ACT.Exp,
                                           bias=nmx[i % 2][:, h0 + q, slot:slot + 1])
                e.then_inc(S["prob_made"], 1)

            def outs(n):
                un = units[n]
                act.wait_ge(S["o_made"], n + 1)
                ps = bank[5 + n % 2]
                if un[0] == "cmp":
                    i = un[1]
                    if i >= 2:
                        act.wait_ge(S["y_made"], i - 1)
                    act.activation(OB[i % 2][:, :, 0, :], ps[:, 0:NH * 65].rearrange("p (h n) -> p h n", h=NH), ACT.Copy
                                   ).then_inc(S["o_out"], 1)
                else:
                    br, i, h0, g, k0, t, slot, mask = un
                    act.activation(OB[i % 2][:, h0:h0 + g, slot, :],
                                   ps[:, 0:g * 65].rearrange("p (h n) -> p h n", h=g), ACT.Copy).then_inc(S["o_out"], 1)

            N = len(units)
            for n in range(-1, N + LATE):
                for i in range(NT):
                    if n - 2 == last_of[i]:
                        act.wait_ge(S["d_made"], i + 1)
                        ns = n_slc[i] + n_win[i]
                        v = small[:, 0:4, 8:8 + ns]
                        act.activation(v, v, ACT.Exp).then_inc(S["f_made"], 1)
                for i in range(NT):
                    if n - LATE == last_of[i]:
                        act.wait_ge(S["yT_made"], i + 1)
                        act.activation(yT[:, 6:8, i * P:(i + 1) * P],
                                       bank[7][:, 256:512].rearrange("p (m n) -> p m n", m=2), ACT.Copy
                                       ).then_inc(S["yT_out"], 1)
                if 0 <= n + 1 < N:
                    exps(n + 1)
                if 0 <= n - 1 < N:
                    outs(n - 1)
            for t in range(NT + 1):
                if t < NT:
                    act.wait_ge(S["sq_in"], t + 1)
                    act.activation(bst[t % 2][:, 14:15], bst[t % 2][:, 13:14], ACT.Sqrt,
                                   bias=chan[:, CH_EPS:CH_EPS + 1]).then_inc(S["sq_out"], 1)
                if t >= 1:
                    q = t - 1
                    act.wait_ge(S["xt_made"], q + 1)
                    if q >= 2:
                        act.wait_ge(S["lg_made"], q - 1)
                    for m in range(2):
                        act.activation(x1T[q % 2][:, 4 * m:4 * m + 4, :].rearrange("p a b -> p (a b)"), bank[4 + m][:],
                                       ACT.Copy).then_inc(S["xt_out"], 1)
                if t >= 2:
                    q = t - 2
                    act.wait_ge(S["lg_made"], q + 1)
                    act.activation(lgt[:, q, :], bank[6][:, 0:NE], ACT.Copy).then_inc(S["lg_out"], 1)
            act.wait_ge(S["lg_made"], NT)
            act.activation(lgt[:, NT - 1, :], bank[6][:, 0:NE], ACT.Copy).then_inc(S["lg_out"], 1)
            act.wait_ge(S["lg_out"], NT)
            act.activation(aff[:, :, :], lgt[:, :, :], ACT.Sigmoid).then_inc(S["aff_made"], 1)
            act.wait_ge(S["rows_zero"], 32 * (NB - NBMIN))
            act.sem_inc(S["gx_out"], 1)
            act.sem_inc(S["dn_outa"], 1)
            act.sem_inc(S["ysto0"], 16)
            act.sem_inc(S["ysto1"], 16)
            act.wait_ge(S["tab_made"], 1)

            def copy_in(b, u):
                act.wait_ge(S["gx_made"], b + 1)
                for m in range(2):
                    act.activation(xgT[u][:, 4 * m:4 * m + 4, :].rearrange("p a b -> p (a b)"), bank[m][:],
                                   ACT.Copy).then_inc(S["gx_out"], 1)

            copy_in(0, 0)
            pairs = act.value_load(tables[0:1, 1, NE:NE + 1], min_val=1, max_val=NB // 2)
            with act.Fori(0, NB // 2) as bb, act.If(bb < pairs):
                for u in range(2):
                    b = bb * 2 + u
                    act.wait_ge(S["gu_made"], b + 1)
                    act.wait_ge(S["ht_made"], b + 1)
                    act.activation(hrow[u], bank[2][:], ACT.Silu).then_inc(S["act_made"], 1)
                    copy_in(b + 1, 1 - u)
                    act.wait_ge(S["blk_done"], b + 2)
                    act.wait_ge(S[f"ysto{u}"], 16 * bb + 16)
                    act.activation(yrw[u][:, 0:512], bank[5][:], ACT.Copy).then_inc(S["dn_outa"], 1)
                    act.wait_ge(S["dn_outa"], b + 2)
                    act.wait_ge(S["dn_outd"], b + 2)
                    act.dma_start(y_dram[bass.ds(b * P, P), :], yrw[u]).then_inc(S[f"ysto{u}"], 16)
            with act.Fori(0, NT // R6) as tt:
                for u in range(R6):
                    t = tt * R6 + u
                    apart()
                    act.wait_ge(S[f"ya_in{u}"], 32 * tt + 32)
                    act.activation(ya[u], ya[u], ACT.Copy, scale=dest_w[:, 0, bass.ds(t, 1)]).then_inc(S["w6"], 1)
                    act.wait_ge(S["s6_in"], t + 1)
                    act.activation(b6[u][:, 14:15], b6[u][:, 13:14], ACT.Sqrt,
                                   bias=chan[:, CH_EPS:CH_EPS + 1]).then_inc(S["s6_out"], 1)

        @block.vector
        def _(ve):
            V_STEPS = [0]

            def step(ins):
                V_STEPS[0] += 1
                ins.then_inc(S["dve_step"], 1)
                return V_STEPS[0]

            ve.sem_inc(S["stage_free"], 7)
            ve.sem_inc(S["cpad_free"], 2)
            ve.sem_inc(S["rope_made"], 1)
            ve.sem_inc(S["free6"], 1)
            ve.sem_inc(S["free7"], 1)
            for t in bpad:
                ve.memset(t[:, 0:HB], 0.0)
            for t in cpad:
                ve.memset(t[:, 0:HC], 0.0)
            for t in apad:
                ve.memset(t[:, 0:HA], 0.0)
            ve.memset(VS[:, :, 64:65], 1.0)
            ve.memset(VW[:, :, 64:65], 1.0)
            ve.wait_ge(S["const_in"], 16)
            ve.wait_ge(S["chan_in"], 32)
            ve.wait_ge(S["mk_in"], 16)
            ve.tensor_copy(tok_i[:, :], C(C_TOK, NT))
            ve.tensor_copy(masks[:, :], yT[:, 6, 0:NMASK]).then_inc(S["zeroed"], 1)
            ve.wait_ge(S["zeroed"], 1)
            ve.sem_inc(S["mask_ready"], 1)
            w = lambda at: chan[:, at:at + 1]
            PER = 88
            with ve.Fori(0, NCH // 2) as cc:
                for u in range(2):
                    c = cc * 2 + u
                    cols = bass.ds(c * TC, TC)
                    V_STEPS[0] = 0

                    def need(n):
                        ve.wait_ge(S["dve_step"], PER * c + n)

                    at = [0, 0]
                    for n in range(2):
                        ve.wait_ge(S["tile_out"], MJ * c + NBANK + 2 * n + 2)
                        ve.tensor_tensor(bpad[n][:, HB:HB + TC], stage[2 * n], stage[2 * n + 1], ALU.mult
                                         ).then_inc(S["stage_free"], 1)
                    for k in range(CK):
                        for n in range(2):
                            acc = yT[:, 2 + n, cols]
                            if k == 0:
                                ve.wait_ge(S["stage_free"], 7 * c + 8 + n)
                                ins = ve.tensor_scalar(acc, bpad[n][:, 0:TC], w(CH_B + n * CK), w(CH_BB + n),
                                                       ALU.mult, ALU.add)
                            else:
                                need(at[n])
                                ins = ve.scalar_tensor_tensor(acc, bpad[n][:, k:k + TC], w(CH_B + n * CK + k), acc,
                                                              ALU.mult, ALU.add)
                            if k < CK - 1:
                                at[n] = step(ins)
                            else:
                                ins.then_inc(S["conv_made"], 1)
                    for n in range(2):
                        step(ve.tensor_copy(bpad[n][:, 0:HB], bpad[n][:, TC:TC + HB]))

                    if u:
                        ve.wait_ge(S["rows_zero"], 32 * (NB - NBMIN))
                    ve.wait_ge(S["cs_in"], 16 * c + 16)
                    srcs = [(stage[0], bank[6], "free6"), (QR[:, 0, cols], bank[7], "free7"),
                            (QR[:, 1, cols], bank[6], "free6")]
                    for n, (src, ps, free) in enumerate(srcs):
                        ve.wait_ge(S["sp_made"], 7 * c + n + 1)
                        if n:
                            ve.wait_ge(S["rope_made"], 3 * c + n + 1)
                        x1_ = step(ve.tensor_tensor(t1, src, cs[:, 0, :], ALU.mult))
                        ve.tensor_tensor(t2, ps[:], cs[:, 1, :], ALU.mult).then_inc(S[free], 1)
                        need(x1_)
                        ve.wait_ge(S[free], {0: 4 * c + 2, 1: 3 * c + 2, 2: 4 * c + 3}[n])
                        if n == 0:
                            for m, keys in enumerate((KS, KW)):
                                r = slice(64 * m, 64 * m + 64)
                                for to in (slice(0, 64), slice(64, 128)):
                                    ins = ve.tensor_tensor(keys[to, cols], t1[r, :], t2[r, :], ALU.add)
                            ins.then_inc(S["rope_made"], 1)
                        else:
                            q = step(ve.tensor_tensor(t1, t1, t2, ALU.add))
                            need(q)
                            q = step(ve.tensor_copy(t2r, t1))
                            need(q)
                            for m in range(2):
                                r = slice(64 * m, 64 * m + 64)
                                ve.tensor_tensor(QS[64:128, 2 * n - 2 + m, cols], t1[r, :], t2r[r, :].bitcast(F32), ALU.subtract)
                                ins = ve.tensor_scalar(QS[0:64, 2 * n - 2 + m, cols], t2r[r, :].bitcast(F32), 1.0, None, ALU.mult)
                            ins.then_inc(S["rope_made"], 1)
                        if n == 0:
                            ve.wait_ge(S["rope_made"], 3 * c + 2)
                            ve.sem_inc(S["stage_free"], 1)

                    for n in range(2):
                        x = cpad[n]
                        ve.wait_ge(S["tile_out"], MJ * c + NBANK + M_C0 + n + 1)
                        E = HC + TC
                        q = step(ve.tensor_tensor(s_a[:, 1:E], x[:, 1:E], x[:, 0:E - 1], ALU.add))
                        need(q)
                        if n == 0:
                            q = step(ve.tensor_tensor(s_b[64:128, 3:E], s_a[64:128, 3:E], s_a[64:128, 1:E - 2], ALU.add))
                        else:
                            q = step(ve.tensor_tensor(s_b[:, 3:E], s_a[:, 3:E], s_a[:, 1:E - 2], ALU.add))
                            need(q)
                            q = step(ve.tensor_tensor(s_a[:, 7:E], s_b[:, 7:E], s_b[:, 3:E - 4], ALU.add))
                            need(q)
                            q = step(ve.tensor_tensor(s_b[64:128, 15:E], s_a[64:128, 15:E], s_a[64:128, 7:E - 8], ALU.add))
                        need(q)
                        for lo, sm in ((0, s_a), (64, s_b)):
                            r = slice(lo, lo + 64)
                            ve.scalar_tensor_tensor(pd[n][r, 16:TC], sm[r, HC + 16:E], chan[r, CH_IW + n:CH_IW + n + 1],
                                                    x[r, HC + 16:E], ALU.mult, ALU.subtract)
                            pt = C_PT + n * NCH * 16
                            q = step(ve.tensor_tensor(pd[n][r, 0:16], sm[r, HC:HC + 16],
                                                      consts[r, bass.ds(c * 16 + pt, 16)], ALU.mult))
                            need(q)
                            ins = ve.tensor_tensor(pd[n][r, 0:16], pd[n][r, 0:16], x[r, HC:HC + 16], ALU.subtract)
                            if lo:
                                ins.then_inc(S["pool_d"], 1)
                        ve.tensor_copy(x[:, 0:HC], x[:, TC:TC + HC]).then_inc(S["cpad_free"], 1)

                    ve.wait_ge(S["sp_made"], 7 * c + 4)
                    for n in range(2):
                        ins = ve.tensor_tensor(yT[:, 2 + n, cols], yT[:, 2 + n, cols], bank[7][:], ALU.subtract)
                        ins.then_inc(S["cent"], 1)
                    ve.wait_ge(S["cent"], 2 * c + 2)
                    ve.sem_inc(S["free7"], 1)

                    for n in range(2):
                        x = apad[n]
                        ve.wait_ge(S["tile_out"], MJ * c + NBANK + M_AH0 + 3 * n + 1)
                        cst, hst, bst_ = ((1, 2, 3), (0, 1, 2))[n]
                        ve.tensor_tensor(x[:, HA:HA + TC], stage[cst], stage[hst], ALU.mult).then_inc(S["stage_free"], 1)
                        ve.wait_ge(S["stage_free"], 7 * c + 11 + 2 * n)
                        q = step(ve.tensor_scalar(s_b[:, 0:TC], x[:, 0:TC], w(CH_A + 3 * n), None, ALU.mult))
                        for k in (1, 2):
                            need(q)
                            q = step(ve.scalar_tensor_tensor(s_b[:, 0:TC], x[:, k:k + TC], w(CH_A + 3 * n + k), s_b[:, 0:TC],
                                                             ALU.mult, ALU.add))
                        q = step(ve.tensor_copy(x[:, 0:HA], x[:, TC:TC + HA]))
                        need(q)
                        ve.wait_ge(S["tile_out"], MJ * c + NBANK + M_AB0 + 3 * n + 1)
                        ve.tensor_tensor(yT[:, n, cols], s_b[:, 0:TC], stage[bst_], ALU.mult).then_inc(S["stage_free"], 1)
                        ve.wait_ge(S["stage_free"], 7 * c + 12 + 2 * n)

                    ve.wait_ge(S["std"], c + 1)
                    q = step(ve.reciprocal(sd, sd))
                    need(q)
                    for n in range(2):
                        ve.tensor_tensor(yT[:, 2 + n, cols], yT[:, 2 + n, cols], sd, ALU.mult).then_inc(S["zed"], 1)
                    ve.wait_ge(S["zed"], 2 * c + 2)
                    assert V_STEPS[0] == PER, V_STEPS[0]
            BASE = PER * NCH
            V_STEPS[0] = 0

            def need(n):
                ve.wait_ge(S["dve_step"], BASE + n)

            ve.wait_ge(S["tile_out"], MJ * NCH + NBANK)
            ve.wait_ge(S["yb_done"], 2 * NCH)
            ve.wait_ge(S["sp_made"], 7 * NCH)
            ve.tensor_copy(VC2[0:64, :], KC2[64:128, :])
            ve.tensor_copy(VC2[64:128, 0:SEQ - 1], KC2[64:128, 1:SEQ]).then_inc(S["shifted"], 1)
            ve.wait_ge(S["shifted"], 1)
            ve.tensor_copy(KC2[64:128, 0:SEQ - 1], KC2[0:64, 1:SEQ]).then_inc(S["shifted"], 1)
            step(ve.memset(psm, 0.0))
            for n, (high, keys, low) in enumerate(((KSH, KS, KSL), (KWH, KW, KWL))):
                ve.wait_ge(S["k_high"], n + 1)
                ve.tensor_tensor(low, keys, high.bitcast(F32), ALU.subtract).then_inc(S["k_low"], 1)
            ve.memset(vct[:, HD:HD + 1], 1.0).then_inc(S["cc_out"], 1)
            ve.memset(kct[64:128, 0, :], 0.0).then_inc(S["cc_out"], 1)
            ve.memset(kct[0:64, 1, :], 0.0).then_inc(S["cc_out"], 1)

            def maxes(n):
                un = units[n]
                ve.wait_ge(S["s_made"], n + 1)
                ps = bank[n % 3]
                if un[0] == "cmp":
                    ins = ve.tensor_reduce(nmx[un[1] % 2][:, :, 0:1],
                                           ps[:].rearrange("p (h n) -> p h n", h=NH)[:, :, 0:NCMP], AX.X, ALU.max, negate=True)
                else:
                    br, i, h0, g, k0, t, slot, mask = un
                    ins = ve.tensor_reduce(nmx[i % 2][:, h0:h0 + g, slot:slot + 1],
                                           ps[:, 0:g * t * P].rearrange("p (g n) -> p g n", g=g), AX.X, ALU.max, negate=True)
                ins.then_inc(S["max_made"], 1)

            def copy_turned(n):
                un = units[n]
                ve.wait_ge(S["t_made"], n + 1)
                if n >= 3:
                    ve.wait_ge(S["o_made"], n - 2)
                ps = bank[3 + n % 2]
                if un[0] == "cmp":
                    ins = ve.tensor_copy(probT[n % 3][0:NCMP, :], ps[0:NCMP, :])
                else:
                    w_ = un[3] * un[5] * P
                    ins = ve.tensor_copy(probT[n % 3][:, 0:w_], ps[:, 0:w_])
                ins.then_inc(S["pt_made"], 1)

            def sums(i):
                p_ = pn[i % 2][:, :, 0:NCMP]
                tot, inv = small[:, 0:4, 20:21], small[:, 0:4, 21:22]
                q = step(ve.tensor_reduce(tot, p_, AX.X, ALU.add))
                need(q)
                q = step(ve.reciprocal(inv, tot))
                need(q)
                q = step(ve.tensor_tensor(p_, p_, inv.to_broadcast((P, NH, NCMP)), ALU.mult))
                need(q)
                q = step(ve.tensor_reduce(psm[:, 1:1 + NCMP].rearrange("p (n o) -> p n o", o=1),
                                          p_.rearrange("p h n -> p n h"), AX.X, ALU.add))
                need(q)

            def importance(i):
                if i > 8:
                    ve.wait_ge(S["mkT_made"], i - 8)
                q = step(ve.tensor_reduce(imp[0].rearrange("p (n o) -> p n o", o=1),
                                          psm[:, 0:P].rearrange("p (j k) -> p j k", k=4), AX.X, ALU.add))
                need(q)
                q = step(ve.tensor_tensor(imp[0], imp[0], psm[:, 4:132:4], ALU.add))
                need(q)
                q = step(ve.tensor_tensor(imp[0], imp[0], C(C_KEEP + 32 - 2 * i, NSEL), ALU.mult))
                need(q)
                q = step(ve.tensor_tensor(imp[0], imp[0], C(C_ADD + 32 - 2 * i, NSEL), ALU.add))
                need(q)
                q = step(ve.memset(imp[0][:, 0:1], FORCE))
                need(q)
                m8 = small[:, 1, 22:30]
                for r in range(2):
                    src, dst = (imp[0], imp[1]) if r == 0 else (imp[1], imp[0])
                    q = step(ve.max(m8, src))
                    need(q)
                    q = step(ve.match_replace(dst, m8, src, USED))
                    need(q)
                ve.tensor_scalar(imp[0], imp[0], USED / 2, NEG, ALU.is_gt, ALU.mult).then_inc(S["mk_made"], 1)

            def rows_of_mask(i):
                ve.wait_ge(S["mkT_made"], i - 7)
                ve.tensor_copy(qmask[:, i % 2, :], bank[7][0:NSEL, 0:P]).then_inc(S["mask_rows"], 1)

            MM = small[:, 0:4, 0:2]
            LL, RR = small[:, 4:8, 0:3], small[:, 4:8, 3:6]

            def shifts(i):
                ns, nw = n_slc[i], n_win[i]
                q = step(ve.tensor_reduce(MM[:, :, 0:1], nmx[i % 2][:, :, 1:1 + ns], AX.X, ALU.min))
                q = step(ve.tensor_reduce(MM[:, :, 1:2], nmx[i % 2][:, :, 1 + ns:1 + ns + nw], AX.X, ALU.min))
                need(q)
                for m, (lo, k) in enumerate(((0, ns), (ns, nw))):
                    ins = ve.tensor_tensor(small[:, 0:4, 8 + lo:8 + lo + k], MM[:, :, m:m + 1].to_broadcast((P, NH, k)),
                                           nmx[i % 2][:, :, 1 + lo:1 + lo + k], ALU.subtract)
                    if m == 0:
                        continue
                    ins.then_inc(S["d_made"], 1)

            def weights(i):
                ns, nw = n_slc[i], n_win[i]
                k = ns + nw
                F, FL, AL, ob = small[:, 0:4, 8:8 + k], small[:, 8:12, 0:k], share(i), OB[i % 2]
                ve.wait_ge(S["f_made"], i + 1)
                ve.wait_ge(S["o_out"], last_of[i] + 1)
                if i >= 2:
                    ve.wait_ge(S["y_made"], i - 1)
                q = step(ve.tensor_tensor(FL, F, ob[:, :, 1:k + 1, 64], ALU.mult))
                need(q)
                step(ve.tensor_copy(LL[:, :, 0:1], ob[:, :, 0, 64:65]))
                step(ve.tensor_reduce(LL[:, :, 1:2], FL[:, :, 0:ns], AX.X, ALU.add))
                q = step(ve.tensor_reduce(LL[:, :, 2:3], FL[:, :, ns:k], AX.X, ALU.add))
                need(q)
                q = step(ve.reciprocal(RR, LL))
                need(q)
                q = step(ve.tensor_tensor(RR, RR, gates[:, i, :].rearrange("p (h g) -> p h g", g=3), ALU.mult))
                need(q)
                if i == 0:
                    step(ve.tensor_scalar(AL[:, :, 0:1], RR[:, :, 0:1], C(C_VALID, 1), None, ALU.mult))
                else:
                    step(ve.tensor_copy(AL[:, :, 0:1], RR[:, :, 0:1]))
                step(ve.tensor_tensor(AL[:, :, 1:1 + ns], F[:, :, 0:ns], RR[:, :, 1:2].to_broadcast((P, NH, ns)), ALU.mult))
                ve.tensor_tensor(AL[:, :, 1 + ns:1 + k], F[:, :, ns:k], RR[:, :, 2:3].to_broadcast((P, NH, nw)), ALU.mult
                                 ).then_inc(S["al_made"], 1)

            N = len(units)
            for n in range(-1, N + LATE):
                for i in range(NT):
                    if i >= 8 and n + 2 == first_slc[i]:
                        rows_of_mask(i)
                if 0 <= n + 1 < N:
                    maxes(n + 1)
                if 0 <= n < N:
                    copy_turned(n)
                for i in range(8, NT):
                    if n == cmp_at[i]:
                        sums(i)
                    if n == cmp_at[i] + 2:
                        importance(i)
                for i in range(NT):
                    if n - 2 == last_of[i]:
                        shifts(i)
                    if n - 3 == last_of[i]:
                        weights(i)

            ve.wait_ge(S["ln_in"], 48)
            for t in range(NT):
                u = t % 2
                r_, st = rrow[u], bst[u]
                ve.wait_ge(S["mix_made"], t + 1)
                ve.wait_ge(S[f"xr_in{u}"], 16 * (t // 2) + 16)
                for m in range(2):
                    c_ = slice(m * 512, (m + 1) * 512)
                    ve.scalar_tensor_tensor(r_[:, c_], xrow[u][:, c_], ALPHA, bank[2 * u + m][:], ALU.mult, ALU.add
                                            ).then_inc(S["mix_used"], 1)
                ve.wait_ge(S["mix_used"], 2 * (t + 1))
                step(ve.bn_stats(st[:, 0:6], r_[:, 0:512]))
                q = step(ve.bn_stats(st[:, 6:12], r_[:, 512:1024]))
                need(q)
                ve.bn_aggr(st[:, 12:14], st[:, 0:12]).then_inc(S["sq_in"], 1)
                ve.wait_ge(S["sq_out"], t + 1)
                q = step(ve.reciprocal(st[:, 15:16], st[:, 14:15]))
                need(q)
                ve.tensor_scalar(x1s[:, t, :], r_, st[:, 12:13], st[:, 15:16], ALU.subtract, ALU.mult
                                 ).then_inc(S["norm_made"], 1)

            ve.wait_ge(S["aff_made"], 1)
            ve.wait_ge(S["route_in"], 16)

            def do(ins):
                need(step(ins))

            b16 = lambda x, n: x[:, :, None].to_broadcast((P, NT, n))
            bia = rt[1]
            do(ve.tensor_tensor(bia[:, :, :], aff[:, :, :], rbias[:, None, :].to_broadcast((P, NT, NE)), ALU.add))
            v = bia[:, :, :].rearrange("p t (g k) -> p t g k", k=4)
            vk = [v[:, :, :, k] for k in range(4)]
            do(ve.tensor_tensor(r4[0][:, :, :], vk[0], vk[1], ALU.max))
            do(ve.tensor_tensor(r4[1][:, :, :], vk[0], vk[1], ALU.min))
            do(ve.tensor_tensor(r4[2][:, :, :], vk[2], vk[3], ALU.max))
            do(ve.tensor_tensor(r4[3][:, :, :], vk[2], vk[3], ALU.min))
            do(ve.tensor_tensor(r4[4][:, :, :], r4[0][:, :, :], r4[2][:, :, :], ALU.max))
            do(ve.tensor_tensor(r4[5][:, :, :], r4[0][:, :, :], r4[2][:, :, :], ALU.min))
            do(ve.tensor_tensor(r4[6][:, :, :], r4[1][:, :, :], r4[3][:, :, :], ALU.max))
            do(ve.tensor_tensor(r4[5][:, :, :], r4[5][:, :, :], r4[6][:, :, :], ALU.max))
            do(ve.tensor_tensor(r4[7][:, :, :], r4[4][:, :, :], r4[5][:, :, :], ALU.add))

            def first_max(out_, x, order, eq, wgt, m1, m2, n):
                do(ve.tensor_reduce(m1[:, :, None], x, AX.X, ALU.max))
                do(ve.tensor_tensor(eq, x, b16(m1, n), ALU.is_equal))
                do(ve.tensor_tensor(wgt, eq, order[:, None, :].to_broadcast((P, NT, n)), ALU.mult))
                do(ve.tensor_reduce(m2[:, :, None], wgt, AX.X, ALU.max))
                do(ve.tensor_tensor(out_, wgt, b16(m2, n), ALU.is_equal))

            first_max(r4[2][:, :, :], r4[7][:, :, :], C(C_GW, 4), r4[0][:, :, :], r4[1][:, :, :], r1[0], r1[1], 4)
            do(ve.tensor_copy(rt[2][:, :, :].rearrange("p t (g k) -> p t g k", k=4),
                              r4[2][:, :, :, None].to_broadcast((P, NT, 4, 4))))
            do(ve.tensor_tensor(rt[3][:, :, :], bia[:, :, :], rt[2][:, :, :], ALU.mult))
            do(ve.tensor_scalar(rt[4][:, :, :], rt[2][:, :, :], -NEG, NEG, ALU.mult, ALU.add))
            do(ve.tensor_tensor(rt[5][:, :, :], rt[3][:, :, :], rt[4][:, :, :], ALU.add))
            for c in range(2):
                oh = rt[8 + c][:, :, :]
                first_max(oh, rt[5][:, :, :], C(C_EW, NE), rt[6][:, :, :], rt[7][:, :, :], r1[2], r1[3], NE)
                do(ve.scalar_tensor_tensor(rt[5][:, :, :], oh, 2 * NEG, rt[5][:, :, :], ALU.mult, ALU.add))
                do(ve.tensor_tensor(rt[6][:, :, :], aff[:, :, :], oh, ALU.mult))
                do(ve.tensor_reduce(r1[4 + c][:, :, None], rt[6][:, :, :], AX.X, ALU.add))
            ve.tensor_tensor(rt[0][:, :, :], rt[8][:, :, :], rt[9][:, :, :], ALU.add).then_inc(S["oh_made"], 1)
            do(ve.tensor_tensor(r1[2], r1[4], r1[5], ALU.add))
            do(ve.reciprocal(r1[3], r1[2]))
            for c in range(2):
                do(ve.tensor_tensor(dest_w[:, c, :], r1[4 + c], r1[3], ALU.mult))
            ve.wait_ge(S["cum_made"], 1)
            fl = lambda t: t[:, :, :].rearrange("p a b -> p (a b)")
            do(ve.tensor_copy(fl(rt[10]), bank[0][:, 0:256]))
            do(ve.tensor_copy(fl(rt[11]), bank[1][:, 0:256]))
            do(ve.memset(rt[12][:, 0, :], 0.0))
            for t in range(1, NT):
                do(ve.tensor_tensor(rt[12][:, t, :], rt[12][:, t - 1, :], rt[11][:, t - 1, :], ALU.add))
            cnt, nblk, sb_, incl = (cnt16[:, k, :] for k in range(4))
            do(ve.tensor_tensor(cnt, rt[12][:, NT - 1, :], rt[11][:, NT - 1, :], ALU.add))
            do(ve.tensor_tensor(cmp256[:, :, :], cnt[:, :, None].to_broadcast((P, NE, NE)),
                                C(C_K128, NE)[:, None, :].to_broadcast((P, NE, NE)), ALU.is_gt))
            do(ve.tensor_reduce(nblk[:, :, None], cmp256[:, :, :], AX.X, ALU.add))
            do(ve.tensor_tensor(cmp256[:, :, :], C(C_LT, 256).rearrange("p (a b) -> p a b", a=NE),
                                nblk[:, None, :].to_broadcast((P, NE, NE)), ALU.mult))
            do(ve.tensor_reduce(sb_[:, :, None], cmp256[:, :, :], AX.X, ALU.add))
            do(ve.tensor_tensor(incl, sb_, nblk, ALU.add))
            do(ve.tensor_tensor(rt[13][:, :, :], rt[10][:, :, :], rt[12][:, :, :], ALU.add))
            do(ve.scalar_tensor_tensor(rt[13][:, :, :], sb_[:, None, :].to_broadcast((P, NT, NE)), float(P),
                                       rt[13][:, :, :], ALU.mult, ALU.add))
            for c in range(2):
                do(ve.tensor_tensor(rt[6][:, :, :], rt[8 + c][:, :, :], rt[13][:, :, :], ALU.mult))
                do(ve.tensor_reduce(r1[6 + c][:, :, None], rt[6][:, :, :], AX.X, ALU.add))
                do(ve.tensor_copy(dest_i[:, c, :], r1[6 + c]))
            ve.sem_inc(S["dest_made"], 1)
            do(ve.tensor_tensor(tb[0][0:1, :, :], incl[0:1, None, :].to_broadcast((1, 64, NE)),
                                consts[0:1, C_BIDX:C_BIDX + 64, None].to_broadcast((1, 64, NE)), ALU.is_le))
            do(ve.tensor_reduce(tb1[0][0:1, :, None], tb[0][0:1, :, :], AX.X, ALU.add))
            do(ve.tensor_scalar(tb1[0][0:1, :], tb1[0][0:1, :], float(NE - 1), None, ALU.min))
            do(ve.tensor_copy(tables[0:1, 0, :], tb1[0][0:1, :]))
            do(ve.tensor_copy(tables[0:1, 1, 0:NE], incl[0:1, :]))
            do(ve.tensor_scalar(tables[0:1, 2, :], tables[0:1, 0, :], 1, 1, ALU.bitwise_and, ALU.bitwise_xor))
            do(ve.tensor_scalar(tb1[1][0:1, :], consts[0:1, C_BIDX:C_BIDX + 64], 2.0, incl[0:1, NE - 1:NE], ALU.mult, ALU.is_lt))
            do(ve.tensor_reduce(tb1[2][0:1, 0:1], tb1[1][0:1, :], AX.X, ALU.add))
            do(ve.tensor_copy(tables[0:1, 1, NE:NE + 1], tb1[2][0:1, 0:1]))
            ve.sem_inc(S["tab_made"], 1)

            ve.sem_inc(S["h_made"], 1)
            ve.sem_inc(S["ht_out"], 1)
            ve.sem_inc(S["dn_outd"], 1)
            pairs = ve.value_load(tables[0:1, 1, NE:NE + 1], min_val=1, max_val=NB // 2)
            with ve.Fori(0, NB // 2) as bb, ve.If(bb < pairs):
                for u in range(2):
                    b = bb * 2 + u
                    ve.wait_ge(S["act_made"], b + 1)
                    ve.tensor_tensor(hrow[u], hrow[u], bank[3][:], ALU.mult).then_inc(S["h_made"], 1)
                    ve.wait_ge(S["ht_made"], b + 3)
                    ve.tensor_copy(hTm[u][:, :, :].rearrange("p a b -> p (a b)"), bank[4][:]).then_inc(S["ht_out"], 1)
                    ve.wait_ge(S["blk_done"], b + 2)
                    ve.wait_ge(S[f"ysto{u}"], 16 * bb + 16)
                    ve.tensor_copy(yrw[u][:, 512:1024], bank[6][:]).then_inc(S["dn_outd"], 1)

            base6 = BASE + V_STEPS[0]
            with ve.Fori(0, NT // R6) as tt:
                for u in range(R6):
                    t = tt * R6 + u
                    V_STEPS[0] = 4 * u
                    def need6(n):
                        ve.wait_ge(S["dve_step"], base6 + 4 * R6 * tt + n)
                    st = b6[u]
                    ve.wait_ge(S["w6"], t + 1)
                    q = step(ve.scalar_tensor_tensor(ya[u], yb[u], dest_w[:, 1, bass.ds(t, 1)], ya[u], ALU.mult, ALU.add))
                    need6(q)
                    ve.scalar_tensor_tensor(ya[u], x1s[:, bass.ds(t, 1), :].rearrange("p a n -> p (a n)"), ALPHA, ya[u],
                                            ALU.mult, ALU.add).then_inc(S["r6"], 1)
                    ve.wait_ge(S["r6"], t + 1)
                    step(ve.bn_stats(st[:, 0:6], ya[u][:, 0:512]))
                    q = step(ve.bn_stats(st[:, 6:12], ya[u][:, 512:1024]))
                    need6(q)
                    ve.sem_inc(S["stats6"], 1)
                    ve.bn_aggr(st[:, 12:14], st[:, 0:12]).then_inc(S["s6_in"], 1)
                    ve.wait_ge(S["s6_out"], t + 1)
                    q = step(ve.reciprocal(st[:, 15:16], st[:, 14:15]))
                    need6(q)
                    ve.wait_ge(S[f"out6{u}"], 16 * tt + 16)
                    ve.tensor_scalar(fin[u], ya[u], st[:, 12:13], st[:, 15:16], ALU.subtract, ALU.mult
                                     ).then_inc(S["c6"], 1)
                    ve.wait_ge(S["c6"], t + 1)
                    ve.tensor_tensor(fin[u], fin[u], ln2_g, ALU.mult).then_inc(S["fin6"], 1)

        @block.gpsimd
        def _(po):
            po.memset(zero_i[:, :], 0).then_inc(S["zero_made"], 1)
            po.memset(zeros, 0.0).then_inc(S["zero_made"], 1)
            po.wait_ge(S["zero_made"], 2)
            po.wait_ge(S["tile_made"], MJ + 1 + MJ)
            for b in range(NBMIN, NB):
                for n in range(2):
                    po.dma_start(y_dram[b * P:(b + 1) * P, n * TC:(n + 1) * TC], zeros).then_inc(S["rows_zero"], 16)
            done = 0
            for i in range(NT):
                k = n_slc[i] + n_win[i] + 1
                v = OB[i % 2][:, :, 0:k, 0:HD]
                y = yrow[i % 2].rearrange("p (h d) -> p h d", h=NH)
                po.wait_ge(S["al_made"], i + 1)
                po.tensor_tensor(v, v, share(i)[:, :, :, None].to_broadcast((P, NH, k, HD)), ALU.mult).then_inc(S["po_step"], 1)
                done += 1
                if i >= 2:
                    po.wait_ge(S["yT_made"], i - 1)
                for m in range(1, k):
                    po.wait_ge(S["po_step"], done)
                    po.tensor_tensor(y, v[:, :, 0, :] if m == 1 else y, v[:, :, m, :], ALU.add
                                     ).then_inc(S["po_step" if m < k - 1 else "y_made"], 1)
                    done += m < k - 1
            po.wait_ge(S["ln_in"], 48)
            for t in range(NT):
                x_ = x1s[:, t, :]
                po.wait_ge(S["norm_made"], t + 1)
                po.tensor_tensor(x_, x_, ln_g, ALU.mult).then_inc(S["n6"], 1)
                po.wait_ge(S["n6"], t + 1)
                po.tensor_tensor(x_, x_, ln_b, ALU.add).then_inc(S["x1_made"], 1)
                po.wait_ge(S["x1_made"], t + 1)
                po.dma_start(x1_dram[t * P:(t + 1) * P, :], x_).then_inc(S["x1_stored"], 16)
            po.wait_ge(S["slot_zero"], 16)
            po.wait_ge(S["dest_made"], 1)
            for c in range(2):
                for t in range(NT):
                    po.indirect_dma_start(slot_dram, bass.IndirectOffsetOnAxis(ap=dest_i[:, c, t:t + 1], axis=0),
                                          tok_i[:, t:t + 1], None).then_inc(S["slot_stored"], 16)
            po.wait_ge(S["slot_stored"], 32 * NT)
            po.wait_ge(S["x1_stored"], 16 * NT)
            po.wait_ge(S["tab_made"], 1)

            def fetch(b, u, n, wait_free):
                if wait_free:
                    po.wait_ge(S["gx_made"], b - 1)
                po.dma_start(idx[u][:, :], slot_dram[bass.ds(b * P, P), :]).then_inc(S[f"idx{u}"], 16)
                po.wait_ge(S[f"idx{u}"], 16 * n + 16)
                po.sem_inc(S["idx_in"], 1)
                po.indirect_dma_start(xg[u], None, x1_dram, bass.IndirectOffsetOnAxis(ap=idx[u][:, 0:1], axis=0)
                                      ).then_inc(S[f"g_in{u}"], 16)

            fetch(0, 0, 0, False)
            fetch(1, 1, 0, False)
            fetch(2, 0, 1, True)
            pairs = po.value_load(tables[0:1, 1, NE:NE + 1], min_val=1, max_val=NB // 2)
            with po.Fori(0, NB // 2 - 1) as bb, po.If(bb + 1 < pairs):
                for u in range(2):
                    fetch(bb * 2 + u + 3, 1 - u, bb + 1 + u, True)
            po.wait_ge(S["ysto0"], pairs * 16 + 16)
            po.wait_ge(S["ysto1"], pairs * 16 + 16)
            po.wait_ge(S["l2_in"], 32)
            po.wait_ge(S["gx_made"], pairs * 2 + 1)
            po.sem_inc(S["idx_in"], 1)

            def rows(t, u):
                for c, buf in enumerate((ya, yb)):
                    po.indirect_dma_start(buf[u], None, y_dram,
                                          bass.IndirectOffsetOnAxis(ap=dest_i[:, c, t:t + 1], axis=0)
                                          ).then_inc(S[f"ya_in{u}"], 16)

            for t in range(R6):
                rows(t, t)
            for t in range(NT):
                u = t % R6
                if t + R6 < NT:
                    po.wait_ge(S["c6"], t + 1)
                    rows(t + R6, u)
                po.wait_ge(S["fin6"], t + 1)
                po.tensor_tensor(fin[u], fin[u], ln2_b, ALU.add).then_inc(S["p6"], 1)


def layout(x, w_in, conv_a_w, conv_b_w, conv_b_b, cf_ln_g, cf_ln_b, pool_w, pool_scale,
           cmp_pe_k, cmp_pe_v, cmp_k_w1, cmp_k_w2, cmp_v_w1, cmp_v_w2, w_out,
           ln1_g, ln1_b, ln2_g, ln2_b, router_w, router_bias, moe_w_gate, moe_w_up, moe_w_down):
    x = np.asarray(x).reshape(SEQ, D)
    w_in = np.asarray(w_in)[0]
    tiles, tm = column_tiles()
    c, k, cs, iw = shape_constants()
    two = lambda v: np.asarray(v).reshape(2, P).T
    taps = lambda v, n: np.asarray(v)[0].reshape(n, 2, P).transpose(2, 1, 0).reshape(P, 2 * n)
    chan = np.concatenate([taps(conv_a_w, AK), taps(conv_b_w, CK), two(conv_b_b), two(cf_ln_g), two(cf_ln_b),
                           two(pool_scale), iw, np.full((P, 1), EPS, np.float32)], 1)
    pw = np.zeros((P, 2, P), np.float32)
    for g in range(4):
        r = slice(64 * (g % 2), 64 * (g % 2) + 64)
        pw[r, g // 2, r] = np.asarray(pool_w)[0, g]
    kt = lambda w_: np.asarray(w_).reshape(KD, P, -1).transpose(1, 0, 2)
    w2 = np.zeros((P, 2, 2, P), np.float32)
    for n, w_ in enumerate((cmp_k_w2, cmp_v_w2)):
        w_ = np.asarray(w_)[0].reshape(2, P, HD).transpose(1, 0, 2)
        w2[:, n, :, 0:HD] = w_
        w2[:, n, :, HD:] = w_
    pe2 = np.stack([np.asarray(p_)[0].reshape(16, P).T for p_ in (cmp_pe_k, cmp_pe_v)], 1)
    we = np.stack([np.asarray(moe_w_gate)[0].reshape(NE, KD, P, DE).transpose(0, 2, 1, 3).reshape(NE, P, KD * DE),
                   np.asarray(moe_w_up)[0].reshape(NE, KD, P, DE).transpose(0, 2, 1, 3).reshape(NE, P, KD * DE),
                   np.asarray(moe_w_down)[0].reshape(NE, 4, P, D).transpose(0, 2, 1, 3).reshape(NE, P, 4 * D)], 1)
    arrays = {
        "x": x,
        "xT": x.reshape(NCH, TC, KD, P).transpose(0, 3, 2, 1).reshape(NCH, P, KD * TC),
        "w_in": np.stack([kt(w_in[:, t]).reshape(P, KD * P) for t in tiles]),
        "w_tm": kt(w_in[:, tm]).reshape(P, -1),
        "consts": c, "masks": k, "cs": cs, "chan": chan, "pool_w": pw.reshape(P, -1),
        "cmp_w1": np.stack([np.asarray(w_)[0].reshape(16, P, CHID).transpose(1, 0, 2).reshape(P, -1)
                            for w_ in (cmp_k_w1, cmp_v_w1)]),
        "cmp_w2": w2.reshape(P, -1), "cmp_pe": pe2.reshape(P, -1),
        "w_out": np.asarray(w_out)[0].reshape(2, KD // 2, P, D).transpose(0, 2, 1, 3).reshape(2, P, -1),
        "ln1_g": np.asarray(ln1_g)[0], "ln1_b": np.asarray(ln1_b)[0],
        "ln2_g": np.asarray(ln2_g)[0], "ln2_b": np.asarray(ln2_b)[0],
        "router_w": kt(router_w).reshape(P, -1), "router_bias": np.asarray(router_bias), "w_exp": we,
    }
    return {"in_" + n: np.ascontiguousarray(v) for n, v in arrays.items()}


def kernel(**inputs):
    import concourse.bacc as bacc
    from concourse.bass_utils import run_bass_kernel_spmd

    arrays = layout(**inputs)
    nc = bacc.Bacc("TRN2", target_bir_lowering=False, num_devices=1, dynamic_dma_scratch_size=2048)
    aps = {n[3:]: nc.dram_tensor(n, v.shape, F32, kind="ExternalInput").ap() for n, v in arrays.items()}
    out = nc.dram_tensor("out", (SEQ, D), F32, kind="ExternalOutput").ap()
    hybrid_layer(nc, aps, out)
    r = run_bass_kernel_spmd(nc, [arrays], core_ids=[0])
    return r.results[0]["out"].reshape(1, SEQ, D)
```

```python
from contextlib import ExitStack

import numpy as np
import concourse.bass as bass
import concourse.mybir as mybir

F32 = mybir.dt.float32
BF16 = mybir.dt.bfloat16
F32R = mybir.dt.float32r
I32 = mybir.dt.int32
ACT = mybir.ActivationFunctionType
ALU = mybir.AluOpType
AX = mybir.AxisListType

P = 128
SEQ, D = 2048, 1024
KD = D // P
TC = 512
NCH = SEQ // TC
NT = SEQ // P
GW = 256
HD = 64
NH = 4
CK, AK = 31, 3
HB, HA, HC = CK - 1, AK - 1, 16
NCMP = (SEQ - 32) // 16 + 1
CHID = 256
NSEL = SEQ // 64
WT = 4
NE, DE = 16, 512
R6 = 4
ALPHA = 2.0 ** 0.25
EPS = 1e-5
NEG = -1e30
FORCE = 1e4
USED = -3e38
NB = (2 * SEQ + NE * (P - 1)) // P + 1
NB += NB % 2
NBMIN = 2 * SEQ // P

M_BG0, M_BV0, M_BG1, M_BV1, M_KC, M_KS, M_Q0, M_Q1, M_C0, M_C1 = range(10)
M_AC0, M_AH0, M_AB0, M_AC1, M_AH1, M_AB1 = range(10, 16)
NM = 16
NTM = 140
MJ = NM + 2
NBANK = 6


def column_tiles():
    r = lambda a, n=P: list(range(a, a + n))
    o_b, o_c, o_h, o_val, o_gate, o_p, o_q, o_kc = 0, 256, 512, 768, 1024, 1280, 1536, 1792
    vc, ks, vs, kw, vw, g = (o_kc + 64 * n for n in range(1, 7))
    tiles = [r(o_gate), r(o_val), r(o_gate + P), r(o_val + P), r(o_kc, 64) + r(vc, 64), r(ks, 64) + r(kw, 64),
             r(o_q), r(o_q + P), r(o_p), r(o_p + P),
             r(o_c), r(o_h), r(o_b), r(o_c + P), r(o_h + P), r(o_b + P)]
    return tiles, r(vs, 64) + r(vw, 64) + r(g, 12)


CH_A, CH_B, CH_BB, CH_G, CH_BE, CH_PS, CH_IW, CH_EPS = 0, 6, 68, 70, 72, 74, 76, 78
NCHAN = 79

C_PERM, C_MEAN, C_ID = 0, P, 2 * P
C_VALID = 3 * P
C_KEEP = C_VALID + 4
C_ADD = C_KEEP + 64
C_EW = C_ADD + 64
C_GW = C_EW + 16
C_K128 = C_GW + 4
C_LT = C_K128 + 16
C_BIDX = C_LT + 256
C_TOK = C_BIDX + 64
C_PT = C_TOK + 16
NCONST = C_PT + 2 * NCH * 16
K_ID, K_TRI, K_WIN, K_CMP = 0, P, P + 512, P + 1024
K_ONE = K_CMP + 256
NMASK = K_ONE + 2 * P


def shape_constants():
    p = np.arange(P)[:, None]
    c = np.zeros((P, NCONST), np.float32)
    perm = np.zeros((P, P), np.float32)
    for m in range(P):
        b, d = m // 64 * 64, m % 64
        if d < 32:
            perm[b + d + 32, m] = -1.0
        else:
            perm[b + d - 32, m] = 1.0
    c[:, C_PERM:C_PERM + P] = perm
    c[:, C_MEAN:C_MEAN + P] = 1.0 / GW
    c[:, C_ID:C_ID + P] = np.eye(P)
    c[:, C_VALID] = (p[:, 0] >= 31)
    j = np.arange(64)[None] - 32
    cur = p // 64
    forced = (j == cur) | (j == cur - 1)
    future = j > cur
    c[:, C_KEEP:C_KEEP + 64] = ~(forced | future)
    c[:, C_ADD:C_ADD + 64] = np.where(future, NEG, np.where(forced, FORCE, 0.0))
    c[:, C_EW:C_EW + 16] = 16 - np.arange(16)
    c[:, C_GW:C_GW + 4] = 4 - np.arange(4)
    c[:, C_K128:C_K128 + 16] = P * np.arange(16)
    e = np.arange(16)
    c[:, C_LT:C_LT + 256] = (e[None, :] < e[:, None]).reshape(1, 256)
    c[:, C_BIDX:C_BIDX + 64] = np.arange(64)
    c[:, C_TOK:C_TOK + 16] = p + P * np.arange(16)[None]
    win = np.array([[2, 4], [8, 16]])
    pt = np.zeros((P, 2, NCH, 16), np.float32)
    for t in range(2):
        for half in range(2):
            w = win[t, half]
            for ch in range(NCH):
                cnt = np.minimum(ch * TC + np.arange(16) + 1, w)
                pt[64 * half:64 * half + 64, t, ch] = 1.0 / cnt.astype(np.float32)
    c[:, C_PT:] = pt.reshape(P, -1)
    k = np.zeros((P, NMASK), np.float32)
    k[:, K_ID:K_ID + P] = np.eye(P)
    q, key = p, np.arange(P)[None]
    k[:, K_TRI + 384:K_TRI + 512] = np.where(key > q, NEG, 0.0)
    k[:, K_WIN:K_WIN + P] = np.where(key > q, 0.0, NEG)
    k[:, K_ONE:K_ONE + P] = 1.0
    k[:, K_ONE + P:K_ONE + 2 * P] = p < np.arange(P)[None]
    n = np.arange(256)[None] - P
    k[:, K_CMP:K_CMP + 256] = np.where(16 * n + 31 <= p, 0.0, NEG)
    inv = (1.0 / (np.float32(10000.0) ** (np.arange(0, HD, 2, dtype=np.float32) / np.float32(HD)))).astype(np.float32)
    ang = (np.arange(SEQ, dtype=np.float32)[None] * np.tile(inv, 4)[:, None]).astype(np.float32)
    cs = np.stack([np.cos(ang), np.sin(ang)]).astype(np.float32)
    cs = np.ascontiguousarray(cs.reshape(2, P, NCH, TC).transpose(2, 1, 0, 3).reshape(NCH, P, 2 * TC))
    iw = np.stack([np.where(np.arange(P) < 64, 1.0 / win[t, 0], 1.0 / win[t, 1]) for t in range(2)], 1)
    return c, k, cs, iw.astype(np.float32)


def attention_units():
    def rest(branch, i, k0, r, slot):
        g = 4 // r
        return [(branch, i, h, g, k0, r, slot, "tri") for h in range(0, NH, g)]

    def n_slc(i):
        return i // 4 + 1

    units = [("cmp", 0)]
    for i in range(NT):
        ns = n_slc(i)
        if i < WT:
            units += rest("win", i, 0, i + 1, ns + 1)
        else:
            units += [("win", i, h, 1, i - WT, WT, ns + 1, "win") for h in range(NH)]
            units += rest("win", i, i, 1, ns + 2)
        if i + 1 < NT:
            units.append(("cmp", i + 1))
        for c in range(ns - 1):
            units += [("slc", i, h, 1, 4 * c, 4, c + 1, None) for h in range(NH)]
        units += rest("slc", i, 4 * (ns - 1), i + 1 - 4 * (ns - 1), ns)
    return units


def hybrid_layer(nc, a, out):
    units = attention_units()
    last_of = {i: max(n for n, u in enumerate(units) if u[0] != "cmp" and u[1] == i) for i in range(NT)}
    LATE = 8
    cmp_at = {u[1]: n for n, u in enumerate(units) if u[0] == "cmp"}
    first_slc = {i: min(n for n, u in enumerate(units) if u[0] == "slc" and u[1] == i) for i in range(NT)}
    n_slc = {i: i // 4 + 1 for i in range(NT)}
    n_win = {i: 1 if i < WT else 2 for i in range(NT)}

    x1_dram = nc.dram_tensor("x1_rows", (SEQ, D), F32).ap()
    y_dram = nc.dram_tensor("expert_rows", (NB * P, D), F32).ap()
    slot_dram = nc.dram_tensor("slot_token", ((NB + 1) * P, 1), I32).ap()

    with ExitStack() as ctx:
        sem_ = {}

        def sem(name):
            sem_[name] = ctx.enter_context(nc.semaphore(name))
            return sem_[name]

        ARENA = 55632
        ARENA_AT = -(-nc.sbuf_base // 32) * 32
        ctx.enter_context(nc.sbuf_tensor("arena", [P, ARENA], F32))
        top, carved = [0], []

        def carve(*shape, at=None, dtype=F32):
            n = int(np.prod(shape))
            if at is None:
                at = top[0]
                top[0] += -(-n // 8) * 8
            assert at + n <= ARENA, (at, n)
            v = nc.alloc_sbuf_tensor_at(f"at{at}_{len(carved)}", [P, n], dtype, offset=ARENA_AT + 4 * at)[:, :]
            carved.append(at)
            if len(shape) == 2:
                v = v.rearrange("p (a b) -> p a b", a=shape[0])
            if len(shape) == 3:
                v = v.rearrange("p (a b c) -> p a b c", a=shape[0], b=shape[1])
            return v

        def carve_parts(*shape, at=None):
            return carve(*shape, at=at, dtype=F32R)

        consts = carve(NCONST)
        chan = carve(NCHAN)
        masks = ctx.enter_context(nc.sbuf_tensor("masks", [P, NMASK], BF16))
        gates = carve(NT, 12)
        dest_w = carve(2, NT)
        dest_i = ctx.enter_context(nc.sbuf_tensor("dest_i", [P, 2, NT], I32))
        tok_i = ctx.enter_context(nc.sbuf_tensor("tok_i", [P, NT], I32))
        tables = ctx.enter_context(nc.sbuf_tensor("tables", [1, 3, 64], I32))
        PERSIST = top[0]
        WE = KD * DE * 2 + 4 * D
        yT = carve(KD, SEQ)
        QS = carve_parts(NH, SEQ)
        QR = carve(2, SEQ)
        AT_K = top[0]
        KS, KW = carve(SEQ), carve(SEQ)
        KSL, KWL = (carve_parts(SEQ, at=AT_K + n * SEQ) for n in range(2))
        VS = carve(NT, 65)
        VW = carve(NT, 65)
        TEMP = top[0]
        KC2 = yT[:, 6, :]
        VC2 = yT[:, 7, :]
        yTl = carve_parts(KD, SEQ, at=PERSIST)
        x1t = lambda t: yT[:, :, bass.ds(t * P, P)]
        WEIGHTS = PERSIST + KD * SEQ
        zeros = carve(TC, at=PERSIST + KD * SEQ + NH * SEQ - TC)
        xT = [carve(KD, TC) for _ in range(2)]
        wt = [carve(KD, P) for _ in range(2)]
        w_tm = carve(KD, NTM)
        cs = carve(2, TC)
        stage = [carve(TC) for _ in range(4)]
        cpad = [carve(HC + TC) for _ in range(2)]
        bpad = [carve(HB + TC) for _ in range(2)]
        apad = [carve(HA + TC) for _ in range(2)]
        s_a, s_b = carve(HC + TC), carve(HC + TC)
        pd = [yT[:, 7, n * TC:(n + 1) * TC] for n in range(2)]
        pool_w = carve(2, P)
        t1, t2 = (yT[:, 7, n * TC:(n + 1) * TC] for n in (2, 3))
        sd = s_a[:, 0:TC]
        t2r = t2.bitcast(F32R)
        top[0] = TEMP
        w1 = [carve(16, CHID), carve(16, CHID, at=ARENA - 16 * CHID)]
        KSH, KWH = (carve_parts(SEQ, at=TEMP + n * SEQ) for n in range(2))
        w2 = carve(2, 2, P)
        pe2 = carve(2, 16)
        hT = [carve(2, P) for _ in range(2)]
        hbias = carve(4)
        kct = carve(2, P)
        vct = carve(HD + 1)
        PROB = top[0]
        prob = [carve(TC) for _ in range(4)]
        probT = [carve(TC) for _ in range(3)]
        pn = [carve(NH, P) for _ in range(2)]
        OB = [carve(NH, 7, 65) for _ in range(2)]
        nmx = [carve(NH, 8) for _ in range(2)]
        small = carve(16, 32)
        psm = carve(132)
        imp = [carve(NSEL) for _ in range(2)]
        masks_in = carve(NMASK, at=PROB)
        yrow = [carve(GW) for _ in range(2)]
        qmask = carve(P)[0:NSEL, :].bitcast(BF16).rearrange("p (a b) -> p a b", a=2)
        HALF = KD // 2 * D
        w_raw = [carve(KD // 2, D, at=ARENA - HALF), carve(KD // 2, D, at=WEIGHTS)]
        w_low = [carve_parts(KD // 2, D, at=ARENA - HALF), carve_parts(KD // 2, D, at=WEIGHTS)]
        xrow = [carve(D, at=WEIGHTS + (4 + n) * D) for n in range(2)]
        rrow = [carve(D, at=WEIGHTS + (6 + n) * D) for n in range(2)]
        w_high = carve_parts(KD, D, at=WEIGHTS + 8 * D)
        y_high = [carve_parts(KD, P, at=WEIGHTS + (16 + n) * D) for n in range(2)]
        top[0] = TEMP
        ln_g, ln_b = carve(D), carve(D)
        bst = [carve(16) for _ in range(2)]
        top[0] = WEIGHTS + 2 * WE
        AFTER_WX = top[0]
        x1T = [carve(KD, P) for _ in range(2)]
        rw = carve(KD, NE)
        lgt = carve(NT, NE)
        aff = carve(NT, NE)
        assert top[0] <= ARENA - KD // 2 * D
        top[0] = WEIGHTS
        rt = [carve(NT, NE) for _ in range(11)]
        chosen_both = carve(NT, NE, dtype=BF16)
        r4 = [carve(NT, 4) for _ in range(8)]
        r1 = [carve(NT) for _ in range(8)]
        cnt16 = carve(3, NE)
        cmp256 = carve(NE, NE)
        tb = [carve(64, NE) for _ in range(3)]
        tb1 = [carve(64) for _ in range(3)]
        rbias = carve(NE)
        zero_i = ctx.enter_context(nc.sbuf_tensor("zero_i", [P, NB + 1], I32))
        assert top[0] <= WEIGHTS + WE
        top[0] = WEIGHTS
        wx = carve(2, WE)
        top[0] = AFTER_WX
        xg = [carve(D) for _ in range(2)]
        xgT = [carve(KD, P) for _ in range(2)]
        hrow = [carve(DE) for _ in range(2)]
        hTm = [carve(4, P) for _ in range(2)]
        yrw = [carve(D) for _ in range(2)]
        idx = [ctx.enter_context(nc.sbuf_tensor(f"idx{u}", [P, 1], I32)) for u in range(2)]
        ln2_g, ln2_b = carve(D), carve(D)
        top[0] = WEIGHTS
        ya = [carve(D) for _ in range(R6)]
        yb = [carve(D) for _ in range(R6)]
        fin = [carve(D) for _ in range(R6)]
        b6 = [carve(16) for _ in range(R6)]

        share = lambda i: small[:, 12:16, 8 * (i % 2):8 * (i % 2) + 1 + n_slc[i] + n_win[i]]
        bank = [ctx.enter_context(nc.psum_tensor(f"bank{n}", [P, 512], F32)) for n in range(8)]
        C = lambda at, n: consts[:, at:at + n]
        ident = C(C_ID, P)

        for n in ("const_in", "chan_in", "mask_ready", "tm_in", "cs_in", "tile_made", "tile_out", "zeroed",
                  "stage_free", "cpad_free", "rope_made", "sp_made", "free6", "free7", "conv_made", "pool_d",
                  "cent", "squared", "std", "zed", "dve_step", "w_in0", "w_in1", "xa_in0", "xa_in1", "xb_in0",
                  "xb_in1", "xr_in0", "xr_in1", "g_in0", "g_in1", "ysto0", "ysto1", "idx0", "idx1", "ya_in0",
                  "ya_in1", "ya_in2", "ya_in3", "out60", "out61", "out62", "out63", "w6", "r6", "c6", "p6",
                  "mk_in", "yb_done", "cw0_in", "cw_in", "k_high", "k_low", "shifted", "ch_made", "ch_out",
                  "cc_made", "cc_out", "s_made", "max_made", "prob_made", "t_made", "pt_made", "o_made",
                  "o_out", "al_made", "po_step", "mk_made", "mkT_made", "mask_rows", "d_made", "f_made",
                  "y_made", "yT_made", "yT_out", "cd_step", "wo_in0", "wo_in1", "wh_made", "wl_made",
                  "yh_made", "yl_made", "ln_in", "rw_in", "mix_made", "mix_used", "sq_in", "sq_out",
                  "norm_made", "x1_made", "x1_stored", "xt_made", "xt_out", "lg_made", "lg_out", "route_in",
                  "aff_made", "oh_made", "cum_made", "dest_made", "zero_made", "rows_zero", "slot_zero",
                  "slot_stored", "tab_made", "we_in", "idx_in", "gx_made", "gx_out", "gu_made", "act_made",
                  "h_made", "ht_made", "ht_out", "ht_outa", "dn_outa", "dn_outd", "blk_done", "l2_in",
                  "s6_in", "s6_out", "fin6", "n6", "stats6"):
            sem(n)
        S = sem_

        block = ctx.enter_context(nc.Block())

        @block.sync
        def _(sp):
            sp.dma_start(chan, a["chan"]).then_inc(S["chan_in"], 16)
            with sp.Fori(0, NCH // 2) as cc:
                for u in range(2):
                    c = cc * 2 + u
                    sp.wait_ge(S["tile_made"], MJ * c + 1)
                    for half, name in enumerate(("xa", "xb")):
                        n = KD // 2 * TC
                        sp.dma_start(xT[u][:, half * KD // 2:(half + 1) * KD // 2, :],
                                     a["xT"][bass.ds(c, 1), :, half * n:(half + 1) * n].rearrange("a p n -> (a p) n")
                                     ).then_inc(S[f"{name}_in{u}"], 16)
                    sp.wait_ge(S["rope_made"], 3 * c + 1)
                    sp.dma_start(cs[:, :, :], a["cs"][bass.ds(c, 1), :, :].rearrange("a p n -> (a p) n")
                                 ).then_inc(S["cs_in"], 16)
                    for m in range(NM):
                        before = MJ * c + m - 1 if m >= 2 else MJ * c + m - 3
                        sp.wait_ge(S["tile_made"], before + MJ + 1)
                        sp.dma_start(wt[m % 2][:, :, :], a["w_in"][m]).then_inc(S[f"w_in{m % 2}"], 16)
            sp.wait_ge(S["tile_made"], MJ * (NCH - 1) + MJ + 1)
            sp.dma_start(w1[0][:, :, :], a["cmp_w1"][0]).then_inc(S["cw0_in"], 16)
            sp.wait_ge(S["tile_made"], MJ * NCH + MJ + 1)
            sp.dma_start(w2[:, :, :, :], a["cmp_w2"]).then_inc(S["cw_in"], 16)
            sp.dma_start(pe2[:, :, :], a["cmp_pe"]).then_inc(S["cw_in"], 16)
            sp.wait_ge(S["yb_done"], 2 * NCH)
            sp.dma_start(w1[1][:, :, :], a["cmp_w1"][1]).then_inc(S["cw_in"], 16)
            sp.dma_start(masks_in, a["masks"]).then_inc(S["mk_in"], 16)
            sp.wait_ge(S["ch_made"], 4)
            sp.dma_start(w_raw[0][:, :, :], a["w_out"][0]).then_inc(S["wo_in0"], 16)
            sp.wait_ge(S["s_made"], len(units))
            sp.dma_start(w_raw[1][:, :, :], a["w_out"][1]).then_inc(S["wo_in1"], 16)
            def row(t):
                sp.dma_start(xrow[t % 2], a["x"][t * P:(t + 1) * P, :]).then_inc(S[f"xr_in{t % 2}"], 16)

            row(0)
            row(1)
            sp.dma_start(ln_g, a["ln1_g"][None, :].to_broadcast((P, D))).then_inc(S["ln_in"], 16)
            sp.dma_start(ln_b, a["ln1_b"][None, :].to_broadcast((P, D))).then_inc(S["ln_in"], 16)
            sp.wait_ge(S["yT_out"], NT)
            sp.dma_start(rw[:, :, :], a["router_w"]).then_inc(S["rw_in"], 16)
            for t in range(2, NT):
                sp.wait_ge(S["mix_used"], 2 * (t - 1))
                row(t)
            sp.wait_ge(S["zero_made"], 1)
            sp.dma_start(slot_dram.rearrange("(p n) o -> p (n o)", p=P), zero_i[:, :]).then_inc(S["slot_zero"], 16)
            sp.wait_ge(S["x1_made"], NT)
            sp.dma_start(rbias, a["router_bias"][None, :].to_broadcast((P, NE))).then_inc(S["route_in"], 16)
            for n in range(3):
                sp.dma_start(wx[:, 1, n * KD * DE:(n + 1) * KD * DE], a["w_exp"][0, n]).then_inc(S["we_in"], 16)
            sp.wait_ge(S["tab_made"], 1)
            sp.dma_start(ln2_g, a["ln2_g"][None, :].to_broadcast((P, D))).then_inc(S["l2_in"], 16)
            sp.dma_start(ln2_b, a["ln2_b"][None, :].to_broadcast((P, D))).then_inc(S["l2_in"], 16)
            for e in range(1, NE):
                sp.wait_ge(S["we_in"], 48 * e)
                if e >= 2:
                    done = sp.value_load(tables[0:1, 1, e - 2:e - 1], min_val=0, max_val=NB)
                    sp.wait_ge(S["blk_done"], done + 1)
                for n in range(3):
                    sp.dma_start(wx[:, 1 - e % 2, n * KD * DE:(n + 1) * KD * DE], a["w_exp"][e, n]
                                 ).then_inc(S["we_in"], 16)
            for u in range(R6):
                sp.sem_inc(S[f"out6{u}"], 16)
            with sp.Fori(0, NT // R6) as tt:
                for u in range(R6):
                    t = tt * R6 + u
                    sp.wait_ge(S["p6"], t + 1)
                    sp.dma_start(out[bass.ds(t * P, P), :], fin[u]).then_inc(S[f"out6{u}"], 16)
            for u in range(R6):
                sp.wait_ge(S[f"out6{u}"], 16 * (NT // R6) + 16)

        @block.tensor
        def _(pe):
            pe.sem_inc(S["tile_made"], MJ + 1)

            def special(b, free, value, out_, lhs_rhs):
                pe.wait_ge(S[free], value)
                for n, (l, r) in enumerate(lhs_rhs):
                    mm = pe.matmul(out_, l, r, start=(n == 0), stop=(n == len(lhs_rhs) - 1))
                mm.then_inc(S["sp_made"], 1)

            with pe.Fori(0, NCH // 2) as cc:
                for u in range(2):
                    c = cc * 2 + u
                    cols = bass.ds(c * TC, TC)
                    for j in range(MJ):
                        pe.wait_ge(S["tile_out"], MJ * c + j + 1)
                        ps = bank[j % NBANK]
                        if j < NM:
                            pe.wait_ge(S[f"w_in{j % 2}"], 8 * NM * c + 16 * (j // 2) + 16)
                            for k in range(KD):
                                if j == 0 and k % (KD // 2) == 0:
                                    pe.wait_ge(S[f"{'xb' if k else 'xa'}_in{u}"], 16 * cc + 16)
                                mm = pe.matmul(ps[:], wt[j % 2][:, k, :], xT[u][:, k, :],
                                               start=(k == 0), stop=(k == KD - 1))
                        else:
                            for s in range(2):
                                tok = (j - NM) * 2 + s
                                for k in range(KD):
                                    mm = pe.matmul(ps[:, s * NTM:(s + 1) * NTM], xT[u][:, k, tok * P:(tok + 1) * P],
                                                   w_tm[:, k, :], start=(k == 0), stop=(k == KD - 1))
                        mm.then_inc(S["tile_made"], 1)
                        if j == M_C0:
                            pe.wait_ge(S["const_in"], 16)
                            pe.wait_ge(S["tile_out"], MJ * c + NBANK + M_KS + 1)
                            special(6, "free6", 4 * c + 1, bank[6][:], [(C(C_PERM, P), stage[0])])
                        if j == M_C1:
                            pe.wait_ge(S["tile_out"], MJ * c + NBANK + M_Q0 + 1)
                            special(7, "free7", 3 * c + 1, bank[7][:], [(C(C_PERM, P), QR[:, 0, cols])])
                        if j == M_AC0:
                            pe.wait_ge(S["tile_out"], MJ * c + NBANK + M_Q1 + 1)
                            special(6, "free6", 4 * c + 2, bank[6][:], [(C(C_PERM, P), QR[:, 1, cols])])
                        if j == M_AH0:
                            pe.wait_ge(S["conv_made"], 2 * c + 2)
                            special(7, "free7", 3 * c + 2, bank[7][:],
                                    [(C(C_MEAN, P), yT[:, 2 + n, cols]) for n in range(2)])
                        if j == M_AB0:
                            pe.wait_ge(S["tm_in"], 32)
                            for n in range(2):
                                pe.wait_ge(S["pool_d"], 2 * c + n + 1)
                                special(6 + n, f"free{6 + n}", (4 if n == 0 else 3) * c + 3, bank[6 + n][:],
                                        [(pool_w[:, n, :], pd[n])])
                        if j == M_AH1:
                            pe.wait_ge(S["squared"], 2 * c + 2)
                            special(6, "free6", 4 * c + 4, bank[6][:], [(C(C_MEAN, P), t) for t in (t1, t2)])

            pe.wait_ge(S["cw0_in"], 16)
            pe.wait_ge(S["tile_out"], MJ * NCH + NBANK)
            for n, src in enumerate((VC2, KC2)):
                pe.wait_ge(S["shifted"], 2 + n)
                if n:
                    pe.wait_ge(S["free6"], 4 * NCH + 1)
                    pe.wait_ge(S["free7"], 3 * NCH + 1)
                for m in range(2):
                    ps = bank[2 * n + m]
                    for s in range(16):
                        pe.matmul(ps[:, 0:NCMP], w1[n][:, s, m * P:(m + 1) * P],
                                  src[:, 2 * s:2 * s + 16 * (NCMP - 1) + 1:16], start=(s == 0), stop=(s == 15))
                for m in range(2):
                    pe.wait_ge(S["cw_in"], 48)
                    for s in range(16):
                        mm = pe.matmul(bank[4 + 2 * n + m][:, 0:1], w1[n][:, s, m * P:(m + 1) * P],
                                       pe2[:, n, s:s + 1], start=(s == 0), stop=(s == 15))
                    mm.then_inc(S["ch_made"], 1)
            pe.wait_ge(S["ch_out"], 4)
            for m in range(2):
                mm = pe.matmul(bank[0][:, 0:NCMP], w2[:, 1, m, :], hT[1][:, m, 0:NCMP], start=(m == 0), stop=(m == 1))
            mm.then_inc(S["cc_made"], 1)
            for m in range(2):
                mm = pe.matmul(bank[1][0:NCMP, 0:HD], hT[0][:, m, 0:NCMP], w2[:, 0, m, 0:HD],
                               start=(m == 0), stop=(m == 1))
            mm.then_inc(S["cc_made"], 1)
            pe.wait_ge(S["cc_out"], 6)
            pe.wait_ge(S["k_low"], 2)
            pe.wait_ge(S["mask_ready"], 1)

            def scores(n):
                un = units[n]
                ps = bank[n % 3]
                if n >= 3:
                    pe.wait_ge(S["prob_made"], n - 2)
                if un[0] == "cmp":
                    i = un[1]
                    pe.matmul(ps[:].rearrange("p (h n) -> p h n", h=NH)[:, :, 0:NCMP], masks[:, K_ID:K_ID + P],
                              masks[:, None, K_CMP + P - 8 * i:K_CMP + P - 8 * i + NCMP].to_broadcast((P, NH, NCMP)),
                              start=True, stop=True)
                    for m in range(2):
                        mm = pe.matmul(ps[:, 2 * m * P:2 * (m + 1) * P].rearrange("p (h n) -> p h n", h=2)[:, :, 0:NCMP],
                                       QR[:, m, i * P:(i + 1) * P], kct[:, :, 0:NCMP],
                                       start=False, stop=True, skip_group_check=True)
                    mm.then_inc(S["s_made"], 1)
                    return
                br, i, h0, g, k0, t, slot, mask = un
                n_ = t * P
                if br == "slc" and i >= 8 and n == first_slc[i]:
                    pe.wait_ge(S["mask_rows"], i - 7)
                high, low = (KSH, KSL) if br == "slc" else (KWH, KWL)
                chosen = br == "slc" and i >= 8
                if mask:
                    m = masks[:, K_TRI + 512 - n_:K_TRI + 512] if mask == "tri" else masks[:, K_WIN:K_WIN + n_]
                    pe.matmul(ps[:, 0:g * n_].rearrange("p (g n) -> p g n", g=g), masks[:, K_ID:K_ID + P],
                              m[:, None, :].to_broadcast((P, g, n_)), start=True, stop=True)
                if chosen:
                    blocks = masks[0:NSEL, K_ID + 2 * k0:K_ID + 2 * (k0 + t)]
                    for q in range(g):
                        pe.matmul(ps[:, q * n_:(q + 1) * n_].rearrange("p (b k) -> p b k", k=64), qmask[:, i % 2, :],
                                  blocks[:, :, None].to_broadcast((NSEL, 2 * t, 64)), start=(not mask), stop=True,
                                  skip_group_check=bool(mask))
                for q in range(g):
                    for keys in (high, low):
                        mm = pe.matmul(ps[:, q * n_:(q + 1) * n_], QS[:, h0 + q, i * P:(i + 1) * P],
                                       keys[:, k0 * P:k0 * P + n_],
                                       start=(keys is high and not mask and not chosen), stop=True,
                                       skip_group_check=True)
                mm.then_inc(S["s_made"], 1)

            def turn(n):
                un = units[n]
                pe.wait_ge(S["prob_made"], n + 1)
                if n >= 2:
                    pe.wait_ge(S["pt_made"], n - 1)
                ps = bank[3 + n % 2]
                if un[0] == "cmp":
                    for h in range(NH):
                        mm = pe.transpose(ps[0:NCMP, h * P:(h + 1) * P], pn[un[1] % 2][:, h, 0:NCMP], ident)
                else:
                    for k in range(un[3] * un[5]):
                        mm = pe.transpose(ps[:, k * P:(k + 1) * P], prob[n % 4][:, k * P:(k + 1) * P], ident)
                mm.then_inc(S["t_made"], 1)

            def values(n):
                un = units[n]
                pe.wait_ge(S["pt_made"], n + 1)
                if n >= 2:
                    pe.wait_ge(S["o_out"], n - 1)
                ps = bank[5 + n % 2]
                pt = probT[n % 3]
                if un[0] == "cmp":
                    for h in range(NH):
                        mm = pe.matmul(ps[:, h * 65:(h + 1) * 65], pt[0:NCMP, h * P:(h + 1) * P], vct[0:NCMP, :],
                                       start=True, stop=True)
                else:
                    br, i, h0, g, k0, t, slot, mask = un
                    v = VS if br == "slc" else VW
                    for q in range(g):
                        for k in range(t):
                            mm = pe.matmul(ps[:, q * 65:(q + 1) * 65], pt[:, (q * t + k) * P:(q * t + k + 1) * P],
                                           v[:, k0 + k, :], start=(k == 0), stop=(k == t - 1))
                mm.then_inc(S["o_made"], 1)

            rows, turned = [0], [0]

            def turn_mask(i):
                pe.wait_ge(S["mk_made"], i - 7)
                pe.wait_ge(S["yT_out"], rows[0])
                pe.transpose(bank[7][0:NSEL, 0:P], imp[0], ident).then_inc(S["mkT_made"], 1)
                turned[0] += 1

            def turn_rows(i):
                pe.wait_ge(S["y_made"], i + 1)
                if turned[0]:
                    pe.wait_ge(S["mask_rows"], turned[0])
                if i:
                    pe.wait_ge(S["yT_out"], i)
                rows[0] += 1
                for m in range(2):
                    mm = pe.transpose(bank[7][:, 256 + m * P:256 + (m + 1) * P], yrow[i % 2][:, m * P:(m + 1) * P], ident)
                mm.then_inc(S["yT_made"], 1)

            N = len(units)
            for n in range(-2, N + LATE):
                for i in range(NT):
                    if i >= 8 and n + 2 == first_slc[i]:
                        turn_mask(i)
                    if n - LATE == last_of[i] and i < NT - 1:
                        turn_rows(i)
                if 0 <= n + 2 < N:
                    scores(n + 2)
                if 0 <= n < N:
                    turn(n)
                if 0 <= n - 1 < N:
                    values(n - 1)

            pe.wait_ge(S["prob_made"], N)
            pe.wait_ge(S["pt_made"], N)

            def mix(t):
                pe.wait_ge(S["yl_made"], t + 1)
                if t >= 2:
                    pe.wait_ge(S["mix_used"], 2 * (t - 1))
                for m in range(2):
                    c_ = slice(m * 512, (m + 1) * 512)
                    for k in range(KD):
                        if t == 0 and m == 0:
                            pe.wait_ge(S["wl_made"], k + 1)
                        high = y_high[t % 2][:, k, :]
                        terms = ((high, w_high[:, k, c_]), (high, w_low[k // 4][:, k % 4, c_]),
                                 (yTl[:, k, t * P:(t + 1) * P], w_high[:, k, c_]))
                        for n, (y, w_) in enumerate(terms):
                            mm = pe.matmul(bank[2 * (t % 2) + m][:], y, w_, start=(k == 0 and n == 0),
                                           stop=(k == KD - 1 and n == 2))
                mm.then_inc(S["mix_made"], 1)

            def turn_x1(t):
                pe.wait_ge(S["x1_made"], t + 1)
                if t >= 1:
                    pe.wait_ge(S["xt_out"], 2 * t)
                for k in range(KD):
                    mm = pe.transpose(bank[4 + k // 4][:, (k % 4) * P:(k % 4 + 1) * P], x1t(t)[:, k, :], ident)
                mm.then_inc(S["xt_made"], 1)

            def logits(t):
                pe.wait_ge(S["xt_out"], 2 * (t + 1))
                if t >= 1:
                    pe.wait_ge(S["lg_out"], t)
                for k in range(KD):
                    mm = pe.matmul(bank[6][:, 0:NE], x1T[t % 2][:, k, :], rw[:, k, :], start=(k == 0), stop=(k == KD - 1))
                mm.then_inc(S["lg_made"], 1)

            for t in range(NT + 2):
                if t < NT:
                    mix(t)
                if t == 0:
                    turn_rows(NT - 1)
                if 1 <= t <= NT:
                    turn_x1(t - 1)
                if t == 2:
                    pe.wait_ge(S["rw_in"], 16)
                if t >= 2:
                    logits(t - 2)

            pe.wait_ge(S["oh_made"], 1)
            ones, below = masks[:, K_ONE:K_ONE + P], masks[:, K_ONE + P:K_ONE + 2 * P]
            before = bank[0][:, 0:NT * NE].rearrange("p (t e) -> p t e", e=NE)
            pe.matmul(before, below, chosen_both, start=True, stop=True)
            for t in range(NT - 1):
                pe.matmul(before[:, t + 1:, :], ones, chosen_both[:, t:t + 1, :].to_broadcast((P, NT - 1 - t, NE)),
                          start=False, stop=True, skip_group_check=True)
            for t in range(NT):
                mm = pe.matmul(bank[1][:, 0:NE], ones, chosen_both[:, t, :], start=(t == 0), stop=(t == NT - 1))
            mm.then_inc(S["cum_made"], 1)

            pe.wait_ge(S["tab_made"], 1)

            def turn_in(b, u, pair, m):
                pe.wait_ge(S[f"g_in{u}"], 16 * pair + 16)
                pe.wait_ge(S["gx_out"], 2 * b + 1)
                for k in range(4 * m, 4 * m + 4):
                    mm = pe.transpose(bank[m][:, (k % 4) * P:(k % 4 + 1) * P], xg[u][:, k * P:(k + 1) * P], ident)
                mm.then_inc(S["gx_made"], 1)

            pe.sem_inc(S["blk_done"], 1)
            pe.sem_inc(S["ht_made"], 4)
            for m in range(2):
                turn_in(0, 0, 0, m)
            pairs = pe.value_load(tables[0:1, 1, NE:NE + 1], min_val=1, max_val=NB // 2)
            with pe.Fori(0, NB // 2) as bb, pe.If(bb < pairs):
                for u in range(2):
                    b = bb * 2 + u
                    e = pe.value_load(tables[0:1, 0, bass.ds(b, 1)], min_val=0, max_val=NE - 1)
                    half = pe.value_load(tables[0:1, 2, bass.ds(b, 1)], min_val=0, max_val=1)
                    pe.wait_ge(S["we_in"], e * 48 + 48)
                    pe.wait_ge(S["gx_out"], 2 * b + 3)
                    pe.wait_ge(S["h_made"], 2 * b + 1)
                    for m in range(2):
                        for k in range(KD):
                            at = m * KD * DE + k * DE
                            mm = pe.matmul(bank[2 + m][:], xgT[u][:, k, :],
                                           wx[:, bass.ds(half, 1), at:at + DE].rearrange("p a n -> p (a n)"),
                                           start=(k == 0), stop=(k == KD - 1))
                        mm.then_inc(S["gu_made"], 1)
                    turn_in(b + 1, 1 - u, bb + u, 0)
                    for m, free in enumerate(("ht_out", "ht_outa")):
                        pe.wait_ge(S["h_made"], 2 * b + m + 2)
                        pe.wait_ge(S[free], b + 1)
                        for k in range(2):
                            at = (2 * m + k) * P
                            mm = pe.transpose(bank[4 + 3 * m][:, k * P:(k + 1) * P], hrow[u][:, at:at + P], ident)
                        mm.then_inc(S["ht_made"], 1)
                    turn_in(b + 1, 1 - u, bb + u, 1)
                    pe.wait_ge(S["dn_outa"], b + 1)
                    pe.wait_ge(S["dn_outd"], b + 1)
                    for k in range(4):
                        if k % 2 == 0:
                            pe.wait_ge(S["ht_outa" if k else "ht_out"], b + 2)
                        for m in range(2):
                            at = 2 * KD * DE + k * D + m * 512
                            mm = pe.matmul(bank[5 + m][:], hTm[u][:, k, :],
                                           wx[:, bass.ds(half, 1), at:at + 512].rearrange("p a n -> p (a n)"),
                                           start=(k == 0), stop=(k == 3))
                    mm.then_inc(S["blk_done"], 1)

        @block.scalar
        def _(act):
            act.sem_inc(S["tile_out"], NBANK)
            act.wait_ge(S["chan_in"], 16)
            act.wait_ge(S["zeroed"], 1)

            def apart():
                act.wait_ge(S["zeroed"], 1)

            with act.Fori(0, NCH // 2) as cc:
                for u in range(2):
                    c = cc * 2 + u
                    cols = bass.ds(c * TC, TC)
                    slot = {M_BG0: (0, 6), M_BV0: (1, 6), M_BG1: (2, 7), M_BV1: (3, 5), M_KS: (0, 8),
                            M_AC0: (1, 8), M_AH0: (2, 9), M_AB0: (3, 9), M_AC1: (0, 10), M_AH1: (1, 11), M_AB1: (2, 11)}

                    def copy_out(j):
                        ps = bank[j % NBANK]
                        if j not in slot:
                            apart()
                        act.wait_ge(S["tile_made"], MJ * c + MJ + 1 + j + 1)
                        if j in slot:
                            s, v = slot[j]
                            act.wait_ge(S["stage_free"], 7 * c + v)
                            f = ACT.Sigmoid if j in (M_BG0, M_BG1) else ACT.Copy
                            act.activation(stage[s], ps[:], f).then_inc(S["tile_out"], 1)
                        elif j == M_KC:
                            act.activation(KC2[:, cols], ps[:], ACT.Copy).then_inc(S["tile_out"], 1)
                        elif j in (M_Q0, M_Q1):
                            act.activation(QR[:, j - M_Q0, cols], ps[:], ACT.Copy, scale=0.125
                                           ).then_inc(S["tile_out"], 1)
                        elif j in (M_C0, M_C1):
                            n = j - M_C0
                            act.wait_ge(S["cpad_free"], 2 * c + n + 1)
                            act.activation(cpad[n][:, HC:HC + TC], ps[:], ACT.Copy).then_inc(S["tile_out"], 1)
                        else:
                            v = ps[:, 0:2 * NTM].rearrange("p (s n) -> p s n", s=2)
                            t0 = c * 4 + (j - NM) * 2
                            act.activation(VS[:, bass.ds(t0, 2), 0:64], v[:, :, 0:64], ACT.Copy)
                            act.activation(VW[:, bass.ds(t0, 2), 0:64], v[:, :, 64:128], ACT.Copy)
                            act.activation(gates[:, bass.ds(t0, 2), :], v[:, :, 128:140], ACT.Sigmoid
                                           ).then_inc(S["tile_out"], 1)

                    for j in range(M_AB0 + 1):
                        copy_out(j)
                    for n, t in enumerate((t1, t2)):
                        apart()
                        act.wait_ge(S["cent"], 2 * c + n + 1)
                        act.activation(t, yT[:, 2 + n, cols], ACT.Square).then_inc(S["squared"], 1)
                    for n in range(2):
                        apart()
                        act.wait_ge(S["sp_made"], 7 * c + 5 + n)
                        act.activation(yT[:, 4 + n, cols], bank[6 + n][:], ACT.Copy,
                                       scale=chan[:, CH_PS + n:CH_PS + n + 1]).then_inc(S[f"free{6 + n}"], 1)
                    for j in (M_AC1, M_AH1, M_AB1):
                        copy_out(j)
                    act.wait_ge(S["sp_made"], 7 * c + 7)
                    act.activation(sd, bank[6][:], ACT.Sqrt, bias=chan[:, CH_EPS:CH_EPS + 1]).then_inc(S["std"], 1)
                    act.wait_ge(S["std"], c + 1)
                    act.sem_inc(S["free6"], 1)
                    copy_out(NM)
                    copy_out(NM + 1)
                    for n in range(2):
                        apart()
                        act.wait_ge(S["zed"], 2 * c + n + 1)
                        act.activation(yT[:, 2 + n, cols], yT[:, 2 + n, cols], ACT.Silu,
                                       scale=chan[:, CH_G + n:CH_G + n + 1],
                                       bias=chan[:, CH_BE + n:CH_BE + n + 1]).then_inc(S["yb_done"], 1)
            for n in range(2):
                if n:
                    for high, keys in ((KSH, KS), (KWH, KW)):
                        act.activation(high, keys, ACT.Copy).then_inc(S["k_high"], 1)
                for m in range(2):
                    act.wait_ge(S["ch_made"], 2 * n + m + 1)
                    act.activation(hbias[:, 2 * n + m:2 * n + m + 1], bank[4 + 2 * n + m][:, 0:1], ACT.Copy
                                   ).then_inc(S["cd_step"], 1)
                    act.wait_ge(S["cd_step"], 2 * n + m + 1)
                    act.activation(hT[n][:, m, 0:NCMP], bank[2 * n + m][:, 0:NCMP], ACT.Silu,
                                   bias=hbias[:, 2 * n + m:2 * n + m + 1]).then_inc(S["ch_out"], 1)
            act.wait_ge(S["cc_made"], 2)
            for n in range(2):
                r = slice(64 * n, 64 * n + 64)
                act.activation(kct[r, n, 0:NCMP], bank[0][r, 0:NCMP], ACT.Copy).then_inc(S["cc_out"], 1)
            act.activation(vct[0:NCMP, 0:HD], bank[1][0:NCMP, 0:HD], ACT.Copy).then_inc(S["cc_out"], 1)

            def exps(n):
                un = units[n]
                act.wait_ge(S["max_made"], n + 1)
                if n >= 4:
                    act.wait_ge(S["t_made"], n - 3)
                if un[0] == "cmp":
                    i = un[1]
                    if i >= 2:
                        act.wait_ge(S["t_made"], cmp_at[i - 2] + 1)
                    if i >= 10:
                        act.wait_ge(S["mk_made"], i - 9)
                    for h in range(NH):
                        e = act.activation(pn[i % 2][:, h, 0:NCMP], bank[n % 3][:, h * P:h * P + NCMP], ACT.Exp,
                                           bias=nmx[i % 2][:, h, 0:1])
                else:
                    br, i, h0, g, k0, t, slot, mask = un
                    for q in range(g):
                        r = slice(q * t * P, (q + 1) * t * P)
                        e = act.activation(prob[n % 4][:, r], bank[n % 3][:, r], ACT.Exp,
                                           bias=nmx[i % 2][:, h0 + q, slot:slot + 1])
                e.then_inc(S["prob_made"], 1)

            def outs(n):
                un = units[n]
                act.wait_ge(S["o_made"], n + 1)
                ps = bank[5 + n % 2]
                if un[0] == "cmp":
                    i = un[1]
                    if i >= 2:
                        act.wait_ge(S["y_made"], i - 1)
                    act.activation(OB[i % 2][:, :, 0, :], ps[:, 0:NH * 65].rearrange("p (h n) -> p h n", h=NH), ACT.Copy
                                   ).then_inc(S["o_out"], 1)
                else:
                    br, i, h0, g, k0, t, slot, mask = un
                    act.activation(OB[i % 2][:, h0:h0 + g, slot, :],
                                   ps[:, 0:g * 65].rearrange("p (h n) -> p h n", h=g), ACT.Copy).then_inc(S["o_out"], 1)

            def rows_turned(i):
                act.wait_ge(S["yT_made"], i + 1)
                act.activation(yT[:, 6:8, i * P:(i + 1) * P], bank[7][:, 256:512].rearrange("p (m n) -> p m n", m=2),
                               ACT.Copy).then_inc(S["yT_out"], 1)

            N = len(units)
            for n in range(-1, N + LATE):
                for i in range(NT):
                    if n - 2 == last_of[i]:
                        act.wait_ge(S["d_made"], i + 1)
                        ns = n_slc[i] + n_win[i]
                        v = small[:, 0:4, 8:8 + ns]
                        act.activation(v, v, ACT.Exp).then_inc(S["f_made"], 1)
                for i in range(NT):
                    if n - LATE == last_of[i] and i < NT - 1:
                        rows_turned(i)
                if 0 <= n + 1 < N:
                    exps(n + 1)
                if 0 <= n - 1 < N:
                    outs(n - 1)
            def high_y(t):
                act.wait_ge(S["yT_out"], t + 1)
                if t >= 2:
                    act.wait_ge(S["mix_made"], t - 1)
                act.activation(y_high[t % 2][:, :, :], yT[:, :, t * P:(t + 1) * P], ACT.Copy).then_inc(S["yh_made"], 1)

            act.wait_ge(S["o_made"], N)
            act.wait_ge(S["s_made"], N)
            high_y(0)
            for k in range(KD):
                if k % 4 == 0:
                    act.wait_ge(S[f"wo_in{k // 4}"], 16)
                act.activation(w_high[:, k, :], w_raw[k // 4][:, k % 4, :], ACT.Copy).then_inc(S["wh_made"], 1)
            high_y(1)
            rows_turned(NT - 1)
            for t in range(NT + 1):
                if 1 <= t < NT - 1:
                    high_y(t + 1)
                if t < NT:
                    act.wait_ge(S["sq_in"], t + 1)
                    act.activation(bst[t % 2][:, 14:15], bst[t % 2][:, 13:14], ACT.Sqrt,
                                   bias=chan[:, CH_EPS:CH_EPS + 1]).then_inc(S["sq_out"], 1)
                if t >= 1:
                    q = t - 1
                    act.wait_ge(S["xt_made"], q + 1)
                    if q >= 2:
                        act.wait_ge(S["lg_made"], q - 1)
                    for m in range(2):
                        act.activation(x1T[q % 2][:, 4 * m:4 * m + 4, :].rearrange("p a b -> p (a b)"), bank[4 + m][:],
                                       ACT.Copy).then_inc(S["xt_out"], 1)
                if t >= 2:
                    q = t - 2
                    act.wait_ge(S["lg_made"], q + 1)
                    act.activation(lgt[:, q, :], bank[6][:, 0:NE], ACT.Copy).then_inc(S["lg_out"], 1)
            act.wait_ge(S["lg_made"], NT)
            act.activation(lgt[:, NT - 1, :], bank[6][:, 0:NE], ACT.Copy).then_inc(S["lg_out"], 1)
            act.wait_ge(S["lg_out"], NT)
            act.activation(aff[:, :, :], lgt[:, :, :], ACT.Sigmoid).then_inc(S["aff_made"], 1)
            act.wait_ge(S["rows_zero"], 32 * (NB - NBMIN))
            act.sem_inc(S["gx_out"], 1)
            act.sem_inc(S["dn_outa"], 1)
            act.sem_inc(S["ht_outa"], 1)
            act.sem_inc(S["ysto0"], 16)
            act.sem_inc(S["ysto1"], 16)
            act.wait_ge(S["tab_made"], 1)

            def copy_in(b, u, m):
                act.wait_ge(S["gx_made"], 2 * b + m + 1)
                act.activation(xgT[u][:, 4 * m:4 * m + 4, :].rearrange("p a b -> p (a b)"), bank[m][:],
                               ACT.Copy).then_inc(S["gx_out"], 1)

            copy_in(0, 0, 0)
            copy_in(0, 0, 1)
            pairs = act.value_load(tables[0:1, 1, NE:NE + 1], min_val=1, max_val=NB // 2)
            with act.Fori(0, NB // 2) as bb, act.If(bb < pairs):
                for u in range(2):
                    b = bb * 2 + u
                    act.wait_ge(S["gu_made"], 2 * b + 1)
                    act.wait_ge(S["ht_made"], 2 * b + 2)
                    act.activation(hrow[u], bank[2][:], ACT.Silu).then_inc(S["act_made"], 1)
                    copy_in(b + 1, 1 - u, 0)
                    act.wait_ge(S["ht_made"], 2 * b + 6)
                    act.activation(hTm[u][:, 2:4, :].rearrange("p a b -> p (a b)"), bank[7][:, 0:2 * P], ACT.Copy
                                   ).then_inc(S["ht_outa"], 1)
                    copy_in(b + 1, 1 - u, 1)
                    act.wait_ge(S["blk_done"], b + 2)
                    act.wait_ge(S[f"ysto{u}"], 16 * bb + 16)
                    act.activation(yrw[u][:, 0:512], bank[5][:], ACT.Copy).then_inc(S["dn_outa"], 1)
                    act.wait_ge(S["dn_outa"], b + 2)
                    act.wait_ge(S["dn_outd"], b + 2)
                    act.dma_start(y_dram[bass.ds(b * P, P), :], yrw[u]).then_inc(S[f"ysto{u}"], 16)
            def weigh(t, tt, u):
                apart()
                act.wait_ge(S[f"ya_in{u}"], 32 * tt + 32)
                act.activation(ya[u], ya[u], ACT.Copy, scale=dest_w[:, 0, bass.ds(t, 1)]).then_inc(S["w6"], 1)

            def deviation(t, u):
                act.wait_ge(S["s6_in"], t + 1)
                act.activation(b6[u][:, 14:15], b6[u][:, 13:14], ACT.Sqrt,
                               bias=chan[:, CH_EPS:CH_EPS + 1]).then_inc(S["s6_out"], 1)

            def divide(t, u):
                act.wait_ge(S["c6"], t + 1)
                act.wait_ge(S["fin6"], t + 1)
                act.activation(fin[u], fin[u], ACT.Copy, scale=b6[u][:, 15:16]).then_inc(S["n6"], 1)

            weigh(0, 0, 0)
            weigh(1, 0, 1)
            with act.Fori(0, NT // R6 - 1) as tt:
                for u in range(R6):
                    deviation(tt * R6 + u, u)
                    weigh(tt * R6 + u + 2, tt + (u + 2) // R6, (u + 2) % R6)
                    divide(tt * R6 + u, u)
            for t in range(NT - R6, NT):
                deviation(t, t % R6)
                if t + 2 < NT:
                    weigh(t + 2, (t + 2) // R6, (t + 2) % R6)
                divide(t, t % R6)

        @block.vector
        def _(ve):
            V_STEPS = [0]

            def step(ins):
                V_STEPS[0] += 1
                ins.then_inc(S["dve_step"], 1)
                return V_STEPS[0]

            ve.sem_inc(S["stage_free"], 7)
            ve.sem_inc(S["cpad_free"], 2)
            ve.sem_inc(S["rope_made"], 1)
            ve.sem_inc(S["free6"], 1)
            ve.sem_inc(S["free7"], 1)
            for t in bpad:
                ve.memset(t[:, 0:HB], 0.0)
            for t in cpad:
                ve.memset(t[:, 0:HC], 0.0)
            for t in apad:
                ve.memset(t[:, 0:HA], 0.0)
            ve.memset(VS[:, :, 64:65], 1.0)
            ve.memset(VW[:, :, 64:65], 1.0).then_inc(S["zeroed"], 1)
            ve.wait_ge(S["chan_in"], 16)
            w = lambda at: chan[:, at:at + 1]
            PER = 88
            with ve.Fori(0, NCH // 2) as cc:
                for u in range(2):
                    c = cc * 2 + u
                    cols = bass.ds(c * TC, TC)
                    V_STEPS[0] = 0

                    def need(n):
                        ve.wait_ge(S["dve_step"], PER * c + n)

                    at = [0, 0]
                    for n in range(2):
                        ve.wait_ge(S["tile_out"], MJ * c + NBANK + 2 * n + 2)
                        ve.tensor_tensor(bpad[n][:, HB:HB + TC], stage[2 * n], stage[2 * n + 1], ALU.mult
                                         ).then_inc(S["stage_free"], 1)
                    for k in range(CK):
                        for n in range(2):
                            acc = yT[:, 2 + n, cols]
                            if k == 0:
                                ve.wait_ge(S["stage_free"], 7 * c + 8 + n)
                                ins = ve.tensor_scalar(acc, bpad[n][:, 0:TC], w(CH_B + n * CK), w(CH_BB + n),
                                                       ALU.mult, ALU.add)
                            else:
                                need(at[n])
                                ins = ve.scalar_tensor_tensor(acc, bpad[n][:, k:k + TC], w(CH_B + n * CK + k), acc,
                                                              ALU.mult, ALU.add)
                            if k < CK - 1:
                                at[n] = step(ins)
                            else:
                                ins.then_inc(S["conv_made"], 1)
                    for n in range(2):
                        step(ve.tensor_copy(bpad[n][:, 0:HB], bpad[n][:, TC:TC + HB]))

                    if u:
                        ve.wait_ge(S["rows_zero"], 32 * (NB - NBMIN))
                    ve.wait_ge(S["cs_in"], 16 * c + 16)
                    srcs = [(stage[0], bank[6], "free6"), (QR[:, 0, cols], bank[7], "free7"),
                            (QR[:, 1, cols], bank[6], "free6")]
                    for n, (src, ps, free) in enumerate(srcs):
                        ve.wait_ge(S["sp_made"], 7 * c + n + 1)
                        if n:
                            ve.wait_ge(S["rope_made"], 3 * c + n + 1)
                        x1_ = step(ve.tensor_tensor(t1, src, cs[:, 0, :], ALU.mult))
                        ve.tensor_tensor(t2, ps[:], cs[:, 1, :], ALU.mult).then_inc(S[free], 1)
                        need(x1_)
                        ve.wait_ge(S[free], {0: 4 * c + 2, 1: 3 * c + 2, 2: 4 * c + 3}[n])
                        if n == 0:
                            for m, keys in enumerate((KS, KW)):
                                r = slice(64 * m, 64 * m + 64)
                                for to in (slice(0, 64), slice(64, 128)):
                                    ins = ve.tensor_tensor(keys[to, cols], t1[r, :], t2[r, :], ALU.add)
                            ins.then_inc(S["rope_made"], 1)
                        else:
                            q = step(ve.tensor_tensor(t1, t1, t2, ALU.add))
                            need(q)
                            q = step(ve.tensor_copy(t2r, t1))
                            need(q)
                            for m in range(2):
                                r = slice(64 * m, 64 * m + 64)
                                ve.tensor_tensor(QS[64:128, 2 * n - 2 + m, cols], t1[r, :], t2r[r, :].bitcast(F32), ALU.subtract)
                                ins = ve.tensor_scalar(QS[0:64, 2 * n - 2 + m, cols], t2r[r, :].bitcast(F32), 1.0, None, ALU.mult)
                            ins.then_inc(S["rope_made"], 1)
                        if n == 0:
                            ve.wait_ge(S["rope_made"], 3 * c + 2)
                            ve.sem_inc(S["stage_free"], 1)

                    for n in range(2):
                        x = cpad[n]
                        if n == 0:
                            ve.wait_ge(S["const_in"], 16)
                        ve.wait_ge(S["tile_out"], MJ * c + NBANK + M_C0 + n + 1)
                        E = HC + TC
                        q = step(ve.tensor_tensor(s_a[:, 1:E], x[:, 1:E], x[:, 0:E - 1], ALU.add))
                        need(q)
                        if n == 0:
                            q = step(ve.tensor_tensor(s_b[64:128, 3:E], s_a[64:128, 3:E], s_a[64:128, 1:E - 2], ALU.add))
                        else:
                            q = step(ve.tensor_tensor(s_b[:, 3:E], s_a[:, 3:E], s_a[:, 1:E - 2], ALU.add))
                            need(q)
                            q = step(ve.tensor_tensor(s_a[:, 7:E], s_b[:, 7:E], s_b[:, 3:E - 4], ALU.add))
                            need(q)
                            q = step(ve.tensor_tensor(s_b[64:128, 15:E], s_a[64:128, 15:E], s_a[64:128, 7:E - 8], ALU.add))
                        need(q)
                        for lo, sm in ((0, s_a), (64, s_b)):
                            r = slice(lo, lo + 64)
                            ve.scalar_tensor_tensor(pd[n][r, 16:TC], sm[r, HC + 16:E], chan[r, CH_IW + n:CH_IW + n + 1],
                                                    x[r, HC + 16:E], ALU.mult, ALU.subtract)
                            pt = C_PT + n * NCH * 16
                            q = step(ve.tensor_tensor(pd[n][r, 0:16], sm[r, HC:HC + 16],
                                                      consts[r, bass.ds(c * 16 + pt, 16)], ALU.mult))
                            need(q)
                            ins = ve.tensor_tensor(pd[n][r, 0:16], pd[n][r, 0:16], x[r, HC:HC + 16], ALU.subtract)
                            if lo:
                                ins.then_inc(S["pool_d"], 1)
                        ve.tensor_copy(x[:, 0:HC], x[:, TC:TC + HC]).then_inc(S["cpad_free"], 1)

                    ve.wait_ge(S["sp_made"], 7 * c + 4)
                    for n in range(2):
                        ins = ve.tensor_tensor(yT[:, 2 + n, cols], yT[:, 2 + n, cols], bank[7][:], ALU.subtract)
                        ins.then_inc(S["cent"], 1)
                    ve.wait_ge(S["cent"], 2 * c + 2)
                    ve.sem_inc(S["free7"], 1)

                    for n in range(2):
                        x = apad[n]
                        ve.wait_ge(S["tile_out"], MJ * c + NBANK + M_AH0 + 3 * n + 1)
                        cst, hst, bst_ = ((1, 2, 3), (0, 1, 2))[n]
                        ve.tensor_tensor(x[:, HA:HA + TC], stage[cst], stage[hst], ALU.mult).then_inc(S["stage_free"], 1)
                        ve.wait_ge(S["stage_free"], 7 * c + 11 + 2 * n)
                        q = step(ve.tensor_scalar(s_b[:, 0:TC], x[:, 0:TC], w(CH_A + 3 * n), None, ALU.mult))
                        for k in (1, 2):
                            need(q)
                            q = step(ve.scalar_tensor_tensor(s_b[:, 0:TC], x[:, k:k + TC], w(CH_A + 3 * n + k), s_b[:, 0:TC],
                                                             ALU.mult, ALU.add))
                        q = step(ve.tensor_copy(x[:, 0:HA], x[:, TC:TC + HA]))
                        need(q)
                        ve.wait_ge(S["tile_out"], MJ * c + NBANK + M_AB0 + 3 * n + 1)
                        ve.tensor_tensor(yT[:, n, cols], s_b[:, 0:TC], stage[bst_], ALU.mult).then_inc(S["stage_free"], 1)
                        ve.wait_ge(S["stage_free"], 7 * c + 12 + 2 * n)

                    ve.wait_ge(S["std"], c + 1)
                    q = step(ve.reciprocal(sd, sd))
                    need(q)
                    for n in range(2):
                        ve.tensor_tensor(yT[:, 2 + n, cols], yT[:, 2 + n, cols], sd, ALU.mult).then_inc(S["zed"], 1)
                    ve.wait_ge(S["zed"], 2 * c + 2)
                    assert V_STEPS[0] == PER, V_STEPS[0]
            BASE = PER * NCH
            V_STEPS[0] = 0

            def need(n):
                ve.wait_ge(S["dve_step"], BASE + n)

            ve.wait_ge(S["tile_out"], MJ * NCH + NBANK)
            ve.wait_ge(S["yb_done"], 2 * NCH)
            ve.wait_ge(S["sp_made"], 7 * NCH)
            ve.tensor_copy(tok_i[:, :], C(C_TOK, NT))
            ve.wait_ge(S["mk_in"], 16)
            ve.tensor_copy(masks[:, :], masks_in).then_inc(S["mask_ready"], 1)
            step(ve.memset(psm, 0.0))
            for n, (high, keys, low) in enumerate(((KSH, KS, KSL), (KWH, KW, KWL))):
                ve.wait_ge(S["k_high"], n + 1)
                ve.tensor_tensor(low, keys, high.bitcast(F32), ALU.subtract).then_inc(S["k_low"], 1)
            ve.memset(vct[:, HD:HD + 1], 1.0).then_inc(S["cc_out"], 1)
            ve.memset(kct[64:128, 0, :], 0.0).then_inc(S["cc_out"], 1)
            ve.memset(kct[0:64, 1, :], 0.0).then_inc(S["cc_out"], 1)

            def maxes(n):
                un = units[n]
                ve.wait_ge(S["s_made"], n + 1)
                ps = bank[n % 3]
                if un[0] == "cmp":
                    ins = ve.tensor_reduce(nmx[un[1] % 2][:, :, 0:1],
                                           ps[:].rearrange("p (h n) -> p h n", h=NH)[:, :, 0:NCMP], AX.X, ALU.max, negate=True)
                else:
                    br, i, h0, g, k0, t, slot, mask = un
                    ins = ve.tensor_reduce(nmx[i % 2][:, h0:h0 + g, slot:slot + 1],
                                           ps[:, 0:g * t * P].rearrange("p (g n) -> p g n", g=g), AX.X, ALU.max, negate=True)
                ins.then_inc(S["max_made"], 1)

            def copy_turned(n):
                un = units[n]
                ve.wait_ge(S["t_made"], n + 1)
                if n >= 3:
                    ve.wait_ge(S["o_made"], n - 2)
                ps = bank[3 + n % 2]
                if un[0] == "cmp":
                    ins = ve.tensor_copy(probT[n % 3][0:NCMP, :], ps[0:NCMP, :])
                else:
                    w_ = un[3] * un[5] * P
                    ins = ve.tensor_copy(probT[n % 3][:, 0:w_], ps[:, 0:w_])
                ins.then_inc(S["pt_made"], 1)

            def sums(i):
                p_ = pn[i % 2][:, :, 0:NCMP]
                tot, inv = small[:, 0:4, 20:21], small[:, 0:4, 21:22]
                q = step(ve.tensor_reduce(tot, p_, AX.X, ALU.add))
                need(q)
                q = step(ve.reciprocal(inv, tot))
                need(q)
                q = step(ve.tensor_tensor(p_, p_, inv.to_broadcast((P, NH, NCMP)), ALU.mult))
                need(q)
                q = step(ve.tensor_reduce(psm[:, 1:1 + NCMP].rearrange("p (n o) -> p n o", o=1),
                                          p_.rearrange("p h n -> p n h"), AX.X, ALU.add))
                need(q)

            def importance(i):
                if i > 8:
                    ve.wait_ge(S["mkT_made"], i - 8)
                q = step(ve.tensor_reduce(imp[0].rearrange("p (n o) -> p n o", o=1),
                                          psm[:, 0:P].rearrange("p (j k) -> p j k", k=4), AX.X, ALU.add))
                need(q)
                q = step(ve.tensor_tensor(imp[0], imp[0], psm[:, 4:132:4], ALU.add))
                need(q)
                q = step(ve.tensor_tensor(imp[0], imp[0], C(C_KEEP + 32 - 2 * i, NSEL), ALU.mult))
                need(q)
                q = step(ve.tensor_tensor(imp[0], imp[0], C(C_ADD + 32 - 2 * i, NSEL), ALU.add))
                need(q)
                q = step(ve.memset(imp[0][:, 0:1], FORCE))
                need(q)
                m8 = small[:, 1, 22:30]
                for r in range(2):
                    src, dst = (imp[0], imp[1]) if r == 0 else (imp[1], imp[0])
                    q = step(ve.max(m8, src))
                    need(q)
                    q = step(ve.match_replace(dst, m8, src, USED))
                    need(q)
                ve.tensor_scalar(imp[0], imp[0], USED / 2, NEG, ALU.is_gt, ALU.mult).then_inc(S["mk_made"], 1)

            def rows_of_mask(i):
                ve.wait_ge(S["mkT_made"], i - 7)
                ve.tensor_copy(qmask[:, i % 2, :], bank[7][0:NSEL, 0:P]).then_inc(S["mask_rows"], 1)

            MM = small[:, 0:4, 0:2]
            LL, RR = small[:, 4:8, 0:3], small[:, 4:8, 3:6]

            def shifts(i):
                ns, nw = n_slc[i], n_win[i]
                q = step(ve.tensor_reduce(MM[:, :, 0:1], nmx[i % 2][:, :, 1:1 + ns], AX.X, ALU.min))
                q = step(ve.tensor_reduce(MM[:, :, 1:2], nmx[i % 2][:, :, 1 + ns:1 + ns + nw], AX.X, ALU.min))
                need(q)
                for m, (lo, k) in enumerate(((0, ns), (ns, nw))):
                    ins = ve.tensor_tensor(small[:, 0:4, 8 + lo:8 + lo + k], MM[:, :, m:m + 1].to_broadcast((P, NH, k)),
                                           nmx[i % 2][:, :, 1 + lo:1 + lo + k], ALU.subtract)
                    if m == 0:
                        continue
                    ins.then_inc(S["d_made"], 1)

            def weights(i):
                ns, nw = n_slc[i], n_win[i]
                k = ns + nw
                F, FL, AL, ob = small[:, 0:4, 8:8 + k], small[:, 8:12, 0:k], share(i), OB[i % 2]
                ve.wait_ge(S["f_made"], i + 1)
                ve.wait_ge(S["o_out"], last_of[i] + 1)
                if i >= 2:
                    ve.wait_ge(S["y_made"], i - 1)
                q = step(ve.tensor_tensor(FL, F, ob[:, :, 1:k + 1, 64], ALU.mult))
                need(q)
                step(ve.tensor_copy(LL[:, :, 0:1], ob[:, :, 0, 64:65]))
                step(ve.tensor_reduce(LL[:, :, 1:2], FL[:, :, 0:ns], AX.X, ALU.add))
                q = step(ve.tensor_reduce(LL[:, :, 2:3], FL[:, :, ns:k], AX.X, ALU.add))
                need(q)
                q = step(ve.reciprocal(RR, LL))
                need(q)
                q = step(ve.tensor_tensor(RR, RR, gates[:, i, :].rearrange("p (h g) -> p h g", g=3), ALU.mult))
                need(q)
                if i == 0:
                    step(ve.tensor_scalar(AL[:, :, 0:1], RR[:, :, 0:1], C(C_VALID, 1), None, ALU.mult))
                else:
                    step(ve.tensor_copy(AL[:, :, 0:1], RR[:, :, 0:1]))
                step(ve.tensor_tensor(AL[:, :, 1:1 + ns], F[:, :, 0:ns], RR[:, :, 1:2].to_broadcast((P, NH, ns)), ALU.mult))
                ve.tensor_tensor(AL[:, :, 1 + ns:1 + k], F[:, :, ns:k], RR[:, :, 2:3].to_broadcast((P, NH, nw)), ALU.mult
                                 ).then_inc(S["al_made"], 1)

            N = len(units)
            for n in range(-1, N + LATE):
                for i in range(NT):
                    if i >= 8 and n + 2 == first_slc[i]:
                        rows_of_mask(i)
                if 0 <= n + 1 < N:
                    maxes(n + 1)
                if 0 <= n < N:
                    copy_turned(n)
                for i in range(8, NT):
                    if n == cmp_at[i]:
                        sums(i)
                    if n == cmp_at[i] + 2:
                        importance(i)
                for i in range(NT):
                    if n - 2 == last_of[i]:
                        shifts(i)
                    if n - 3 == last_of[i]:
                        weights(i)

            def low_y(t):
                ve.wait_ge(S["yh_made"], t + 1)
                tile = slice(t * P, (t + 1) * P)
                ve.tensor_tensor(yTl[:, :, tile], yT[:, :, tile], y_high[t % 2][:, :, :].bitcast(F32), ALU.subtract
                                 ).then_inc(S["yl_made"], 1)

            tiled = lambda v: v.rearrange("p (a b) -> p a b", a=KD)
            low_y(0)
            for k in range(KD):
                ve.wait_ge(S["wh_made"], k + 1)
                ve.tensor_tensor(w_low[k // 4][:, k % 4, :], w_raw[k // 4][:, k % 4, :], w_high[:, k, :].bitcast(F32),
                                 ALU.subtract).then_inc(S["wl_made"], 1)
            for t in range(NT):
                if t + 1 < NT:
                    low_y(t + 1)
                u = t % 2
                r_, st = rrow[u], bst[u]
                ve.wait_ge(S["mix_made"], t + 1)
                ve.wait_ge(S[f"xr_in{u}"], 16 * (t // 2) + 16)
                for m in range(2):
                    c_ = slice(m * 512, (m + 1) * 512)
                    ve.scalar_tensor_tensor(r_[:, c_], xrow[u][:, c_], ALPHA, bank[2 * u + m][:], ALU.mult, ALU.add
                                            ).then_inc(S["mix_used"], 1)
                if t == 0:
                    ve.wait_ge(S["ln_in"], 32)
                ve.wait_ge(S["mix_used"], 2 * (t + 1))
                step(ve.bn_stats(st[:, 0:6], r_[:, 0:512]))
                q = step(ve.bn_stats(st[:, 6:12], r_[:, 512:1024]))
                need(q)
                ve.bn_aggr(st[:, 12:14], st[:, 0:12]).then_inc(S["sq_in"], 1)
                x_ = x1t(t)
                ve.wait_ge(S["sq_in"], t + 1)
                ve.scalar_tensor_tensor(x_, tiled(r_), st[:, 12:13], tiled(ln_g), ALU.subtract, ALU.mult).then_inc(S["norm_made"], 1)
                ve.wait_ge(S["sq_out"], t + 1)
                q = step(ve.reciprocal(st[:, 15:16], st[:, 14:15]))
                need(q)
                ve.wait_ge(S["norm_made"], t + 1)
                ve.scalar_tensor_tensor(x_, x_, st[:, 15:16], tiled(ln_b), ALU.mult, ALU.add).then_inc(S["x1_made"], 1)

            ve.wait_ge(S["aff_made"], 1)
            ve.wait_ge(S["route_in"], 16)

            def do(ins):
                need(step(ins))

            b16 = lambda x, n: x[:, :, None].to_broadcast((P, NT, n))
            bia = rt[1]
            do(ve.tensor_tensor(bia[:, :, :], aff[:, :, :], rbias[:, None, :].to_broadcast((P, NT, NE)), ALU.add))
            v = bia[:, :, :].rearrange("p t (g k) -> p t g k", k=4)
            vk = [v[:, :, :, k] for k in range(4)]
            do(ve.tensor_tensor(r4[0][:, :, :], vk[0], vk[1], ALU.max))
            do(ve.tensor_tensor(r4[1][:, :, :], vk[0], vk[1], ALU.min))
            do(ve.tensor_tensor(r4[2][:, :, :], vk[2], vk[3], ALU.max))
            do(ve.tensor_tensor(r4[3][:, :, :], vk[2], vk[3], ALU.min))
            do(ve.tensor_tensor(r4[4][:, :, :], r4[0][:, :, :], r4[2][:, :, :], ALU.max))
            do(ve.tensor_tensor(r4[5][:, :, :], r4[0][:, :, :], r4[2][:, :, :], ALU.min))
            do(ve.tensor_tensor(r4[6][:, :, :], r4[1][:, :, :], r4[3][:, :, :], ALU.max))
            do(ve.tensor_tensor(r4[5][:, :, :], r4[5][:, :, :], r4[6][:, :, :], ALU.max))
            do(ve.tensor_tensor(r4[7][:, :, :], r4[4][:, :, :], r4[5][:, :, :], ALU.add))

            def first_max(out_, x, order, eq, wgt, m1, m2, n):
                do(ve.tensor_reduce(m1[:, :, None], x, AX.X, ALU.max))
                do(ve.tensor_tensor(eq, x, b16(m1, n), ALU.is_equal))
                do(ve.tensor_tensor(wgt, eq, order[:, None, :].to_broadcast((P, NT, n)), ALU.mult))
                do(ve.tensor_reduce(m2[:, :, None], wgt, AX.X, ALU.max))
                do(ve.tensor_tensor(out_, wgt, b16(m2, n), ALU.is_equal))

            first_max(r4[2][:, :, :], r4[7][:, :, :], C(C_GW, 4), r4[0][:, :, :], r4[1][:, :, :], r1[0], r1[1], 4)
            do(ve.tensor_copy(rt[2][:, :, :].rearrange("p t (g k) -> p t g k", k=4),
                              r4[2][:, :, :, None].to_broadcast((P, NT, 4, 4))))
            do(ve.tensor_tensor(rt[3][:, :, :], bia[:, :, :], rt[2][:, :, :], ALU.mult))
            do(ve.tensor_scalar(rt[4][:, :, :], rt[2][:, :, :], -NEG, NEG, ALU.mult, ALU.add))
            do(ve.tensor_tensor(rt[5][:, :, :], rt[3][:, :, :], rt[4][:, :, :], ALU.add))
            for c in range(2):
                oh = rt[8 + c][:, :, :]
                first_max(oh, rt[5][:, :, :], C(C_EW, NE), rt[6][:, :, :], rt[7][:, :, :], r1[2], r1[3], NE)
                do(ve.scalar_tensor_tensor(rt[5][:, :, :], oh, 2 * NEG, rt[5][:, :, :], ALU.mult, ALU.add))
                do(ve.tensor_tensor(rt[6][:, :, :], aff[:, :, :], oh, ALU.mult))
                do(ve.tensor_reduce(r1[4 + c][:, :, None], rt[6][:, :, :], AX.X, ALU.add))
            ve.tensor_tensor(chosen_both, rt[8][:, :, :], rt[9][:, :, :], ALU.add).then_inc(S["oh_made"], 1)
            do(ve.tensor_tensor(r1[2], r1[4], r1[5], ALU.add))
            do(ve.reciprocal(r1[3], r1[2]))
            for c in range(2):
                do(ve.tensor_tensor(dest_w[:, c, :], r1[4 + c], r1[3], ALU.mult))
            ve.wait_ge(S["cum_made"], 1)
            nblk, sb_, incl = (cnt16[:, k, :] for k in range(3))
            do(ve.tensor_tensor(cmp256[:, :, :], bank[1][:, 0:NE, None].to_broadcast((P, NE, NE)),
                                C(C_K128, NE)[:, None, :].to_broadcast((P, NE, NE)), ALU.is_gt))
            do(ve.tensor_reduce(nblk[:, :, None], cmp256[:, :, :], AX.X, ALU.add))
            do(ve.tensor_tensor(cmp256[:, :, :], C(C_LT, 256).rearrange("p (a b) -> p a b", a=NE),
                                nblk[:, None, :].to_broadcast((P, NE, NE)), ALU.mult))
            do(ve.tensor_reduce(sb_[:, :, None], cmp256[:, :, :], AX.X, ALU.add))
            do(ve.tensor_tensor(incl, sb_, nblk, ALU.add))
            do(ve.scalar_tensor_tensor(rt[10][:, :, :], sb_[:, None, :].to_broadcast((P, NT, NE)), float(P),
                                       bank[0][:, 0:NT * NE].rearrange("p (t e) -> p t e", e=NE), ALU.mult, ALU.add))
            for c in range(2):
                do(ve.tensor_tensor(rt[6][:, :, :], rt[8 + c][:, :, :], rt[10][:, :, :], ALU.mult))
                do(ve.tensor_reduce(r1[6 + c][:, :, None], rt[6][:, :, :], AX.X, ALU.add))
                do(ve.tensor_copy(dest_i[:, c, :], r1[6 + c]))
            ve.sem_inc(S["dest_made"], 1)
            do(ve.tensor_tensor(tb[0][0:1, :, :], incl[0:1, None, :].to_broadcast((1, 64, NE)),
                                consts[0:1, C_BIDX:C_BIDX + 64, None].to_broadcast((1, 64, NE)), ALU.is_le))
            do(ve.tensor_reduce(tb1[0][0:1, :, None], tb[0][0:1, :, :], AX.X, ALU.add))
            do(ve.tensor_scalar(tb1[0][0:1, :], tb1[0][0:1, :], float(NE - 1), None, ALU.min))
            do(ve.tensor_copy(tables[0:1, 0, :], tb1[0][0:1, :]))
            do(ve.tensor_copy(tables[0:1, 1, 0:NE], incl[0:1, :]))
            do(ve.tensor_scalar(tables[0:1, 2, :], tables[0:1, 0, :], 1, 1, ALU.bitwise_and, ALU.bitwise_xor))
            do(ve.tensor_scalar(tb1[1][0:1, :], consts[0:1, C_BIDX:C_BIDX + 64], 2.0, incl[0:1, NE - 1:NE], ALU.mult, ALU.is_lt))
            do(ve.tensor_reduce(tb1[2][0:1, 0:1], tb1[1][0:1, :], AX.X, ALU.add))
            do(ve.tensor_copy(tables[0:1, 1, NE:NE + 1], tb1[2][0:1, 0:1]))
            ve.sem_inc(S["tab_made"], 1)

            ve.sem_inc(S["h_made"], 1)
            ve.sem_inc(S["ht_out"], 1)
            ve.sem_inc(S["dn_outd"], 1)
            pairs = ve.value_load(tables[0:1, 1, NE:NE + 1], min_val=1, max_val=NB // 2)
            with ve.Fori(0, NB // 2) as bb, ve.If(bb < pairs):
                for u in range(2):
                    b = bb * 2 + u
                    ve.wait_ge(S["act_made"], b + 1)
                    ve.wait_ge(S["gu_made"], 2 * b + 2)
                    for m in range(2):
                        h_ = slice(m * DE // 2, (m + 1) * DE // 2)
                        ve.tensor_tensor(hrow[u][:, h_], hrow[u][:, h_], bank[3][:, h_], ALU.mult).then_inc(S["h_made"], 1)
                    ve.wait_ge(S["ht_made"], 2 * b + 5)
                    ve.tensor_copy(hTm[u][:, 0:2, :].rearrange("p a b -> p (a b)"), bank[4][:, 0:2 * P]
                                   ).then_inc(S["ht_out"], 1)
                    ve.wait_ge(S["blk_done"], b + 2)
                    ve.wait_ge(S[f"ysto{u}"], 16 * bb + 16)
                    ve.tensor_copy(yrw[u][:, 512:1024], bank[6][:]).then_inc(S["dn_outd"], 1)

            base6 = BASE + V_STEPS[0]

            def need6(n):
                ve.wait_ge(S["dve_step"], base6 + n)

            def gather_sum(t, u, steps):
                st = b6[u]
                ve.wait_ge(S["w6"], t + 1)
                step(ve.scalar_tensor_tensor(ya[u], yb[u], dest_w[:, 1, bass.ds(t, 1)], ya[u], ALU.mult, ALU.add))
                need6(steps + 1)
                ve.scalar_tensor_tensor(tiled(ya[u]), x1t(t), ALPHA, tiled(ya[u]), ALU.mult, ALU.add
                                        ).then_inc(S["r6"], 1)
                ve.wait_ge(S["r6"], t + 1)
                step(ve.bn_stats(st[:, 0:6], ya[u][:, 0:512]))
                step(ve.bn_stats(st[:, 6:12], ya[u][:, 512:1024]))
                need6(steps + 3)
                ve.sem_inc(S["stats6"], 1)
                ve.bn_aggr(st[:, 12:14], st[:, 0:12]).then_inc(S["s6_in"], 1)

            def centre(t, tt, u):
                st = b6[u]
                ve.wait_ge(S["s6_in"], t + 1)
                ve.wait_ge(S[f"out6{u}"], 16 * tt + 16)
                ve.scalar_tensor_tensor(fin[u], ya[u], st[:, 12:13], ln2_g, ALU.subtract, ALU.mult).then_inc(S["c6"], 1)
                ve.wait_ge(S["s6_out"], t + 1)
                ve.reciprocal(st[:, 15:16], st[:, 14:15]).then_inc(S["fin6"], 1)

            gather_sum(0, 0, 0)
            with ve.Fori(0, NT // R6 - 1) as tt:
                for u in range(R6):
                    t = tt * R6 + u
                    gather_sum(t + 1, (u + 1) % R6, 3 * t + 3)
                    centre(t, tt, u)
            for t in range(NT - R6, NT):
                if t + 1 < NT:
                    gather_sum(t + 1, (t + 1) % R6, 3 * t + 3)
                centre(t, t // R6, t % R6)

        @block.gpsimd
        def _(po):
            po.memset(zero_i[:, :], 0).then_inc(S["zero_made"], 1)
            po.memset(zeros, 0.0).then_inc(S["zero_made"], 1)
            po.wait_ge(S["w_in0"], 16)
            po.dma_start(consts, a["consts"]).then_inc(S["const_in"], 16)
            po.dma_start(pool_w[:, :, :], a["pool_w"]).then_inc(S["tm_in"], 16)
            po.dma_start(w_tm[:, :, :], a["w_tm"]).then_inc(S["tm_in"], 16)
            po.wait_ge(S["zero_made"], 2)
            po.wait_ge(S["tile_made"], MJ + 1 + MJ)
            for b in range(NBMIN, NB):
                for n in range(2):
                    po.dma_start(y_dram[b * P:(b + 1) * P, n * TC:(n + 1) * TC], zeros).then_inc(S["rows_zero"], 16)
            po.wait_ge(S["tile_out"], MJ * (NCH - 1) + NBANK + M_KC + 1)
            po.wait_ge(S["sp_made"], 7 * NCH)
            po.tensor_copy(VC2[0:64, :], KC2[64:128, :]).then_inc(S["shifted"], 1)
            po.tensor_copy(VC2[64:128, 0:SEQ - 1], KC2[64:128, 1:SEQ]).then_inc(S["shifted"], 1)
            po.wait_ge(S["shifted"], 2)
            po.tensor_copy(KC2[64:128, 0:SEQ - 1], KC2[0:64, 1:SEQ]).then_inc(S["shifted"], 1)
            done = 0
            for i in range(NT):
                k = n_slc[i] + n_win[i] + 1
                v = OB[i % 2][:, :, 0:k, 0:HD]
                y = yrow[i % 2].rearrange("p (h d) -> p h d", h=NH)
                po.wait_ge(S["al_made"], i + 1)
                po.tensor_tensor(v, v, share(i)[:, :, :, None].to_broadcast((P, NH, k, HD)), ALU.mult).then_inc(S["po_step"], 1)
                done += 1
                if i >= 2:
                    po.wait_ge(S["yT_made"], i - 1)
                for m in range(1, k):
                    po.wait_ge(S["po_step"], done)
                    po.tensor_tensor(y, v[:, :, 0, :] if m == 1 else y, v[:, :, m, :], ALU.add
                                     ).then_inc(S["po_step" if m < k - 1 else "y_made"], 1)
                    done += m < k - 1
            for t in range(NT):
                po.wait_ge(S["x1_made"], t + 1)
                po.dma_start(x1_dram[t * P:(t + 1) * P, :].rearrange("n (a b) -> n a b", a=KD), x1t(t)).then_inc(S["x1_stored"], 16)
            po.wait_ge(S["slot_zero"], 16)
            po.wait_ge(S["dest_made"], 1)
            for c in range(2):
                for t in range(NT):
                    po.indirect_dma_start(slot_dram, bass.IndirectOffsetOnAxis(ap=dest_i[:, c, t:t + 1], axis=0),
                                          tok_i[:, t:t + 1], None).then_inc(S["slot_stored"], 16)
            po.wait_ge(S["slot_stored"], 32 * NT)
            po.wait_ge(S["x1_stored"], 16 * NT)
            po.wait_ge(S["tab_made"], 1)

            def fetch(b, u, n, wait_free):
                if wait_free:
                    po.wait_ge(S["gx_made"], 2 * b - 2)
                po.dma_start(idx[u][:, :], slot_dram[bass.ds(b * P, P), :]).then_inc(S[f"idx{u}"], 16)
                po.wait_ge(S[f"idx{u}"], 16 * n + 16)
                po.sem_inc(S["idx_in"], 1)
                po.indirect_dma_start(xg[u], None, x1_dram, bass.IndirectOffsetOnAxis(ap=idx[u][:, 0:1], axis=0)
                                      ).then_inc(S[f"g_in{u}"], 16)

            fetch(0, 0, 0, False)
            fetch(1, 1, 0, False)
            fetch(2, 0, 1, True)
            pairs = po.value_load(tables[0:1, 1, NE:NE + 1], min_val=1, max_val=NB // 2)
            with po.Fori(0, NB // 2 - 1) as bb, po.If(bb + 1 < pairs):
                for u in range(2):
                    fetch(bb * 2 + u + 3, 1 - u, bb + 1 + u, True)
            po.wait_ge(S["ysto0"], pairs * 16 + 16)
            po.wait_ge(S["ysto1"], pairs * 16 + 16)
            po.wait_ge(S["l2_in"], 32)
            po.wait_ge(S["gx_made"], pairs * 4 + 2)
            po.sem_inc(S["idx_in"], 1)

            def rows(t, u):
                for c, buf in enumerate((ya, yb)):
                    po.indirect_dma_start(buf[u], None, y_dram,
                                          bass.IndirectOffsetOnAxis(ap=dest_i[:, c, t:t + 1], axis=0)
                                          ).then_inc(S[f"ya_in{u}"], 16)

            for t in range(R6):
                rows(t, t)
            for t in range(NT):
                u = t % R6
                if t + R6 < NT:
                    po.wait_ge(S["c6"], t + 1)
                    rows(t + R6, u)
                po.wait_ge(S["n6"], t + 1)
                po.tensor_tensor(fin[u], fin[u], ln2_b, ALU.add).then_inc(S["p6"], 1)


def layout(x, w_in, conv_a_w, conv_b_w, conv_b_b, cf_ln_g, cf_ln_b, pool_w, pool_scale,
           cmp_pe_k, cmp_pe_v, cmp_k_w1, cmp_k_w2, cmp_v_w1, cmp_v_w2, w_out,
           ln1_g, ln1_b, ln2_g, ln2_b, router_w, router_bias, moe_w_gate, moe_w_up, moe_w_down):
    x = np.asarray(x).reshape(SEQ, D)
    w_in = np.asarray(w_in)[0]
    tiles, tm = column_tiles()
    c, k, cs, iw = shape_constants()
    two = lambda v: np.asarray(v).reshape(2, P).T
    taps = lambda v, n: np.asarray(v)[0].reshape(n, 2, P).transpose(2, 1, 0).reshape(P, 2 * n)
    chan = np.concatenate([taps(conv_a_w, AK), taps(conv_b_w, CK), two(conv_b_b), two(cf_ln_g), two(cf_ln_b),
                           two(pool_scale), iw, np.full((P, 1), EPS, np.float32)], 1)
    pw = np.zeros((P, 2, P), np.float32)
    for g in range(4):
        r = slice(64 * (g % 2), 64 * (g % 2) + 64)
        pw[r, g // 2, r] = np.asarray(pool_w)[0, g]
    kt = lambda w_: np.asarray(w_).reshape(KD, P, -1).transpose(1, 0, 2)
    w2 = np.zeros((P, 2, 2, P), np.float32)
    for n, w_ in enumerate((cmp_v_w2, cmp_k_w2)):
        w_ = np.asarray(w_)[0].reshape(2, P, HD).transpose(1, 0, 2)
        w2[:, n, :, 0:HD] = w_
        w2[:, n, :, HD:] = w_
    pe2 = np.stack([np.asarray(p_)[0].reshape(16, P).T for p_ in (cmp_pe_v, cmp_pe_k)], 1)
    we = np.stack([np.asarray(moe_w_gate)[0].reshape(NE, KD, P, DE).transpose(0, 2, 1, 3).reshape(NE, P, KD * DE),
                   np.asarray(moe_w_up)[0].reshape(NE, KD, P, DE).transpose(0, 2, 1, 3).reshape(NE, P, KD * DE),
                   np.asarray(moe_w_down)[0].reshape(NE, 4, P, D).transpose(0, 2, 1, 3).reshape(NE, P, 4 * D)], 1)
    arrays = {
        "x": x,
        "xT": x.reshape(NCH, TC, KD, P).transpose(0, 3, 2, 1).reshape(NCH, P, KD * TC),
        "w_in": np.stack([kt(w_in[:, t]).reshape(P, KD * P) for t in tiles]),
        "w_tm": kt(w_in[:, tm]).reshape(P, -1),
        "consts": c, "masks": k, "cs": cs, "chan": chan, "pool_w": pw.reshape(P, -1),
        "cmp_w1": np.stack([np.asarray(w_)[0].reshape(16, P, CHID).transpose(1, 0, 2).reshape(P, -1)
                            for w_ in (cmp_v_w1, cmp_k_w1)]),
        "cmp_w2": w2.reshape(P, -1), "cmp_pe": pe2.reshape(P, -1),
        "w_out": np.asarray(w_out)[0].reshape(2, KD // 2, P, D).transpose(0, 2, 1, 3).reshape(2, P, -1),
        "ln1_g": np.asarray(ln1_g)[0], "ln1_b": np.asarray(ln1_b)[0],
        "ln2_g": np.asarray(ln2_g)[0], "ln2_b": np.asarray(ln2_b)[0],
        "router_w": kt(router_w).reshape(P, -1), "router_bias": np.asarray(router_bias), "w_exp": we,
    }
    return {"in_" + n: np.ascontiguousarray(v) for n, v in arrays.items()}


def kernel(**inputs):
    import concourse.bacc as bacc
    from concourse.bass_utils import run_bass_kernel_spmd

    arrays = layout(**inputs)
    nc = bacc.Bacc("TRN2", target_bir_lowering=False, num_devices=1, dynamic_dma_scratch_size=2048)
    aps = {n[3:]: nc.dram_tensor(n, v.shape, F32, kind="ExternalInput").ap() for n, v in arrays.items()}
    out = nc.dram_tensor("out", (SEQ, D), F32, kind="ExternalOutput").ap()
    hybrid_layer(nc, aps, out)
    r = run_bass_kernel_spmd(nc, [arrays], core_ids=[0])
    return r.results[0]["out"].reshape(1, SEQ, D)
```
